# Optimizing a Trainium2 kernel written in Bass

```python
import jax, jax.numpy as jnp
from jax import lax
import numpy as np
import math

D_MODEL = 1024
BATCH = 1
SEQ = 512
DEPTH = 1

CHUNK = 64
LEFT_CHUNKS = 8
BAND = (LEFT_CHUNKS + 1) * CHUNK
N_HEADS = 8
HEAD_DIM = 64
D_ATTN = N_HEADS * HEAD_DIM
D_CONV = 512
CONV_K = 31
MAX_REL = 128
D_FF = 2816
FFN_CONV_K = 3
EPS = 1e-6
NEG_INF = -1e30
IN_WIDTHS = (D_ATTN, D_ATTN, D_ATTN, D_CONV, D_CONV, D_MODEL, D_MODEL)
D_IN = D_ATTN * 3 + D_CONV * 2 + D_MODEL * 2


def rms_norm(x, g):
    xf = x.astype(jnp.float32)
    y = xf * lax.rsqrt(jnp.mean(xf * xf, axis=-1, keepdims=True) + EPS)
    return (y * g.astype(jnp.float32)).astype(x.dtype)

def layer_norm(x, g, b):
    xf = x.astype(jnp.float32)
    mu = jnp.mean(xf, axis=-1, keepdims=True)
    var = jnp.mean(jnp.square(xf - mu), axis=-1, keepdims=True)
    y = (xf - mu) * lax.rsqrt(var + EPS)
    return (y * g.astype(jnp.float32) + b.astype(jnp.float32)).astype(x.dtype)

def causal_dwconv(x, w, b):
    k = w.shape[0]
    y = lax.conv_general_dilated(
        x, w[:, None, :].astype(x.dtype), window_strides=(1,), padding=[(k - 1, 0)],
        dimension_numbers=('NWC', 'WIO', 'NWC'), feature_group_count=x.shape[-1])
    return y + b

def chunk_band(t):
    b, s, h, dh = t.shape
    nc = s // CHUNK
    tc = t.reshape(b, nc, CHUNK, h, dh)
    tp = jnp.pad(tc, ((0, 0), (LEFT_CHUNKS, 0), (0, 0), (0, 0), (0, 0)))
    band = jnp.stack([tp[:, j:j + nc] for j in range(LEFT_CHUNKS + 1)], axis=2)
    return band.reshape(b, nc, BAND, h, dh)

def chunked_rel_attention(q, k, v, rel_bias):
    b, s, _ = q.shape
    nc = s // CHUNK
    qc = q.reshape(b, nc, CHUNK, N_HEADS, HEAD_DIM)
    kb = chunk_band(k.reshape(b, s, N_HEADS, HEAD_DIM))
    vb = chunk_band(v.reshape(b, s, N_HEADS, HEAD_DIM))
    scores = jnp.einsum('bcqhd,bckhd->bhcqk', qc, kb).astype(jnp.float32) * (HEAD_DIM ** -0.5)
    qi = jnp.arange(CHUNK)
    kj = jnp.arange(BAND)
    rel = LEFT_CHUNKS * CHUNK + qi[:, None] - kj[None, :]
    idx = jnp.clip(rel, -MAX_REL, MAX_REL) + MAX_REL
    bias = rel_bias[:, idx].astype(jnp.float32)
    scores = scores + bias[None, :, None, :, :]
    key_chunk = jnp.arange(nc)[:, None] - LEFT_CHUNKS + (kj // CHUNK)[None, :]
    valid = key_chunk >= 0
    scores = jnp.where(valid[None, None, :, None, :], scores, NEG_INF)
    probs = jax.nn.softmax(scores, axis=-1).astype(v.dtype)
    out = jnp.einsum('bhcqk,bckhd->bcqhd', probs, vb)
    return out.reshape(b, s, D_ATTN)

def token_mixer(h, w_in, b_in, rel_bias, w_attn_o, w_dw, b_dw, g_ln, b_ln,
                w_conv_o, b_conv_o, w_mix_o):
    z = h @ w_in + b_in
    splits = list(np.cumsum(IN_WIDTHS)[:-1])
    q, k, v, glu_a, glu_b, gate_a, gate_b = jnp.split(z, splits, axis=-1)
    a = chunked_rel_attention(q, k, v, rel_bias) @ w_attn_o
    u = glu_a * jax.nn.sigmoid(glu_b)
    u = causal_dwconv(u, w_dw, b_dw)
    u = jax.nn.silu(layer_norm(u, g_ln, b_ln))
    cb = u @ w_conv_o + b_conv_o
    y = jax.nn.sigmoid(gate_a) * a + jax.nn.sigmoid(gate_b) * cb
    return y @ w_mix_o

def conv_ffn(h, w_up, w_dw, b_dw, w_down):
    u = causal_dwconv(h @ w_up, w_dw, b_dw)
    val, gt = jnp.split(u, 2, axis=-1)
    return (jax.nn.gelu(gt) * val) @ w_down

def first_inputs(seed: int = 0) -> dict:
    key = jax.random.key(seed)
    ks = jax.random.split(key, 26)
    L = DEPTH

    def nrm(k, shape, scale):
        return jax.random.normal(k, shape, jnp.float32) * scale

    def gain(k, shape):
        return 1.0 + 0.1 * jax.random.normal(k, shape, jnp.float32)

    return {
        "x": nrm(ks[0], (BATCH, SEQ, D_MODEL), 1.0),
        "c": nrm(ks[1], (BATCH, D_MODEL), 1.0),
        "w_ada": nrm(ks[2], (L, D_MODEL, 6 * D_MODEL), 0.5 * D_MODEL ** -0.5),
        "b_ada": nrm(ks[3], (L, 6 * D_MODEL), 0.01),
        "g_pre_mix": gain(ks[4], (L, D_MODEL)),
        "g_post_mix": gain(ks[5], (L, D_MODEL)),
        "w_in": nrm(ks[6], (L, D_MODEL, D_IN), D_MODEL ** -0.5),
        "b_in": nrm(ks[7], (L, D_IN), 0.01),
        "rel_bias": nrm(ks[8], (L, N_HEADS, 2 * MAX_REL + 1), 0.5),
        "w_attn_o": nrm(ks[9], (L, D_ATTN, D_MODEL), D_ATTN ** -0.5),
        "w_dw_conv": nrm(ks[10], (L, CONV_K, D_CONV), CONV_K ** -0.5),
        "b_dw_conv": nrm(ks[11], (L, D_CONV), 0.01),
        "g_conv_ln": gain(ks[12], (L, D_CONV)),
        "b_conv_ln": nrm(ks[13], (L, D_CONV), 0.01),
        "w_conv_o": nrm(ks[14], (L, D_CONV, D_MODEL), D_CONV ** -0.5),
        "b_conv_o": nrm(ks[15], (L, D_MODEL), 0.01),
        "w_mix_o": nrm(ks[16], (L, D_MODEL, D_MODEL), D_MODEL ** -0.5),
        "g_pre_ffn": gain(ks[17], (L, D_MODEL)),
        "g_post_ffn": gain(ks[18], (L, D_MODEL)),
        "w_up": nrm(ks[19], (L, D_MODEL, 2 * D_FF), D_MODEL ** -0.5),
        "w_dw_ffn": nrm(ks[20], (L, FFN_CONV_K, 2 * D_FF), FFN_CONV_K ** -0.5),
        "b_dw_ffn": nrm(ks[21], (L, 2 * D_FF), 0.01),
        "w_down": nrm(ks[22], (L, D_FF, D_MODEL), D_FF ** -0.5),
    }

def first_block(x, c, w_ada, b_ada, g_pre_mix, g_post_mix, w_in, b_in, rel_bias,
              w_attn_o, w_dw_conv, b_dw_conv, g_conv_ln, b_conv_ln, w_conv_o,
              b_conv_o, w_mix_o, g_pre_ffn, g_post_ffn, w_up, w_dw_ffn, b_dw_ffn,
              w_down):
    c_act = jax.nn.silu(c)
    for l in range(DEPTH):
        mod = c_act @ w_ada[l] + b_ada[l]
        sh_m, sc_m, gt_m, sh_f, sc_f, gt_f = [m[:, None, :] for m in jnp.split(mod, 6, axis=-1)]
        h = rms_norm(x, g_pre_mix[l]) * (1.0 + sc_m) + sh_m
        y = token_mixer(h, w_in[l], b_in[l], rel_bias[l], w_attn_o[l], w_dw_conv[l],
                        b_dw_conv[l], g_conv_ln[l], b_conv_ln[l], w_conv_o[l],
                        b_conv_o[l], w_mix_o[l])
        x = x + gt_m * rms_norm(y, g_post_mix[l])
        h = rms_norm(x, g_pre_ffn[l]) * (1.0 + sc_f) + sh_f
        y = conv_ffn(h, w_up[l], w_dw_ffn[l], b_dw_ffn[l], w_down[l])
        x = x + gt_f * rms_norm(y, g_post_ffn[l])
    return x


N_MEM = 256
R_HEAD = 64
R_HEADS = D_MODEL // R_HEAD
R_WIDTH = R_HEADS * R_HEAD
R_LORA_W = 64
R_LORA_A = 64
R_LORA_G = 160
LNX_EPS = 64e-5
N_HEADS_2 = 16
N_KV = 4
N_HG = N_HEADS_2 // N_KV
CMP_BLOCK = 32
CMP_STRIDE = 16
CMP_HIDDEN = 256
SEL_BLOCK = 64
SEL_TOPK = 16
WINDOW = 512
Q_BLOCK = 32
FORCE_SCORE = 1e4
REL_BUCKETS = 32
REL_MAX_DIST = 128
CA_HEADS = 4
CA_HEAD_DIM = D_MODEL // CA_HEADS
CONV_W = 3
NORM_EPS = 1e-6
QK_EPS = 1e-6
RWKV_COLS = 3 * R_WIDTH + R_LORA_W + R_LORA_A + R_LORA_G
NSA_KV = N_KV * HEAD_DIM
NSA_COLS = N_HEADS_2 * HEAD_DIM + 6 * NSA_KV + 3 * N_HEADS_2
GATE_COLS = 2 * D_MODEL
IN_COLS = RWKV_COLS + NSA_COLS + GATE_COLS


def rms_norm_2(x, g, eps=NORM_EPS):
    xf = x.astype(jnp.float32)
    y = xf * lax.rsqrt(jnp.mean(xf * xf, axis=-1, keepdims=True) + eps)
    return (y * g.astype(jnp.float32)).astype(x.dtype)

def masked_softmax(logits, mask):
    logits = jnp.where(mask, logits.astype(jnp.float32), -jnp.inf)
    m = jnp.max(logits, axis=-1, keepdims=True)
    m = jnp.where(jnp.isfinite(m), m, 0.0)
    e = jnp.exp(logits - m)
    s = jnp.sum(e, axis=-1, keepdims=True)
    return e / jnp.where(s > 0, s, 1.0)

def t5_bucket(dist):
    n = jnp.maximum(dist, 0)
    exact = REL_BUCKETS // 2
    nf = jnp.maximum(n, 1).astype(jnp.float32)
    large = exact + (jnp.log(nf / exact) / math.log(REL_MAX_DIST / exact) * (REL_BUCKETS - exact)).astype(jnp.int32)
    large = jnp.minimum(large, REL_BUCKETS - 1)
    return jnp.where(n < exact, n, large)

def group_bias(table, bucket):
    tg = table.astype(jnp.float32).reshape(REL_BUCKETS, N_KV, N_HG)
    gi = jnp.arange(N_KV).reshape(1, N_KV, 1, 1)
    return jnp.moveaxis(tg[bucket, gi], -1, -2)

def token_shift(z, mu):
    prev = jnp.pad(z[:, :-1], ((0, 0), (1, 0), (0, 0)))
    return z + (prev - z) * mu

def rwkv7_scan(r, w, k, v, a, b):
    B, S, H, N = r.shape
    xs = tuple(jnp.swapaxes(t.astype(jnp.float32), 0, 1) for t in (r, w, k, v, a, b))

    def step(state, inp):
        r_t, w_t, k_t, v_t, a_t, b_t = inp
        sa = jnp.einsum('bhvk,bhk->bhv', state, a_t)
        state = state * w_t[:, :, None, :] + sa[..., None] * b_t[:, :, None, :] + v_t[..., None] * k_t[:, :, None, :]
        return state, jnp.einsum('bhvk,bhk->bhv', state, r_t)

    s0 = jnp.zeros((B, H, N, N), jnp.float32)
    _, ys = lax.scan(step, s0, xs)
    return jnp.swapaxes(ys, 0, 1)

def rwkv7_mixer(z, mu, w0, w2, a0, a2, g2, k_k, k_a, r_k, lnx_w, lnx_b):
    B, S, _ = z.shape
    z = token_shift(z, mu)
    r, k, v, zw, za, zg = jnp.split(z, np.cumsum([R_WIDTH, R_WIDTH, R_WIDTH, R_LORA_W, R_LORA_A]).tolist(), axis=-1)
    w = -jax.nn.softplus(-(w0 + jnp.tanh(zw) @ w2)) - 0.5
    a = jax.nn.sigmoid(a0 + za @ a2)
    g = jax.nn.sigmoid(zg) @ g2
    hd = lambda t: t.reshape(B, S, R_HEADS, R_HEAD)
    kk = hd(k * k_k).astype(jnp.float32)
    kk = kk / jnp.maximum(jnp.sqrt(jnp.sum(kk * kk, axis=-1, keepdims=True)), 1e-12)
    k = k * (1 + (a - 1) * k_a)
    decay = jnp.exp(-jnp.exp(w.astype(jnp.float32)))
    a_h = hd(a).astype(jnp.float32)
    y = rwkv7_scan(hd(r), hd(decay), hd(k), hd(v), -kk, kk * a_h)
    mean = jnp.mean(y, axis=-1, keepdims=True)
    var = jnp.mean(jnp.square(y - mean), axis=-1, keepdims=True)
    y = ((y - mean) * lax.rsqrt(var + LNX_EPS)).reshape(B, S, R_WIDTH)
    y = y * lnx_w.astype(jnp.float32) + lnx_b.astype(jnp.float32)
    bonus = jnp.sum(hd(r) * hd(k) * r_k, axis=-1, keepdims=True) * hd(v)
    out = (y + bonus.reshape(B, S, R_WIDTH).astype(jnp.float32)) * g.astype(jnp.float32)
    return out.astype(z.dtype)

def nsa_mixer(q, kc, vc, ks, vs, kw, vw, gates, rel_table, q_gain, k_gain, pe_k, pe_v, c1k, c2k, c1v, c2v):
    B, S, _ = q.shape
    q = rms_norm_2(q.reshape(B, S, N_KV, N_HG, HEAD_DIM), q_gain, QK_EPS)
    kvh = lambda t: t.reshape(B, S, N_KV, HEAD_DIM)
    scale = HEAD_DIM ** -0.5
    n_cmp = (S - CMP_BLOCK) // CMP_STRIDE + 1
    cidx = jnp.arange(n_cmp)[:, None] * CMP_STRIDE + jnp.arange(CMP_BLOCK)[None, :]

    def compress(t, pe, w1, w2):
        blk = kvh(t)[:, cidx] + pe[:, None, :]
        hid = jax.nn.gelu(jnp.einsum('bnlgd,ldc->bngc', blk, w1.reshape(CMP_BLOCK, HEAD_DIM, CMP_HIDDEN)))
        return jnp.einsum('bngc,cd->bngd', hid, w2)

    k_cmp = rms_norm_2(compress(kc, pe_k, c1k, c2k), k_gain[0], QK_EPS)
    v_cmp = compress(vc, pe_v, c1v, c2v)
    cmp_end = jnp.arange(n_cmp) * CMP_STRIDE + CMP_BLOCK - 1
    n_blk = S // SEL_BLOCK
    n_top = min(SEL_TOPK, n_blk)
    ci = jnp.arange(n_cmp)[:, None] * CMP_STRIDE
    sj = jnp.arange(n_blk)[None, :] * SEL_BLOCK
    cmp_to_sel = ((ci <= sj + SEL_BLOCK - 1) & (ci + CMP_BLOCK - 1 >= sj)).astype(jnp.float32)
    kb = rms_norm_2(kvh(ks), k_gain[1], QK_EPS).reshape(B, n_blk, SEL_BLOCK, N_KV, HEAD_DIM).transpose(0, 3, 1, 2, 4)
    vb = kvh(vs).reshape(B, n_blk, SEL_BLOCK, N_KV, HEAD_DIM).transpose(0, 3, 1, 2, 4)
    pad = ((0, 0), (WINDOW, 0), (0, 0), (0, 0))
    k_win = jnp.pad(rms_norm_2(kvh(kw), k_gain[2], QK_EPS), pad)
    v_win = jnp.pad(kvh(vw), pad)
    g_all = jax.nn.sigmoid(gates.astype(jnp.float32)).reshape(B, S, N_KV, N_HG, 3)
    nq = S // Q_BLOCK
    q_blocks = jnp.swapaxes(q.reshape(B, nq, Q_BLOCK, N_KV, N_HG, HEAD_DIM), 0, 1)
    g_blocks = jnp.swapaxes(g_all.reshape(B, nq, Q_BLOCK, N_KV, N_HG, 3), 0, 1)
    starts = jnp.arange(nq, dtype=jnp.int32) * Q_BLOCK
    bi = jnp.arange(B)[:, None, None, None]
    gi = jnp.arange(N_KV)[None, :, None, None]
    blk_ids = jnp.arange(n_blk)

    def block(args):
        qb, gb, q0 = args
        t = q0 + jnp.arange(Q_BLOCK)
        s_c = jnp.einsum('bqghd,bngd->bgqhn', qb, k_cmp).astype(jnp.float32) * scale
        s_c = s_c + group_bias(rel_table, t5_bucket(t[:, None] - cmp_end[None, :])[None, None])
        p_c = masked_softmax(s_c, (cmp_end[None, :] <= t[:, None])[None, None, :, None, :])
        o_c = jnp.einsum('bgqhn,bngd->bqghd', p_c.astype(v_cmp.dtype), v_cmp)
        imp = jnp.einsum('bgqhn,nj->bgqj', p_c, cmp_to_sel)
        cur = t // SEL_BLOCK
        forced = (blk_ids[None, :] == 0) | (blk_ids[None, :] == cur[:, None]) | (blk_ids[None, :] == cur[:, None] - 1)
        valid = blk_ids[None, :] * SEL_BLOCK <= t[:, None]
        imp = jnp.where(valid, jnp.where(forced, FORCE_SCORE, imp), -jnp.inf)
        _, idx = lax.top_k(imp, n_top)
        k_g = kb[bi, gi, idx].reshape(B, N_KV, Q_BLOCK, n_top * SEL_BLOCK, HEAD_DIM)
        v_g = vb[bi, gi, idx].reshape(B, N_KV, Q_BLOCK, n_top * SEL_BLOCK, HEAD_DIM)
        kpos = (idx[..., None] * SEL_BLOCK + jnp.arange(SEL_BLOCK)).reshape(B, N_KV, Q_BLOCK, n_top * SEL_BLOCK)
        dist_s = t[None, None, :, None] - kpos
        s_s = jnp.einsum('bqghd,bgqkd->bgqhk', qb, k_g).astype(jnp.float32) * scale + group_bias(rel_table, t5_bucket(dist_s))
        p_s = masked_softmax(s_s, (dist_s >= 0)[:, :, :, None, :])
        o_s = jnp.einsum('bgqhk,bgqkd->bqghd', p_s.astype(v_g.dtype), v_g)
        kw_b = lax.dynamic_slice_in_dim(k_win, q0, WINDOW + Q_BLOCK, axis=1)
        vw_b = lax.dynamic_slice_in_dim(v_win, q0, WINDOW + Q_BLOCK, axis=1)
        wpos = q0 - WINDOW + jnp.arange(WINDOW + Q_BLOCK)
        dist_w = t[:, None] - wpos[None, :]
        m_w = (wpos[None, :] >= 0) & (dist_w >= 0) & (dist_w < WINDOW)
        s_w = jnp.einsum('bqghd,bkgd->bgqhk', qb, kw_b).astype(jnp.float32) * scale
        s_w = s_w + group_bias(rel_table, t5_bucket(dist_w)[None, None])
        p_w = masked_softmax(s_w, m_w[None, None, :, None, :])
        o_w = jnp.einsum('bgqhk,bkgd->bqghd', p_w.astype(vw_b.dtype), vw_b)
        out = gb[..., 0:1] * o_c + gb[..., 1:2] * o_s + gb[..., 2:3] * o_w
        return out.astype(qb.dtype)

    o = lax.map(block, (q_blocks, g_blocks, starts))
    return jnp.swapaxes(o, 0, 1).reshape(B, S, N_HEADS_2 * HEAD_DIM)

def cross_attn(xn, mn, wq, wkv, q_gain, k_gain, wo):
    B, S, _ = xn.shape
    M = mn.shape[1]
    q = rms_norm_2((xn @ wq).reshape(B, S, CA_HEADS, CA_HEAD_DIM), q_gain, QK_EPS)
    kv = (mn @ wkv).reshape(B, M, 2, CA_HEADS, CA_HEAD_DIM)
    k = rms_norm_2(kv[:, :, 0], k_gain, QK_EPS)
    v = kv[:, :, 1]
    s = jnp.einsum('bshd,bmhd->bhsm', q, k).astype(jnp.float32) * (CA_HEAD_DIM ** -0.5)
    p = jax.nn.softmax(s, axis=-1).astype(v.dtype)
    o = jnp.einsum('bhsm,bmhd->bshd', p, v).reshape(B, S, CA_HEADS * CA_HEAD_DIM)
    return o @ wo

def conv_ffn_2(xn, w_up, conv_w, conv_b, w_down):
    a, b = jnp.split(xn @ w_up, 2, axis=-1)
    a = lax.conv_general_dilated(a, conv_w[:, None, :].astype(a.dtype), (1,), [(CONV_W - 1, 0)],
                                 dimension_numbers=('NWC', 'WIO', 'NWC'), feature_group_count=D_FF) + conv_b
    return (jax.nn.silu(a) * b) @ w_down

def second_inputs(seed: int = 0) -> dict:
    key = jax.random.key(seed)
    ks = iter(jax.random.split(key, 64))
    L, D = DEPTH, D_MODEL
    nrm = lambda shape, scale: jax.random.normal(next(ks), shape, jnp.float32) * scale
    lin = lambda fi, fo: nrm((L, fi, fo), fi ** -0.5)
    gain = lambda *s: 1.0 + nrm((L,) + s, 0.02)
    return {
        "x": nrm((BATCH, SEQ, D), 1.0),
        "mem": nrm((BATCH, N_MEM, D), 1.0),
        "rel_bias": nrm((REL_BUCKETS, N_HEADS_2), 0.1),
        "norm_mix": gain(D),
        "w_in": lin(D, IN_COLS),
        "rwkv_mu": jax.random.uniform(next(ks), (L, RWKV_COLS), jnp.float32),
        "rwkv_w0": jax.random.uniform(next(ks), (L, R_WIDTH), jnp.float32, -6.0, 0.5),
        "rwkv_w2": nrm((L, R_LORA_W, R_WIDTH), 0.5 * R_LORA_W ** -0.5),
        "rwkv_a0": nrm((L, R_WIDTH), 0.1),
        "rwkv_a2": nrm((L, R_LORA_A, R_WIDTH), 0.5 * R_LORA_A ** -0.5),
        "rwkv_g2": lin(R_LORA_G, R_WIDTH),
        "rwkv_kk": 0.85 + nrm((L, R_WIDTH), 0.02),
        "rwkv_ka": 1.0 + nrm((L, R_WIDTH), 0.02),
        "rwkv_rk": nrm((L, R_HEADS, R_HEAD), 0.1),
        "rwkv_lnx_w": gain(R_WIDTH),
        "rwkv_lnx_b": nrm((L, R_WIDTH), 0.02),
        "nsa_q_gain": gain(HEAD_DIM),
        "nsa_k_gain": gain(3, HEAD_DIM),
        "cmp_pe_k": nrm((L, CMP_BLOCK, HEAD_DIM), 0.1),
        "cmp_pe_v": nrm((L, CMP_BLOCK, HEAD_DIM), 0.1),
        "cmp_w1_k": lin(CMP_BLOCK * HEAD_DIM, CMP_HIDDEN),
        "cmp_w2_k": lin(CMP_HIDDEN, HEAD_DIM),
        "cmp_w1_v": lin(CMP_BLOCK * HEAD_DIM, CMP_HIDDEN),
        "cmp_w2_v": lin(CMP_HIDDEN, HEAD_DIM),
        "w_branch_rwkv": lin(R_WIDTH, D),
        "w_branch_nsa": lin(N_HEADS_2 * HEAD_DIM, D),
        "w_mix_out": lin(D, D),
        "norm_cross": gain(D),
        "norm_mem": gain(D),
        "ca_wq": lin(D, CA_HEADS * CA_HEAD_DIM),
        "ca_wkv": lin(D, 2 * CA_HEADS * CA_HEAD_DIM),
        "ca_q_gain": gain(CA_HEAD_DIM),
        "ca_k_gain": gain(CA_HEAD_DIM),
        "ca_wo": lin(CA_HEADS * CA_HEAD_DIM, D),
        "norm_ffn": gain(D),
        "ffn_up": lin(D, 2 * D_FF),
        "ffn_conv": nrm((L, CONV_W, D_FF), CONV_W ** -0.5),
        "ffn_conv_b": nrm((L, D_FF), 0.02),
        "ffn_down": lin(D_FF, D),
    }

def second_block(x, mem, rel_bias, norm_mix, w_in, rwkv_mu, rwkv_w0, rwkv_w2, rwkv_a0, rwkv_a2, rwkv_g2,
              rwkv_kk, rwkv_ka, rwkv_rk, rwkv_lnx_w, rwkv_lnx_b, nsa_q_gain, nsa_k_gain, cmp_pe_k, cmp_pe_v,
              cmp_w1_k, cmp_w2_k, cmp_w1_v, cmp_w2_v, w_branch_rwkv, w_branch_nsa, w_mix_out,
              norm_cross, norm_mem, ca_wq, ca_wkv, ca_q_gain, ca_k_gain, ca_wo,
              norm_ffn, ffn_up, ffn_conv, ffn_conv_b, ffn_down):
    B, S, D = x.shape
    split_pts = np.cumsum([RWKV_COLS, N_HEADS_2 * HEAD_DIM] + [NSA_KV] * 6 + [3 * N_HEADS_2]).tolist()
    h = x
    for l in range(DEPTH):
        xn = rms_norm_2(h, norm_mix[l])
        z = xn @ w_in[l]
        z_r, z_q, z_kc, z_vc, z_ks, z_vs, z_kw, z_vw, z_g, z_m = jnp.split(z, split_pts, axis=-1)
        y_r = rwkv7_mixer(z_r, rwkv_mu[l], rwkv_w0[l], rwkv_w2[l], rwkv_a0[l], rwkv_a2[l], rwkv_g2[l],
                          rwkv_kk[l], rwkv_ka[l], rwkv_rk[l], rwkv_lnx_w[l], rwkv_lnx_b[l])
        y_n = nsa_mixer(z_q, z_kc, z_vc, z_ks, z_vs, z_kw, z_vw, z_g, rel_bias, nsa_q_gain[l], nsa_k_gain[l],
                        cmp_pe_k[l], cmp_pe_v[l], cmp_w1_k[l], cmp_w2_k[l], cmp_w1_v[l], cmp_w2_v[l])
        gm = jax.nn.sigmoid(z_m.astype(jnp.float32)).reshape(B, S, 2, D)
        merged = gm[:, :, 0] * (y_r @ w_branch_rwkv[l]) + gm[:, :, 1] * (y_n @ w_branch_nsa[l])
        h = h + merged.astype(h.dtype) @ w_mix_out[l]
        h = h + cross_attn(rms_norm_2(h, norm_cross[l]), rms_norm_2(mem, norm_mem[l]), ca_wq[l], ca_wkv[l],
                           ca_q_gain[l], ca_k_gain[l], ca_wo[l])
        h = h + conv_ffn_2(rms_norm_2(h, norm_ffn[l]), ffn_up[l], ffn_conv[l], ffn_conv_b[l], ffn_down[l])
    return h


def setup_inputs(seed=0):
    out = dict(first_inputs(seed))
    for name, value in second_inputs(seed + 1).items():
        if name != "x":
            out[name + "_2"] = value
    return out


def reference(
    x, c, w_ada, b_ada, g_pre_mix, g_post_mix, w_in, b_in, rel_bias, w_attn_o, w_dw_conv,
    b_dw_conv, g_conv_ln, b_conv_ln, w_conv_o, b_conv_o, w_mix_o, g_pre_ffn, g_post_ffn, w_up,
    w_dw_ffn, b_dw_ffn, w_down, mem_2, rel_bias_2, norm_mix_2, w_in_2, rwkv_mu_2, rwkv_w0_2,
    rwkv_w2_2, rwkv_a0_2, rwkv_a2_2, rwkv_g2_2, rwkv_kk_2, rwkv_ka_2, rwkv_rk_2, rwkv_lnx_w_2,
    rwkv_lnx_b_2, nsa_q_gain_2, nsa_k_gain_2, cmp_pe_k_2, cmp_pe_v_2, cmp_w1_k_2, cmp_w2_k_2,
    cmp_w1_v_2, cmp_w2_v_2, w_branch_rwkv_2, w_branch_nsa_2, w_mix_out_2, norm_cross_2,
    norm_mem_2, ca_wq_2, ca_wkv_2, ca_q_gain_2, ca_k_gain_2, ca_wo_2, norm_ffn_2, ffn_up_2,
    ffn_conv_2, ffn_conv_b_2, ffn_down_2,
):
    x = first_block(
        x, c, w_ada, b_ada, g_pre_mix, g_post_mix, w_in, b_in, rel_bias, w_attn_o, w_dw_conv,
        b_dw_conv, g_conv_ln, b_conv_ln, w_conv_o, b_conv_o, w_mix_o, g_pre_ffn, g_post_ffn,
        w_up, w_dw_ffn, b_dw_ffn, w_down,
    )
    return second_block(
        x, mem_2, rel_bias_2, norm_mix_2, w_in_2, rwkv_mu_2, rwkv_w0_2, rwkv_w2_2, rwkv_a0_2,
        rwkv_a2_2, rwkv_g2_2, rwkv_kk_2, rwkv_ka_2, rwkv_rk_2, rwkv_lnx_w_2, rwkv_lnx_b_2,
        nsa_q_gain_2, nsa_k_gain_2, cmp_pe_k_2, cmp_pe_v_2, cmp_w1_k_2, cmp_w2_k_2, cmp_w1_v_2,
        cmp_w2_v_2, w_branch_rwkv_2, w_branch_nsa_2, w_mix_out_2, norm_cross_2, norm_mem_2,
        ca_wq_2, ca_wkv_2, ca_q_gain_2, ca_k_gain_2, ca_wo_2, norm_ffn_2, ffn_up_2, ffn_conv_2,
        ffn_conv_b_2, ffn_down_2,
    )


_drawn_inputs = setup_inputs


def setup_inputs(seed=0):
    import zlib

    import numpy as np

    out = dict(_drawn_inputs(seed))
    spreads = {}
    factors = {'b_ada': 2.892,
     'b_in': 7.749,
     'b_dw_conv': 7.42,
     'b_conv_ln': 8.0,
     'b_conv_o': 8.0,
     'b_dw_ffn': 8.0,
     'rel_bias_2': 64.0,
     'norm_mix_2': 4.876,
     'rwkv_w2_2': 23.049,
     'rwkv_a0_2': 4.537,
     'rwkv_kk_2': 64.0,
     'rwkv_ka_2': 8.0,
     'rwkv_lnx_w_2': 64.0,
     'rwkv_lnx_b_2': 64.0,
     'nsa_q_gain_2': 64.0,
     'nsa_k_gain_2': 64.0,
     'cmp_pe_k_2': 64.0,
     'cmp_pe_v_2': 29.672,
     'norm_cross_2': 33.752,
     'norm_mem_2': 39.551,
     'ca_q_gain_2': 38.569,
     'ca_k_gain_2': 43.718,
     'norm_ffn_2': 33.664,
     'ffn_conv_b_2': 47.088,
     'cmp_w1_k_2': 3.88,
     'cmp_w2_k_2': 3.86,
     'cmp_w1_v_2': 3.45,
     'cmp_w2_v_2': 2.901}
    for name, (base, spread) in spreads.items():
        noise = np.random.default_rng([zlib.crc32(name.encode()), seed]).standard_normal(out[name].shape)
        drawn = base * np.exp(spread * noise) if base else spread * noise
        out[name] = __import__('jax').numpy.asarray(drawn.astype(out[name].dtype))
    for name, factor in factors.items():
        out[name] = (out[name] * factor).astype(out[name].dtype)
    return out
```

```python
from collections import namedtuple
from contextlib import ExitStack

import numpy as np

import concourse.bass as bass
from concourse import mybir

ALU = mybir.AluOpType
ACT = mybir.ActivationFunctionType
F32 = mybir.dt.float32
AX_X = mybir.AxisListType.X

P = 128
S = 512
D = 1024
DT = D // P
DH = 64
D_FF = 2816
FT = D_FF // P
NEG = -1e30
EPS = 1e-6

CHUNK = 64
H1 = 8
CONV_K = 31
MAX_REL = 128

R_HEADS = 16
LNX_EPS = 64e-5
H2, N_KV = 16, 4
HG = H2 // N_KV
BUCKETS = 32
CMP_BLOCK, CMP_STRIDE = 32, 16
N_CMP = (S - CMP_BLOCK) // CMP_STRIDE + 1
CMP_HIDDEN = 256
CA_HEADS = 4
N_MEM = 256
LINE = 640

W_SLOTS = 4

STREAM = [
    ("ada", 48), ("glu", 8), ("qkv", 12), ("mix1", 24), ("mixo1", 8), ("up1", 44), ("down1", 22),
    ("rlora", 4), ("rkv", 24), ("nsa", 20), ("cmp", 8),
    ("mix2", 32), ("mixo2", 8), ("caq", 8), ("cakv", 16), ("cao", 8), ("up2", 44), ("down2", 22),
]
U0 = {}
N_UNITS = 0
for _name, _n in STREAM:
    U0[_name] = N_UNITS
    N_UNITS += _n
assert N_UNITS % W_SLOTS == 0

COLUMNS = [
    ("c", 8), ("b_ada", 48), ("g_pre_mix", 8), ("g_post_mix", 8), ("b_in", 36), ("w_dw_conv", 4 * CONV_K),
    ("b_dw_conv", 4), ("g_conv_ln", 4), ("b_conv_ln", 4), ("b_conv_o", 8), ("g_pre_ffn", 8),
    ("g_post_ffn", 8), ("w_dw_ffn", 2 * FT * 3), ("b_dw_ffn", 2 * FT),
    ("norm_mix", 8), ("mu", 28), ("w0", 8), ("a0", 8), ("kk", 8), ("ka", 8), ("rk", 8),
    ("lnx_w", 8), ("lnx_b", 8), ("q_gain", 1), ("k_gain", 3), ("pe_k", 16), ("pe_v", 16),
    ("norm_cross", 8), ("norm_mem", 8), ("ca_q_gain", 2), ("ca_k_gain", 2), ("norm_ffn", 8),
    ("ffn_conv", FT * 3), ("ffn_conv_b", FT),
]
C0 = {}
N_COLS = 0
for _name, _n in COLUMNS:
    C0[_name] = N_COLS
    N_COLS += _n

CONSTS = [("ident", 128), ("ones", 128), ("blk", 128), ("strict_up", 64), ("incl_up", 64), ("up16", 64),
          ("lo16", 64), ("lo_off", 64), ("eye64", 64), ("scan", 512)]
K0 = {}
N_CONST = 0
for _name, _n in CONSTS:
    K0[_name] = N_CONST
    N_CONST += _n





def norm_steps(n):
    return dict(pe=n, act=n + 1, dve=n + 2)


def heads_steps(batches, n):
    return dict(pe=n, act=n + batches, dve=2 * n + batches)


def turn_steps(n):
    return dict(pe=n, act=n)


FFN1 = dict(ev=2 * FT, conv=FT, tap=2 * FT, gelu=FT, dve=2 * FT)
FFN2 = dict(ev=2 * FT, conv=FT, tap=FT, gelu=FT, dve=FT)
MIX = dict(ev=DT, glu=2 * DT, dve=2 * DT)
STAGES = [
    ("ada", dict(act=1, dve=1, ev=4)), ("norm_x", norm_steps(DT)), ("glu", dict(ev=8, glu=4)),
    ("qkv", dict(ev=12)), ("turn_v", turn_steps(4)), ("ln", dict(pe=2, act=5, dve=11)),
    ("attend1", dict(att=H1 * 4)), ("turn_o", turn_steps(4)), ("mix1", MIX), ("mixo1", dict(ev=8)),
    ("post_mix", norm_steps(DT)), ("norm_ffn1", norm_steps(DT)), ("up1", FFN1), ("down1", dict()),
    ("post_ffn1", norm_steps(DT)),
    ("norm_r", norm_steps(DT)), ("rlora", dict(ev=3, act=3)), ("rprep", dict()), ("rchunks", dict()),
    ("rout", dict()), ("norm_n", norm_steps(DT)), ("nsa", dict(ev=20)), ("nheads", heads_steps(3, 12)),
    ("cmp_k", dict()), ("cmp", dict(pe=6, act=6)), ("nturn", turn_steps(4)), ("attend2", dict(att=H2 * 4 * 3)),
    ("turn_o2", turn_steps(8)), ("mix2", MIX), ("mixo2", dict(ev=8)), ("norm_c", norm_steps(DT)),
    ("caq", dict(ev=8)), ("norm_m", norm_steps(DT)), ("cakv", dict(ev=16)), ("qheads", heads_steps(2, 8)),
    ("kheads", heads_steps(2, 8)), ("turn_v3", turn_steps(4)), ("attend3", dict(att=CA_HEADS * 4)),
    ("turn_o3", turn_steps(8)), ("cao", dict(ev=8)), ("norm_f", norm_steps(DT)), ("up2", FFN2),
    ("down2", dict()),
]
COUNTERS = ("act", "dve", "pe", "ev", "att", "glu", "tap", "conv", "gelu")


Base = namedtuple("Base", ("index",) + COUNTERS)

BASE = {}
_values = {name: 0 for name in COUNTERS}
for _index, (_name, _steps) in enumerate(STAGES):
    BASE[_name] = Base(_index, **_values)
    for _k, _v in _steps.items():
        _values[_k] += _v


def build_program(nc, stream, cols, const, onehot, x_t, mem_t, line1, table2, w2a2, g2, cmp_w2, out, scratch, rows):
    with ExitStack() as ctx:
        def sb(name, shape):
            return ctx.enter_context(nc.sbuf_tensor(name, shape, F32))

        def sem(name):
            return ctx.enter_context(nc.semaphore(name))

        X = sb("X", [P, DT, S])
        H = sb("H", [P, DT, S])
        W = sb("W", [P, W_SLOTS, D])
        PRM = sb("PRM", [P, N_COLS])
        CON = sb("CON", [P, N_CONST])
        SQ = sb("SQ", [P, 4, S])
        ST = sb("ST", [P, 2, S])
        MOD = sb("MOD", [P, 48])
        GM = sb("GM", [P, 5 * DT])
        OMU = sb("OMU", [P, 28])
        DEC = sb("DEC", [P, DT, S // CHUNK])
        GT = sb("GT", [P, S // P, 3 * H2])
        CW2 = sb("CW2", [P, 2, P + DH])
        TAB = sb("TAB", [BUCKETS, H2])
        SM = sb("SM", [P, 64])
        BIG = sb("BIG", [P, 68, S])
        psum = [ctx.enter_context(nc.psum_tensor(f"bank{b}", [P, S], F32)) for b in range(8)]

        def prm(name, j=0, n=1):
            return PRM[:, C0[name] + j:C0[name] + j + n]

        def con(name, n=None, lo=0, hi=P):
            width = dict(CONSTS)[name]
            return CON[lo:hi, K0[name]:K0[name] + (n or width)]

        s_prm = sem("params_loaded")
        s_x = sem("x_loaded")
        w_full = [sem(f"w_full{j}") for j in range(W_SLOTS)]
        unit_done = sem("unit_done")
        s_ev = sem("banks_read")
        s_act = sem("act_step")
        s_dve = sem("dve_step")
        s_pe = sem("pe_step")
        s_bar = sem("stage_end")
        s_sc = sem("scores_ready")
        s_sfree = sem("scores_read")
        s_mx = sem("max_ready")
        s_exp = sem("probs_ready")
        s_tr = sem("probs_turned")
        s_pt = sem("turned_copied")
        s_pv = sem("outputs_ready")
        s_of = sem("outputs_read")
        s_line = sem("bias_line")
        s_bias = sem("bias_loaded")
        s_out = sem("out_stored")
        s_glu = sem("gate_ready")
        s_tap = sem("first_tap_ready")
        s_conv = sem("conv_ready")
        s_gelu = sem("gelu_ready")
        s_mem = sem("mem_loaded")
        s_chain = sem("vector_chain")
        s_cv = sem("taps_done")
        s_blk = sem("blocks_ready")
        s_tap0 = sem("line_ready")
        s_pool = sem("pool_step")
        s_rows = sem("bias_rows_stored")
        s_small = sem("small_weights_loaded")
        s_lora = sem("lora_loaded")
        s_bias2 = sem("bias2_loaded")
        s_line2 = sem("bias2_line")
        e_keep = sem("unshifted_part_ready")
        e_shift = sem("shifted")
        e_log = sem("lora_products_ready")
        e_sig = sem("sigmoids_ready")
        e_scan = sem("log_decays_summed")
        e_dec = sem("decays_ready")
        e_kk = sem("kk_ready")
        e_sq = sem("kk_squared")
        e_ss = sem("kk_summed")
        e_root = sem("kk_norm_ready")
        e_rp = sem("bonus_terms_ready")
        e_bs = sem("bonus_summed")
        e_done = sem("tile_prepared")
        c_pe = sem("chunk_products")
        c_act = sem("chunk_copies")
        c_dve = sem("chunk_vector_steps")
        r_pe = sem("rout_products")
        r_act = sem("rout_scalar_steps")
        r_dve = sem("rout_vector_steps")

        class Steps:

            def __init__(self, s):
                self.s, self.n = s, 0

            def inc(self, ins):
                ins.then_inc(self.s, 1)
                self.n += 1

            def link(self, eng, ins):
                self.inc(ins)
                eng.wait_ge(self.s, self.n)

        def stage_end(eng, stage):
            eng.drain().then_inc(s_bar, 1)
            eng.wait_ge(s_bar, 3 * (BASE[stage].index + 1))


        def pe_unit(pe, stage, n, j, i, per, rhs, bank, ev_wait, lo=0):
            u = U0[stage] + j
            slot = u % W_SLOTS
            pe.wait_ge(w_full[slot], 16 * (u // W_SLOTS + 1) + (per // W_SLOTS) * 16 * i)
            if ev_wait is not None:
                pe.wait_ge(s_ev, ev_wait)
            for k, r in enumerate(rhs):
                last = nc.tensor.matmul(bank, W[:, slot, (lo + k) * P:(lo + k + 1) * P], r,
                                        start=(k == 0), stop=(k == len(rhs) - 1))
            return last

        def pe_project(pe, stage, rhs, n_units, width=S):
            base = BASE[stage]
            e0 = base.ev
            with pe.Fori(0, n_units // 4) as i:
                for j in range(4):
                    pe_unit(pe, stage, 0, j, i, 4, rhs, psum[j][:, 0:width], 4 * i + (e0 + j - 3))\
                        .then_inc(unit_done, 1)

        def act_project(act, stage, dst, n_units, bias=None, func=ACT.Identity, width=S):
            base = BASE[stage]
            u0 = U0[stage]
            with act.Fori(0, n_units // 4) as i:
                for j in range(4):
                    act.wait_ge(unit_done, 4 * i + (u0 + j + 1))
                    b = 0.0 if bias is None else PRM[:, bass.ds(C0[bias[0]] + bias[1] + j + 4 * i, 1)]
                    nc.scalar.activation(dst[:, 4 * i + j, 0:width], psum[j][:, 0:width], func, bias=b)\
                        .then_inc(s_ev, 1)

        def pe_norm(pe, stage, n, width=S):
            base = BASE[stage]
            for k in range(n):
                pe.wait_ge(s_act, base.act + k + 1)
                nc.tensor.matmul(psum[7][:, 0:width], con("ones"), SQ[:, k % 4, 0:width],
                                 start=(k == 0), stop=(k == n - 1)).then_inc(s_pe, 1)

        def act_norm(act, stage, src, n, width=S):
            base = BASE[stage]
            for k in range(n):
                if k >= 4:
                    act.wait_ge(s_pe, base.pe + k - 3)
                nc.scalar.activation(SQ[:, k % 4, 0:width], src[:, k, 0:width], ACT.Square).then_inc(s_act, 1)
            act.wait_ge(s_dve, base.dve + 1)
            nc.scalar.activation(ST[:, 1, 0:width], ST[:, 0, 0:width], ACT.Sqrt).then_inc(s_act, 1)

        def dve_rstd(dve, stage, n, width=S):
            base = BASE[stage]
            dve.wait_ge(s_pe, base.pe + n)
            nc.vector.tensor_scalar(ST[:, 0, 0:width], psum[7][:, 0:width], 1.0 / (n * P), EPS, ALU.mult, ALU.add)\
                .then_inc(s_dve, 1)
            dve.wait_ge(s_act, base.act + n + 1)
            nc.vector.reciprocal(ST[:, 0, 0:width], ST[:, 1, 0:width]).then_inc(s_dve, 1)
            dve.wait_ge(s_dve, base.dve + 2)

        def dve_norm(dve, stage, src, dst, gain, n, shift=None, width=S):
            base = BASE[stage]
            dve_rstd(dve, stage, n, width)
            for k in range(n):
                nc.vector.scalar_tensor_tensor(dst[:, k, 0:width], src[:, k, 0:width], gain[:, k:k + 1],
                                               ST[:, 0, 0:width], ALU.mult, ALU.mult).then_inc(s_dve, 1)
            if shift is not None:
                for k in range(n):
                    dve.wait_ge(s_dve, base.dve + 2 + k + 1)
                    nc.vector.tensor_scalar_add(dst[:, k, 0:width], dst[:, k, 0:width], shift[:, k:k + 1])

        def dve_residual(dve, stage, src, gain, n):
            base = BASE[stage]
            dve_rstd(dve, stage, n)
            for k in range(n):
                nc.vector.scalar_tensor_tensor(src[:, k, :], src[:, k, :], gain[:, k:k + 1],
                                               ST[:, 0, :], ALU.mult, ALU.mult).then_inc(s_dve, 1)
            for k in range(n):
                dve.wait_ge(s_dve, base.dve + 2 + k + 1)
                nc.vector.tensor_tensor(X[:, k, :], X[:, k, :], src[:, k, :], ALU.add)

        def pe_turn(pe, stage, blocks):
            base = BASE[stage]
            for b, four in enumerate(blocks):
                if b >= 4:
                    pe.wait_ge(s_act, base.act + b - 3)
                for q, src in enumerate(four):
                    last = nc.tensor.transpose(psum[b % 4][:, q * P:(q + 1) * P], src, con("ident"))
                last.then_inc(s_pe, 1)

        def act_turn(act, stage, dsts):
            base = BASE[stage]
            for b, dst in enumerate(dsts):
                act.wait_ge(s_pe, base.pe + b + 1)
                n = dst.shape[-1] if len(dst.shape) == 2 else dst.shape[-1] * dst.shape[-2]
                src = psum[b % 4][:, 0:n]
                if len(dst.shape) == 3:
                    src = src.rearrange("p (a b) -> p a b", b=dst.shape[-1])
                nc.scalar.activation(dst, src, ACT.Copy).then_inc(s_act, 1)

        def pe_attend(pe, stage, units):
            base = BASE[stage]
            a0 = base.att
            n = len(units)
            for i in range(n + 2):
                if i < n:
                    u = units[i]
                    if a0 + i >= 2:
                        pe.wait_ge(s_sfree, a0 + i - 1)
                    for c, (q, k) in enumerate(zip(u["q"], u["k"])):
                        last = nc.tensor.matmul(psum[i % 2][:, 0:u["nk"]], q, k, start=(c == 0),
                                                stop=(c == len(u["q"]) - 1))
                    last.then_inc(s_sc, 1)
                if 1 <= i <= n:
                    j = i - 1
                    u = units[j]
                    pe.wait_ge(s_exp, a0 + j + 1)
                    if a0 + j >= 2:
                        pe.wait_ge(s_pt, a0 + j - 1)
                    for b in range((u["nk"] + P - 1) // P):
                        w = min(P, u["nk"] - b * P)
                        out_t, in_t = psum[2 + j % 2][0:w, b * P:(b + 1) * P], PB[:, j % 2, b * P:b * P + w]
                        if w == P:
                            last = nc.tensor.transpose(out_t, in_t, con("ident"))
                        else:
                            last = nc.tensor.matmul(out_t, in_t, con("ident"), start=True, stop=True)
                    last.then_inc(s_tr, 1)
                if i >= 2:
                    j = i - 2
                    u = units[j]
                    pe.wait_ge(s_pt, a0 + j + 1)
                    if a0 + j >= 2:
                        pe.wait_ge(s_of, a0 + j - 1)
                    for b, v in enumerate(u["v"]):
                        w = v.shape[0]
                        last = nc.tensor.matmul(psum[4 + j % 2][:, 0:v.shape[1]], PT[0:w, j % 2, b * P:(b + 1) * P],
                                                v, start=(b == 0), stop=(b == len(u["v"]) - 1))
                    last.then_inc(s_pv, 1)

        def dve_attend(dve, stage, units, steps):
            base = BASE[stage]
            a0 = base.att
            n = len(units)
            for i in range(n + 2):
                if i < n:
                    u = units[i]
                    nk = u["nk"]
                    dve.wait_ge(s_sc, a0 + i + 1)
                    if a0 + i >= 2:
                        dve.wait_ge(s_tr, a0 + i - 1)
                    if u["bias"] is None:
                        ins = nc.vector.tensor_scalar(PB[:, i % 2, 0:nk], psum[i % 2][:, 0:nk], u["scale"], None,
                                                      ALU.mult)
                    else:
                        ins = nc.vector.scalar_tensor_tensor(PB[:, i % 2, 0:nk], psum[i % 2][:, 0:nk], u["scale"],
                                                             u["bias"], ALU.mult, ALU.add)
                    ins.then_inc(s_sfree, 1)
                    dve.wait_ge(s_sfree, a0 + i + 1)
                    if u["guard"]:
                        steps.link(dve, nc.vector.tensor_reduce(SM[:, i % 2:i % 2 + 1], PB[:, i % 2, 0:nk], AX_X,
                                                                ALU.max, negate=True))
                        nc.vector.tensor_scalar(SM[:, i % 2:i % 2 + 1], SM[:, i % 2:i % 2 + 1], -0.01 * NEG, None,
                                                ALU.min).then_inc(s_mx, 1)
                    else:
                        nc.vector.tensor_reduce(SM[:, i % 2:i % 2 + 1], PB[:, i % 2, 0:nk], AX_X, ALU.max,
                                                negate=True).then_inc(s_mx, 1)
                if i >= 2:
                    j = i - 2
                    u = units[j]
                    m = 4 + j % 4
                    dve.wait_ge(s_exp, a0 + j + 1)
                    if u["guard"]:
                        steps.link(dve, nc.vector.tensor_scalar(SM[:, 8 + j % 2:9 + j % 2], SM[:, m:m + 1], 0.5, None, ALU.max))
                        steps.link(dve, nc.vector.reciprocal(SM[:, 10 + j % 2:11 + j % 2], SM[:, 8 + j % 2:9 + j % 2]))
                    else:
                        steps.link(dve, nc.vector.reciprocal(SM[:, 10 + j % 2:11 + j % 2], SM[:, m:m + 1]))
                    f = SM[:, 10 + j % 2:11 + j % 2]
                    if u["gate"] is not None:
                        steps.link(dve, nc.vector.tensor_tensor(SM[:, 12 + j % 2:13 + j % 2], f, u["gate"], ALU.mult))
                        f = SM[:, 12 + j % 2:13 + j % 2]
                    dve.wait_ge(s_pv, a0 + j + 1)
                    src = psum[4 + j % 2][:, 0:u["v"][0].shape[1]]
                    if u["add"]:
                        ins = nc.vector.scalar_tensor_tensor(u["out"], src, f, u["out"], ALU.mult, ALU.add)
                    else:
                        ins = nc.vector.tensor_scalar(u["out"], src, f, None, ALU.mult)
                    ins.then_inc(s_of, 1)
                    dve.wait_ge(s_of, a0 + j + 1)

        def act_attend(act, stage, units):
            base = BASE[stage]
            a0 = base.att
            n = len(units)
            for i in range(n + 1):
                if i < n:
                    u = units[i]
                    nk = u["nk"]
                    m = 4 + i % 4
                    act.wait_ge(s_mx, a0 + i + 1)
                    if a0 + i >= 4:
                        act.wait_ge(s_of, a0 + i - 3)
                    nc.scalar.activation(PB[:, i % 2, 0:nk], PB[:, i % 2, 0:nk], ACT.Exp, bias=SM[:, i % 2:i % 2 + 1],
                                         accum_out=SM[:, m:m + 1]).then_inc(s_exp, 1)
                if i >= 1:
                    j = i - 1
                    u = units[j]
                    nb = (u["nk"] + P - 1) // P
                    w = min(P, u["nk"])
                    act.wait_ge(s_tr, a0 + j + 1)
                    if a0 + j >= 2:
                        act.wait_ge(s_pv, a0 + j - 1)
                    nc.scalar.activation(PT[0:w, j % 2, 0:nb * P], psum[2 + j % 2][0:w, 0:nb * P], ACT.Copy)\
                        .then_inc(s_pt, 1)

        def pe_mix(pe, stage, per, gate_rhs, rhs_a, rhs_b):
            base = BASE[stage]
            e0 = base.ev
            tiles = 4 if per == 3 else 2
            with pe.Fori(0, DT // tiles) as i:
                for j in range(tiles):
                    bk = [psum[4 * (j % 2) + q][:, :] for q in range(4)]
                    ev = tiles * i + (e0 + j - 1)
                    u = per * j
                    pe_unit(pe, stage, 0, u, i, per * tiles, gate_rhs, bk[0], ev).then_inc(unit_done, 1)
                    if per == 3:
                        pe_unit(pe, stage, 0, u + 1, i, per * tiles, rhs_a, bk[1], None)
                        pe_unit(pe, stage, 0, u + 1, i, per * tiles, rhs_b, bk[3], None, lo=4).then_inc(unit_done, 1)
                        pe_unit(pe, stage, 0, u + 2, i, per * tiles, gate_rhs, bk[2], None).then_inc(unit_done, 1)
                    else:
                        pe_unit(pe, stage, 0, u + 1, i, per * tiles, rhs_a, bk[1], None).then_inc(unit_done, 1)
                        pe_unit(pe, stage, 0, u + 2, i, per * tiles, gate_rhs, bk[2], None).then_inc(unit_done, 1)
                        pe_unit(pe, stage, 0, u + 3, i, per * tiles, rhs_b, bk[3], None).then_inc(unit_done, 1)

        def act_mix(act, stage, per, bias_a, bias_b):
            base = BASE[stage]
            tiles = 4 if per == 3 else 2
            e0, g0, u0 = base.ev, base.glu, U0[stage]
            with act.Fori(0, DT // tiles) as i:
                for j in range(tiles):
                    n = tiles * i + j
                    act.wait_ge(s_ev, tiles * i + (e0 + j - 1))
                    for h, bias in enumerate((bias_a, bias_b)):
                        act.wait_ge(unit_done, per * tiles * i + (u0 + per * j + 2 * h + 1))
                        b = 0.0 if bias is None else PRM[:, bass.ds(C0["b_in"] + bias + j + tiles * i, 1)]
                        nc.scalar.activation(SQ[:, 2 * (j % 2) + h, :], psum[4 * (j % 2) + 2 * h][:, :], ACT.Sigmoid,
                                             bias=b).then_inc(s_glu, 1)

        def dve_mix(dve, stage, per, dst, bias):
            base = BASE[stage]
            tiles = 4 if per == 3 else 2
            e0, g0, u0, d0 = base.ev, base.glu, U0[stage], base.dve
            with dve.Fori(0, DT // tiles) as i:
                for j in range(tiles):
                    last = per * tiles * i + (u0 + per * (j + 1))
                    dve.wait_ge(s_glu, 2 * tiles * i + (g0 + 2 * j + 2))
                    dve.wait_ge(unit_done, last)
                    t = SQ[:, 2 * (j % 2), :]
                    v = SQ[:, 2 * (j % 2) + 1, :]
                    nc.vector.tensor_tensor(t, psum[4 * (j % 2) + 1][:, :], t, ALU.mult).then_inc(s_dve, 1)
                    b = 0.0 if bias is None else PRM[:, bass.ds(C0[bias] + j + tiles * i, 1)]
                    nc.vector.scalar_tensor_tensor(v, psum[4 * (j % 2) + 3][:, :], b, v, ALU.add, ALU.mult)\
                        .then_inc(s_dve, 1)
                    dve.wait_ge(s_dve, 2 * tiles * i + (d0 + 2 * j + 2))
                    nc.vector.tensor_tensor(dst[:, tiles * i + j, :], t, v, ALU.add).then_inc(s_ev, 1)

        def pe_up(pe, stage):
            base = BASE[stage]
            e0 = base.ev
            with pe.Fori(0, FT // 2) as i:
                for j in range(4):
                    pe_unit(pe, stage, 0, j, i, 4, h_tiles, psum[j][:, :], 4 * i + (e0 + j - 3)).then_inc(unit_done, 1)

        def taps(name, j, i, t):
            return PRM[:, bass.ds(C0[name] + 3 * j + t + 6 * i, 1)]

        def act_up(act, stage, both):
            base = BASE[stage]
            e0, u0, c0, t0, g0 = base.ev, U0[stage], base.conv, base.tap, base.gelu
            w, b = ("w_dw_ffn", "b_dw_ffn") if both else ("ffn_conv", "ffn_conv_b")
            with act.Fori(0, FT // 2) as i:
                for j in range(2):
                    act.wait_ge(s_ev, 4 * i + (e0 + 2 * j - 2))
                    for h in range(2 if both else 1):
                        off = FT * h
                        act.wait_ge(unit_done, 4 * i + (u0 + 2 * j + h + 1))
                        nc.scalar.activation(SQ[:, 2 * j + h, :], psum[2 * j + h][:, :], ACT.Identity,
                                             scale=taps(w, off + j, i, 2),
                                             bias=PRM[:, bass.ds(C0[b] + off + j + 2 * i, 1)]).then_inc(s_tap, 1)
                    act.wait_ge(s_conv, 2 * i + (c0 + j + 1))
                    t = SQ[:, 2 * j + (1 if both else 0), :]
                    nc.scalar.activation(t, t, ACT.Gelu_apprx_tanh if both else ACT.Silu).then_inc(s_gelu, 1)

        def dve_up(dve, stage, both, hid):
            base = BASE[stage]
            e0, u0, c0, t0, g0, d0 = base.ev, U0[stage], base.conv, base.tap, base.gelu, base.dve
            w = "w_dw_ffn" if both else "ffn_conv"
            nh = 2 if both else 1
            with dve.Fori(0, FT // 2) as i:
                for j in range(2):
                    for h in range(nh):
                        off = FT * h
                        t, bank = SQ[:, 2 * j + h, :], psum[2 * j + h]
                        dve.wait_ge(s_tap, 2 * nh * i + (t0 + nh * j + h + 1))
                        nc.vector.scalar_tensor_tensor(t[:, 1:S], bank[:, 0:S - 1], taps(w, off + j, i, 1),
                                                       t[:, 1:S], ALU.mult, ALU.add).then_inc(s_dve, 1)
                    for h in range(nh):
                        off = FT * h
                        t, bank = SQ[:, 2 * j + h, :], psum[2 * j + h]
                        dve.wait_ge(s_dve, 2 * nh * i + (d0 + nh * j + h + 1))
                        ins = nc.vector.scalar_tensor_tensor(t[:, 2:S], bank[:, 0:S - 2], taps(w, off + j, i, 0),
                                                             t[:, 2:S], ALU.mult, ALU.add)
                    ins.then_inc(s_conv, 1)
                    dve.wait_ge(s_gelu, 2 * i + (g0 + j + 1))
                    if both:
                        dve.wait_ge(s_conv, 2 * i + (c0 + j + 1))
                        val = SQ[:, 2 * j, :]
                        gt = SQ[:, 2 * j + 1, :]
                    else:
                        dve.wait_ge(unit_done, 4 * i + (u0 + 2 * j + 2))
                        val = psum[2 * j + 1][:, :]
                        gt = SQ[:, 2 * j, :]
                    nc.vector.tensor_tensor(hid[:, 2 * i + j, :], val, gt, ALU.mult).then_inc(s_ev, 2)

        def pe_down(pe, stage, hid):
            base = BASE[stage]
            u0 = U0[stage]

            def unit(j, i, k, start=False, stop=False):
                u = u0 + j
                slot = u % W_SLOTS
                pe.wait_ge(w_full[slot], 16 * (u // W_SLOTS + 1) + 16 * i)
                for n in range(DT):
                    last = nc.tensor.matmul(psum[n][:, :], W[:, slot, n * P:(n + 1) * P], hid[:, k, :],
                                            start=start, stop=stop)
                last.then_inc(unit_done, 1)

            unit(0, 0, 0, start=True)
            with pe.Fori(0, (FT - 2) // 4) as i:
                for j in range(4):
                    unit(1 + j, i, 4 * i + (1 + j))
            unit(FT - 1, 0, FT - 1, stop=True)

        def act_down(act, stage, dst):
            base = BASE[stage]
            act.wait_ge(unit_done, U0[stage] + FT)
            for n in range(0, DT, 2):
                nc.scalar.activation(dst[:, n, :], psum[n][:, :], ACT.Copy)

        def dve_down(dve, stage, dst):
            base = BASE[stage]
            dve.wait_ge(unit_done, U0[stage] + FT)
            for n in range(1, DT, 2):
                nc.vector.tensor_copy(dst[:, n, :], psum[n][:, :])


        def dve_add_project(dve, stage, n_units):
            base = BASE[stage]
            u0 = U0[stage]
            with dve.Fori(0, n_units // 4) as i:
                for j in range(4):
                    dve.wait_ge(unit_done, 4 * i + (u0 + j + 1))
                    nc.vector.tensor_tensor(X[:, 4 * i + j, :], X[:, 4 * i + j, :], psum[j][:, :], ALU.add)\
                        .then_inc(s_ev, 1)

        def pe_heads(pe, stage, n, ones, group, width=S):
            base = BASE[stage]
            for t in range(0, n, 4):
                for k in range(4):
                    b = 4 + k // group
                    pe.wait_ge(s_act, base.act + t + t // 4 + k + 1)
                    nc.tensor.matmul(psum[b][:, 0:width], ones, SQ[:, k, 0:width], start=(k % group == 0),
                                     stop=(k % group == group - 1)).then_inc(s_pe, 1)

        def act_heads(act, stage, src, n, group, width=S):
            base = BASE[stage]
            for t in range(0, n, 4):
                if t:
                    act.wait_ge(s_dve, base.dve + (2 * 4 + 1) * (t // 4))
                for k in range(4):
                    nc.scalar.activation(SQ[:, k, 0:width], src[t + k], ACT.Square).then_inc(s_act, 1)
                act.wait_ge(s_dve, base.dve + (2 * 4 + 1) * (t // 4) + 4 // group)
                nc.scalar.activation(SQ[:, 0:4 // group, 0:width], SQ[:, 0:4 // group, 0:width], ACT.Sqrt)\
                    .then_inc(s_act, 1)

        def dve_heads(dve, stage, src, n, group, gain, width, dim):
            base = BASE[stage]
            for t in range(0, n, 4):
                d0 = base.dve + (2 * 4 + 1) * (t // 4)
                for k in range(4 // group):
                    dve.wait_ge(s_pe, base.pe + t + 4)
                    nc.vector.tensor_scalar(SQ[:, k, 0:width], psum[4 + k][:, 0:width], 1.0 / dim, EPS, ALU.mult,
                                            ALU.add).then_inc(s_dve, 1)
                dve.wait_ge(s_act, base.act + t + t // 4 + 5)
                nc.vector.reciprocal(SQ[:, 0:4 // group, 0:width], SQ[:, 0:4 // group, 0:width]).then_inc(s_dve, 1)
                dve.wait_ge(s_dve, d0 + 4 // group + 1)
                for k in range(4):
                    ins = nc.vector.scalar_tensor_tensor(src[t + k], src[t + k], gain[t + k], SQ[:, k // group, 0:width],
                                                         ALU.mult, ALU.mult)
                    ins.then_inc(s_dve, 1 if k < 3 else 1 + 4 - 4 // group)

        h_tiles = [H[:, k, :] for k in range(DT)]

        def tiles(a, n):
            return [BIG[:, a + k, :] for k in range(n)]

        PB = BIG[:, 41:43, :]
        PT = BIG[:, 43:45, :]
        Q1, K1, V1 = BIG[:, 0:4, :], BIG[:, 4:8, :], BIG[:, 8:12, :]
        VT1 = BIG[:, 12:16, :]
        LEAD = 32
        GPAD = LEAD + S
        GLU = BIG[:, 16:21, :].rearrange("p a b -> p (a b)")[:, 0:4 * GPAD].rearrange("p (a b) -> p a b", b=GPAD)
        CV = BIG[:, 21:25, :]
        O1 = BIG[:, 25:29, :]
        OT1 = BIG[:, 29:33, :]
        BIAS1 = BIG[:, 33:41, :]
        Y1 = BIG[:, 45:53, :]
        Z1 = BIG[:, 53:61, :]
        HID = BIG[:, 0:FT, :]
        RT, AT, BT, KT = BIG[:, 0:8, :], BIG[:, 8:16, :], BIG[:, 16:24, :], BIG[:, 24:32, :]
        RV, BON = BIG[:, 32:40, :], BIG[:, 40:48, :]
        ZL = BIG[:, 48:51, :]
        LR = BIG[:, 51:57, :].rearrange("p a b -> p (a b)").rearrange("p (a b) -> p a b", b=D)
        TMP = tiles(57, 11)
        YR = AT
        QN = BIG[:, 16:24, :]
        NSA = BIG[:, 16:36, :]
        KC, VC, KS, VS, KW, VW = (BIG[:, 24 + 2 * k:26 + 2 * k, :] for k in range(6))
        VT2 = BIG[:, 36:40, :]
        SH = BIG[:, 0:4, :]
        BLK = BIG[:, 4:8, :].rearrange("p a b -> p (a b)")[:, 0:16 * 4 * N_CMP].rearrange("p (k n) -> p k n", k=16)
        BLK_V = BIG[:, 48:52, :].rearrange("p a b -> p (a b)")[:, 0:16 * 4 * N_CMP].rearrange("p (k n) -> p k n", k=16)
        HC = BIG[:, 45, 0:2 * 4 * N_CMP].rearrange("p (c n) -> p c n", c=2)
        HV = BIG[:, 46, 0:2 * 4 * N_CMP].rearrange("p (c n) -> p c n", c=2)
        KCN = BIG[:, 47, 0:4 * N_CMP]
        VCT = BIG[:, 47, 128:128 + 4 * DH]
        BIAS2 = BIG[:, 52:68, :]
        O2 = BIG[:, 0:8, :].rearrange("p a b -> p (a b)").rearrange("p (a b) -> p a b", b=D)
        OT2 = BIG[:, 16:24, :]
        Y2 = BIG[:, 24:32, :]
        Q3, K3, V3 = BIG[:, 0:8, :], BIG[:, 8:16, 0:N_MEM], BIG[:, 16:24, 0:N_MEM]
        VT3 = BIG[:, 24:28, :].rearrange("p a b -> p (a b)").rearrange("p (a b) -> p a b", b=D)
        MEM, MN = BIG[:, 48:56, :], BIG[:, 56:64, :]
        O3 = BIG[:, 28:36, :].rearrange("p a b -> p (a b)").rearrange("p (a b) -> p a b", b=D)
        OT3 = BIG[:, 8:16, :]

        units1 = []
        for h in range(H1):
            lo = DH * (h % 2)
            for qi in range(S // P):
                nk = P * (qi + 1)
                units1.append(dict(
                    q=[Q1[lo:lo + DH, h // 2, qi * P:(qi + 1) * P]], k=[K1[lo:lo + DH, h // 2, 0:nk]], nk=nk,
                    bias=BIAS1[:, h, S - nk:S], scale=DH ** -0.5,
                    v=[VT1[:, b, h * DH:(h + 1) * DH] for b in range(qi + 1)],
                    out=O1[:, qi, h * DH:(h + 1) * DH], gate=None, add=False, guard=False))

        units2 = []
        for h in range(H2):
            g, hg = h // HG, h % HG
            lo = DH * (g % 2)
            for qi in range(S // P):
                nk = P * (qi + 1)
                q = QN[lo:lo + DH, (g // 2) * HG + hg, qi * P:(qi + 1) * P]
                out_ap = O2[:, qi, h * DH:(h + 1) * DH]
                for br, (keys, vcol) in enumerate(((KS, 0), (KW, N_KV * DH))):
                    units2.append(dict(
                        q=[q], k=[keys[lo:lo + DH, g // 2, 0:nk]], nk=nk, bias=BIAS2[:, h, S - nk:S],
                        scale=DH ** -0.5, v=[VT2[:, b, vcol + g * DH:vcol + (g + 1) * DH] for b in range(qi + 1)],
                        out=out_ap, gate=GT[:, qi, 3 * h + 1 + br:3 * h + 2 + br], add=(br == 1), guard=False))
                nc_keys = min(N_CMP, (P * (qi + 1) - CMP_BLOCK) // CMP_STRIDE + 1)
                first = S - P * (qi + 1) + CMP_BLOCK - 1
                units2.append(dict(
                    q=[q], k=[KCN[lo:lo + DH, g * N_CMP:g * N_CMP + nc_keys]], nk=nc_keys,
                    bias=BIAS2[:, h, first:first + CMP_STRIDE * (nc_keys - 1) + 1:CMP_STRIDE], scale=DH ** -0.5,
                    v=[VCT[0:nc_keys, g * DH:(g + 1) * DH]], out=out_ap, gate=GT[:, qi, 3 * h:3 * h + 1],
                    add=True, guard=True))

        units3 = []
        for h in range(CA_HEADS):
            for qi in range(S // P):
                units3.append(dict(
                    q=[Q3[:, 2 * h + c, qi * P:(qi + 1) * P] for c in range(2)],
                    k=[K3[:, 2 * h + c, :] for c in range(2)], nk=N_MEM, bias=None, scale=(D // CA_HEADS) ** -0.5,
                    v=[VT3[:, b, h * 256:(h + 1) * 256] for b in range(2)],
                    out=O3[:, qi, h * 256:(h + 1) * 256], gate=None, add=False, guard=False))

        free = TMP + tiles(51, 2) + h_tiles + [SQ[:, k, :] for k in range(4)]
        (AKT, RBT, RKT, Bt, Kt, Vt, XI, FT2, FT4, ND, MD, MO, N2, M2, N4, M4, M8, F2, Rs, U0s, U1s, Us, TS, TN) = free[:24]

        def pair3(ap):
            return ap.rearrange("p (j c) -> p j c", c=CHUNK)

        def mask3(name):
            return con(name).rearrange("p (j c) -> p j c", j=1).to_broadcast([P, DT, CHUNK])

        def pe_rchunks(pe):
            def full(tile, c):
                return lambda lo, j: tile[lo:lo + DH, j, c * CHUNK:(c + 1) * CHUNK]

            def loc(tile):
                return lambda lo, j: tile[lo:lo + CHUNK, j * CHUNK:(j + 1) * CHUNK]

            def eye():
                return lambda lo, j: CON[lo:lo + DH, K0["ident"] + lo:K0["ident"] + lo + DH]

            def products(bank, *pairs):
                for lo in (0, CHUNK):
                    for j in range(DT):
                        for q, (lhs, rhs) in enumerate(pairs):
                            last = nc.tensor.matmul(psum[bank][lo:lo + CHUNK, j * CHUNK:(j + 1) * CHUNK],
                                                    lhs(lo, j), rhs(lo, j), start=(q == 0), stop=(q == len(pairs) - 1))
                last.then_inc(c_pe, 1)

            for c in range(S // CHUNK):
                a0, d0 = 14 * c, 14 * c

                def act(n):
                    pe.wait_ge(c_act, a0 + n)

                def vec(n):
                    pe.wait_ge(c_dve, d0 + 1 + n)

                r, a, b, k, v = (full(t, c) for t in (RT, AT, BT, KT, RV))
                if c:
                    vec(0)
                    act(0)
                products(0, (b, a))
                products(1, (a, b))
                products(2, (k, a))
                products(3, (b, r))
                products(4, (k, r))
                products(5, (b, eye()))
                products(6, (k, eye()))
                products(7, (v, eye()))
                vec(3)
                products(0, (loc(MD), loc(ND)))
                products(1, (loc(ND), loc(MD)))
                vec(5)
                act(5)
                products(2, (loc(M2), loc(XI)))
                vec(7)
                products(3, (loc(M2), loc(N2)))
                products(4, (loc(N2), loc(M2)))
                act(7)
                vec(8)
                products(5, (loc(M4), loc(XI)))
                products(6, (loc(N4), loc(M4)))
                act(8)
                vec(9)
                products(7, (loc(M8), loc(XI)))
                vec(10)
                products(0, (loc(MO), loc(XI)))
                products(1, (loc(XI), loc(MO)))
                act(10)
                products(2, (loc(F2), loc(FT2)))
                pe.wait_ge(c_dve, 14 * c + 1)
                products(3, (a, loc(TS)), (loc(AKT), loc(Vt)))
                act(12)
                products(4, (loc(XI), loc(Rs)))
                act(13)
                products(5, (loc(FT4), loc(U0s)))
                vec(11)
                products(6, (loc(FT2), loc(U1s)))
                vec(12)
                products(7, (loc(TS), r), (loc(Us), loc(RBT)), (loc(Vt), loc(RKT)))
                products(0, (loc(Bt), loc(Us)), (loc(Kt), loc(Vt)))

        def act_rchunks(act):
            for c in range(S // CHUNK):
                p0, d0 = 25 * c, 14 * c + 1
                a = [0]

                def copy(dst, bank, after):
                    act.wait_ge(c_pe, p0 + after)
                    src = psum[bank][:, :]
                    nc.scalar.activation(dst, pair3(src) if len(dst.shape) == 3 else src, ACT.Copy).then_inc(c_act, 1)

                copy(Bt, 5, 6)
                copy(Kt, 6, 7)
                copy(Vt, 7, 8)
                copy(N2, 0, 9)
                copy(M2, 1, 10)
                copy(N4, 3, 12)
                copy(M4, 4, 13)
                copy(M8, 6, 15)
                copy(FT2, 0, 17)
                copy(F2, 1, 18)
                copy(FT4, 2, 19)
                copy(Rs, 3, 20)
                copy(U0s, 4, 21)
                copy(RT[:, :, c * CHUNK:(c + 1) * CHUNK], 7, 24)

        def dve_rchunks(dve):
            nc.vector.memset(TS, 0.0).then_inc(c_dve, 1)
            for c in range(S // CHUNK):
                p0, a0, d0 = 25 * c, 14 * c, 14 * c + 1

                def need(n):
                    dve.wait_ge(c_pe, p0 + n)

                def masked(dst, bank, mask):
                    nc.vector.tensor_tensor(pair3(dst), pair3(psum[bank][:, :]), mask3(mask), ALU.mult).then_inc(c_dve, 1)

                need(2)
                masked(ND, 0, "up16")
                masked(MD, 1, "lo16")
                masked(MO, 1, "lo_off")
                dve.wait_ge(c_dve, d0 + 1)
                nc.vector.tensor_tensor(pair3(XI), pair3(ND), mask3("eye64"), ALU.add).then_inc(c_dve, 1)
                need(3)
                masked(AKT, 2, "strict_up")
                need(4)
                masked(RBT, 3, "incl_up")
                need(5)
                masked(RKT, 4, "incl_up")
                for n, (bank, after) in enumerate(((2, 11), (5, 14), (7, 16))):
                    need(after)
                    dve.wait_ge(c_dve, d0 + (4 if n == 0 else 7 + n))
                    nc.vector.tensor_tensor(XI, psum[bank][:, :], XI, ALU.add).then_inc(c_dve, 1)
                need(22)
                dve.wait_ge(c_act, a0 + 13)
                nc.vector.tensor_tensor(U1s, psum[5][:, :], U0s, ALU.add).then_inc(c_dve, 1)
                need(23)
                dve.wait_ge(c_dve, d0 + 11)
                nc.vector.tensor_tensor(Us, psum[6][:, :], U1s, ALU.add).then_inc(c_dve, 1)
                need(25)
                nc.vector.tensor_tensor(TN, psum[0][:, :], TS, ALU.add).then_inc(c_dve, 1)
                dve.wait_ge(c_dve, d0 + 13)
                nc.vector.tensor_tensor(pair3(TS), pair3(TN),
                                        DEC[:, :, c:c + 1].to_broadcast([P, DT, CHUNK]), ALU.mult).then_inc(c_dve, 1)

        UK = U0["rkv"]
        EH = float(np.exp(-0.5))

        def pe_rprep(pe):
            pe.wait_ge(s_lora, 32)

            def sums(j):
                pe.wait_ge(e_sq, j + 1)
                nc.tensor.matmul(psum[5][:, :], con("blk"), SQ[:, 0, :], start=True, stop=True).then_inc(e_ss, 1)
                pe.wait_ge(e_rp, j + 1)
                nc.tensor.matmul(psum[6][:, :], con("blk"), SQ[:, 1, :], start=True, stop=True).then_inc(e_bs, 1)

            for j in range(DT):
                if j:
                    pe.wait_ge(e_sig, 2 * j)
                nc.tensor.matmul(psum[3][:, :], LR[0:64, 0, j * P:(j + 1) * P], ZL[0:64, 0, :], start=True, stop=True)
                nc.tensor.matmul(psum[4][:, :], LR[64:128, 0, j * P:(j + 1) * P], ZL[64:128, 0, :], start=True,
                                 stop=True).then_inc(e_log, 1)
                for q in range(3):
                    if j:
                        pe.wait_ge(e_shift, 3 * j - 2 + q)
                    pe_unit(pe, "rkv", 0, 3 * j + q, 0, 0, h_tiles, psum[q][:, :], None).then_inc(unit_done, 1)
                    if q == 0 and j:
                        sums(j - 1)
            sums(DT - 1)

        def act_rprep(act):
            sw, a, cs, ex, rt = TMP[0], TMP[1], TMP[2], TMP[3], TMP[4]
            for j in range(DT):
                act.wait_ge(e_log, j + 1)
                if j:
                    act.wait_ge(e_done, j)
                nc.scalar.activation(sw, psum[3][:, :], ACT.Sigmoid, bias=prm("w0", j)).then_inc(e_sig, 1)
                nc.scalar.activation(a, psum[4][:, :], ACT.Sigmoid, bias=prm("a0", j)).then_inc(e_sig, 1)
                for q, dst in enumerate((KT, RT, RV)):
                    act.wait_ge(unit_done, UK + 3 * j + q + 1)
                    nc.scalar.activation(dst[:, j, :], psum[q][:, :], ACT.Copy, scale=OMU[:, 4 + 3 * j + q:5 + 3 * j + q])\
                        .then_inc(e_keep, 1)
                act.wait_ge(e_kk, j + 1)
                nc.scalar.activation(SQ[:, 0, :], TMP[5], ACT.Square).then_inc(e_sq, 1)
                act.wait_ge(e_scan, j + 1)
                nc.scalar.activation(rt, cs, ACT.Exp, scale=-EH).then_inc(e_dec, 1)
                nc.scalar.activation(ex, ex, ACT.Exp, scale=-EH).then_inc(e_dec, 1)
                nc.scalar.activation(TMP[8], cs, ACT.Exp, scale=EH).then_inc(e_dec, 1)
                act.wait_ge(e_ss, j + 1)
                nc.scalar.activation(TMP[6], psum[5][:, :], ACT.Sqrt).then_inc(e_root, 1)

        def dve_rprep(dve, steps):
            V = nc.vector
            sw, a, cs, ex, inc, kk, nrm, k2, inv = TMP[0], TMP[1], TMP[2], TMP[3], TMP[4], TMP[5], TMP[6], TMP[7], TMP[8]
            for j in range(DT):
                k, r, v = KT[:, j, :], RT[:, j, :], RV[:, j, :]
                for q, dst in enumerate((k, r, v)):
                    dve.wait_ge(e_keep, 3 * j + q + 1)
                    V.scalar_tensor_tensor(dst[:, 1:S], psum[q][:, 0:S - 1], prm("mu", 4 + 3 * j + q), dst[:, 1:S],
                                           ALU.mult, ALU.add).then_inc(e_shift, 1)
                dve.wait_ge(e_shift, 3 * j + 3)
                V.tensor_scalar(kk, k, prm("kk", j), None, ALU.mult).then_inc(e_kk, 1)
                dve.wait_ge(e_sig, 2 * j + 2)
                steps.link(dve, V.tensor_tensor_scan(cs, con("scan"), sw, 0.0, ALU.mult, ALU.add))
                V.tensor_tensor(ex, cs, sw, ALU.subtract).then_inc(e_scan, 1)
                steps.link(dve, V.tensor_scalar(k2, a, 1.0, prm("ka", j), ALU.subtract, ALU.mult))
                steps.link(dve, V.scalar_tensor_tensor(k2, k2, 1.0, k, ALU.add, ALU.mult))
                if j:
                    dve.wait_ge(e_bs, j)
                V.scalar_tensor_tensor(SQ[:, 1, :], r, prm("rk", j), k2, ALU.mult, ALU.mult).then_inc(e_rp, 1)
                dve.wait_ge(e_dec, 3 * j + 3)
                V.tensor_copy(DEC[:, j, :], inc[:, CHUNK - 1:S:CHUNK])
                dve.wait_ge(e_rp, j + 1)
                V.tensor_tensor(r, r, inc, ALU.mult)
                V.tensor_tensor(k, k2, inv, ALU.mult)
                dve.wait_ge(e_root, j + 1)
                steps.link(dve, V.tensor_scalar(nrm, nrm, 1e-12, None, ALU.max))
                steps.link(dve, V.reciprocal(nrm, nrm))
                dve.wait_ge(e_kk, j + 1)
                steps.link(dve, V.tensor_tensor(kk, kk, nrm, ALU.mult))
                V.scalar_tensor_tensor(AT[:, j, :], kk, -1.0, ex, ALU.mult, ALU.mult)
                steps.link(dve, V.tensor_tensor(a, a, inv, ALU.mult))
                V.tensor_tensor(BT[:, j, :], kk, a, ALU.mult)
                dve.wait_ge(e_bs, j + 1)
                V.tensor_tensor(BON[:, j, :], psum[6][:, :], v, ALU.mult).then_inc(e_done, 1)

        def pe_rout(pe):
            for j in range(DT):
                if j:
                    pe.wait_ge(r_dve, 6 * j)
                nc.tensor.matmul(psum[0][:, :], con("blk"), RT[:, j, :], start=True, stop=True).then_inc(r_pe, 1)
                nc.tensor.matmul(psum[2][:, :], LR[:, 1, j * P:(j + 1) * P], ZL[:, 1, :], start=True, stop=False)
                nc.tensor.matmul(psum[2][:, :], LR[0:32, 2, j * P:(j + 1) * P], ZL[0:32, 2, :], start=False, stop=True)\
                    .then_inc(r_pe, 1)
                pe.wait_ge(r_act, 3 * j + 1)
                nc.tensor.matmul(psum[1][:, :], con("blk"), TMP[0], start=True, stop=True).then_inc(r_pe, 1)

        def act_rout(act):
            for j in range(DT):
                act.wait_ge(r_dve, 6 * j + 1)
                nc.scalar.activation(TMP[0], RT[:, j, :], ACT.Square).then_inc(r_act, 1)
                act.wait_ge(r_dve, 6 * j + 2)
                nc.scalar.activation(TMP[1], TMP[1], ACT.Sqrt).then_inc(r_act, 1)
                act.wait_ge(r_dve, 6 * j + 4)
                nc.scalar.activation(YR[:, j, :], RT[:, j, :], ACT.Identity, bias=prm("lnx_b", j)).then_inc(r_act, 1)

        def dve_rout(dve, steps):
            V = nc.vector
            for j in range(DT):
                y = RT[:, j, :]
                dve.wait_ge(r_pe, 3 * j + 1)
                V.scalar_tensor_tensor(y, psum[0][:, :], -1.0 / DH, y, ALU.mult, ALU.add).then_inc(r_dve, 1)
                dve.wait_ge(r_pe, 3 * j + 3)
                V.tensor_scalar(TMP[1], psum[1][:, :], 1.0 / DH, LNX_EPS, ALU.mult, ALU.add).then_inc(r_dve, 1)
                dve.wait_ge(r_act, 3 * j + 2)
                V.reciprocal(TMP[2], TMP[1]).then_inc(r_dve, 1)
                dve.wait_ge(r_dve, 6 * j + 3)
                V.scalar_tensor_tensor(y, y, prm("lnx_w", j), TMP[2], ALU.mult, ALU.mult).then_inc(r_dve, 1)
                dve.wait_ge(r_act, 3 * j + 3)
                V.tensor_tensor(YR[:, j, :], YR[:, j, :], BON[:, j, :], ALU.add).then_inc(r_dve, 1)
                dve.wait_ge(r_dve, 6 * j + 5)
                V.tensor_tensor(YR[:, j, :], psum[2][:, :], YR[:, j, :], ALU.mult).then_inc(r_dve, 1)

        block = ctx.enter_context(nc.Block())

        @block.sync
        def _(sp):
            sp.dma_start(PRM[:], cols[:, :]).then_inc(s_prm, 16)
            sp.dma_start(CON[:], const[:, :]).then_inc(s_prm, 16)
            for j in range(W_SLOTS):
                sp.dma_start(W[:, j, :], stream[j]).then_inc(w_full[j], 16)
            with sp.Fori(1, N_UNITS // W_SLOTS) as i:
                for j in range(W_SLOTS):
                    sp.wait_ge(unit_done, W_SLOTS * i + (j - W_SLOTS + 1))
                    sp.dma_start(W[:, j, :], stream[W_SLOTS * i + j]).then_inc(w_full[j], 16)
            sp.wait_ge(s_bar, 3 * len(STAGES))
            sp.dma_start(out.rearrange("(k p) t -> p k t", p=P), X[:]).then_inc(s_out, 16)
            sp.wait_ge(s_out, 16)

        @block.gpsimd
        def _(pool):
            pool.dma_start(X[:], x_t.rearrange("(k p) t -> p k t", p=P)).then_inc(s_x, 16)
            pool.dma_start(TAB[:], table2[:, :]).then_inc(s_small, 16)
            pool.dma_start(CW2[:], cmp_w2[:, :, :]).then_inc(s_small, 16)
            pool.dma_start(BIG[0:BUCKETS, 60, :], onehot[:, :]).then_inc(s_small, 16)
            line = BIG[0:H1, 61:63, :].rearrange("p a b -> p (a b)")
            pool.dma_start(line[:, 383:383 + 257], line1[:, :]).then_inc(s_line, 16)
            pool.wait_ge(s_line, 16)
            pool.tensor_copy(line[:, 0:383], line[:, 383:384].to_broadcast([H1, 383])).then_inc(s_pool, 1)
            pool.wait_ge(s_pool, 1)
            pool.dma_start(scratch[0, 0:H1, :], line[:, 0:LINE]).then_inc(s_line, 16)
            pool.wait_ge(s_line, 32)
            toeplitz = bass.AP(tensor=scratch.tensor, offset=P - 1, ap=[[LINE, H1], [-1, P], [1, S]])
            pool.dma_start(rows[0:H1], toeplitz).then_inc(s_rows, 16)
            pool.wait_ge(s_rows, 16)
            pool.dma_start(BIAS1[:, :, :], rows[0:H1].rearrange("h p m -> p h m")).then_inc(s_bias, 16)
            pool.wait_ge(s_bias, 16)
            pool.memset(BIAS1[0:CHUNK, :, S - CHUNK:S], NEG).then_inc(s_pool, 1)
            pool.wait_ge(s_line2, 16)
            toeplitz2 = bass.AP(tensor=scratch.tensor, offset=H2 * LINE + P - 1, ap=[[LINE, H2], [-1, P], [1, S]])
            pool.dma_start(rows[H1:H1 + H2], toeplitz2).then_inc(s_rows, 16)
            pool.wait_ge(s_rows, 32)
            pool.wait_ge(s_bar, 3 * (BASE["norm_r"].index))
            pool.dma_start(LR[:, 0, :], w2a2[:, :]).then_inc(s_lora, 16)
            pool.dma_start(LR[:, 1:3, :], g2[:, :, :]).then_inc(s_lora, 16)
            pool.wait_ge(s_bar, 3 * (BASE["norm_n"].index))
            pool.dma_start(BIAS2[:, :, :], rows[H1:H1 + H2].rearrange("h p m -> p h m")).then_inc(s_bias2, 16)
            pool.wait_ge(s_bar, 3 * (BASE["norm_c"].index))
            pool.dma_start(MEM[:, :, 0:N_MEM], mem_t.rearrange("(k p) t -> p k t", p=P)).then_inc(s_mem, 16)

        @block.tensor
        def _(pe):
            pe.wait_ge(s_act, 1)
            with pe.Fori(0, 12) as i:
                for j in range(4):
                    pe_unit(pe, "ada", 0, j, i, 4, [GM[:, k:k + 1] for k in range(DT)],
                            psum[0][:, bass.ds(4 * i + j, 1)], None).then_inc(unit_done, 1)
            pe.wait_ge(s_small, 48)
            nc.tensor.matmul(psum[1][0:H2, :], TAB[:, :], BIG[0:BUCKETS, 60, :], start=True, stop=True)
            stage_end(pe, "ada")
            pe_norm(pe, "norm_x", DT)
            stage_end(pe, "norm_x")
            pe_project(pe, "glu", h_tiles, 8)
            stage_end(pe, "glu")
            pe_project(pe, "qkv", h_tiles, 12)
            stage_end(pe, "qkv")
            pe_turn(pe, "turn_v", [[V1[:, j, t * P:(t + 1) * P] for j in range(4)] for t in range(4)])
            stage_end(pe, "turn_v")
            base = BASE["ln"]
            for k in range(4):
                last = nc.tensor.matmul(psum[6][:, :], con("ones"), CV[:, k, :], start=(k == 0), stop=(k == 3))
            last.then_inc(s_pe, 1)
            for k in range(4):
                pe.wait_ge(s_act, base.act + k + 1)
                last = nc.tensor.matmul(psum[7][:, :], con("ones"), SQ[:, k, :], start=(k == 0), stop=(k == 3))
            last.then_inc(s_pe, 1)
            stage_end(pe, "ln")
            pe.wait_ge(s_pool, 2)
            pe_attend(pe, "attend1", units1)
            stage_end(pe, "attend1")
            pe_turn(pe, "turn_o", [[O1[:, t, j * P:(j + 1) * P] for t in range(4)] for j in range(4)])
            stage_end(pe, "turn_o")
            pe_mix(pe, "mix1", 3, h_tiles, [OT1[:, k, :] for k in range(4)], [CV[:, k, :] for k in range(4)])
            stage_end(pe, "mix1")
            pe_project(pe, "mixo1", [Y1[:, k, :] for k in range(DT)], DT)
            stage_end(pe, "mixo1")
            pe_norm(pe, "post_mix", DT)
            stage_end(pe, "post_mix")
            pe_norm(pe, "norm_ffn1", DT)
            stage_end(pe, "norm_ffn1")
            pe_up(pe, "up1")
            stage_end(pe, "up1")
            pe_down(pe, "down1", HID)
            stage_end(pe, "down1")
            pe_norm(pe, "post_ffn1", DT)
            stage_end(pe, "post_ffn1")
            pe_norm(pe, "norm_r", DT)
            stage_end(pe, "norm_r")
            base = BASE["rlora"]
            for j in range(3):
                pe_unit(pe, "rlora", 0, j, 0, 0, h_tiles, psum[j][:, :], None).then_inc(unit_done, 1)
            slot = (U0["rlora"] + 3) % W_SLOTS
            pe.wait_ge(w_full[slot], 16 * ((U0["rlora"] + 3) // W_SLOTS + 1))
            for t in range(4):
                for k in range(DT):
                    last = nc.tensor.matmul(psum[4 + t][:, 0:48], H[:, k, t * P:(t + 1) * P],
                                            W[:, slot, k * P:k * P + 48], start=(k == 0), stop=(k == DT - 1))
            last.then_inc(unit_done, 1)
            stage_end(pe, "rlora")
            pe_rprep(pe)
            stage_end(pe, "rprep")
            pe_rchunks(pe)
            stage_end(pe, "rchunks")
            pe_rout(pe)
            stage_end(pe, "rout")
            pe_norm(pe, "norm_n", DT)
            stage_end(pe, "norm_n")
            pe_project(pe, "nsa", h_tiles, 20)
            stage_end(pe, "nsa")
            pe_heads(pe, "nheads", 12, con("blk"), 1)
            stage_end(pe, "nheads")
            stage_end(pe, "cmp_k")
            base = BASE["cmp"]
            for kind in range(2):
                blk = (BLK, BLK_V)[kind]
                pe.wait_ge(s_blk, 1 + 2 * kind)
                for q in range(4):
                    slot = (U0["cmp"] + 4 * kind + q) % W_SLOTS
                    pe.wait_ge(w_full[slot], 16 * ((U0["cmp"] + 4 * kind + q) // W_SLOTS + 1))
                    for kk in range(4):
                        for c in range(2):
                            last = nc.tensor.matmul(psum[2 * kind + c][:, 0:4 * N_CMP],
                                                    W[:, slot, kk * 256 + c * P:kk * 256 + (c + 1) * P],
                                                    blk[:, 4 * q + kk, :], start=(q == 0 and kk == 0),
                                                    stop=(q == 3 and kk == 3))
                    last.then_inc(unit_done, 1)
            pe.wait_ge(s_act, base.act + 2)
            for c in range(2):
                last = nc.tensor.matmul(psum[4][:, 0:4 * N_CMP], CW2[:, c, 0:P], HC[:, c, :], start=(c == 0), stop=(c == 1))
            last.then_inc(s_pe, 1)
            pe.wait_ge(s_act, base.act + 4)
            for g in range(N_KV):
                for c in range(2):
                    last = nc.tensor.matmul(psum[5][0:N_CMP, g * DH:(g + 1) * DH], HV[:, c, g * N_CMP:(g + 1) * N_CMP],
                                            CW2[:, c, P:P + DH], start=(c == 0), stop=(c == 1))
            last.then_inc(s_pe, 1)
            pe.wait_ge(s_act, base.act + 5)
            nc.tensor.matmul(psum[6][:, 0:4 * N_CMP], con("blk"), SQ[:, 0, 0:4 * N_CMP], start=True, stop=True)\
                .then_inc(s_pe, 4)
            stage_end(pe, "cmp")
            pe_turn(pe, "nturn", [[(VS, VS, VW, VW)[j][:, j % 2, t * P:(t + 1) * P] for j in range(4)] for t in range(4)])
            stage_end(pe, "nturn")
            pe.wait_ge(s_bias2, 16)
            pe_attend(pe, "attend2", units2)
            stage_end(pe, "attend2")
            pe_turn(pe, "turn_o2", [[O2[:, t, j * P:(j + 1) * P] for t in range(4)] for j in range(8)])
            stage_end(pe, "turn_o2")
            pe_mix(pe, "mix2", 4, h_tiles, [YR[:, k, :] for k in range(DT)], [OT2[:, k, :] for k in range(DT)])
            stage_end(pe, "mix2")
            pe_project(pe, "mixo2", [Y2[:, k, :] for k in range(DT)], DT)
            stage_end(pe, "mixo2")
            pe_norm(pe, "norm_c", DT)
            stage_end(pe, "norm_c")
            pe_project(pe, "caq", h_tiles, 8)
            stage_end(pe, "caq")
            pe_norm(pe, "norm_m", DT, N_MEM)
            stage_end(pe, "norm_m")
            pe_project(pe, "cakv", [MN[:, k, 0:N_MEM] for k in range(DT)], 16, N_MEM)
            stage_end(pe, "cakv")
            pe_heads(pe, "qheads", 8, con("ones"), 2)
            stage_end(pe, "qheads")
            pe_heads(pe, "kheads", 8, con("ones"), 2, N_MEM)
            stage_end(pe, "kheads")
            pe_turn(pe, "turn_v3", [[V3[:, 4 * (b % 2) + q, (b // 2) * P:(b // 2 + 1) * P] for q in range(4)] for b in range(4)])
            stage_end(pe, "turn_v3")
            pe_attend(pe, "attend3", units3)
            stage_end(pe, "attend3")
            pe_turn(pe, "turn_o3", [[O3[:, t, j * P:(j + 1) * P] for t in range(4)] for j in range(8)])
            stage_end(pe, "turn_o3")
            pe_project(pe, "cao", [OT3[:, k, :] for k in range(DT)], 8)
            stage_end(pe, "cao")
            pe_norm(pe, "norm_f", DT)
            stage_end(pe, "norm_f")
            pe_up(pe, "up2")
            stage_end(pe, "up2")
            pe_down(pe, "down2", HID)
            stage_end(pe, "down2")

        @block.scalar
        def _(act):
            act.wait_ge(s_prm, 32)
            nc.scalar.activation(GM[:, 0:DT], prm("c", 0, DT), ACT.Silu).then_inc(s_act, 1)
            stage_end(act, "ada")
            act.wait_ge(s_x, 16)
            act_norm(act, "norm_x", X, DT)
            line2 = BIG[0:H2, 63:65, :].rearrange("p a b -> p (a b)")
            act.wait_ge(s_tap0, 2)
            act.dma_start(scratch[1, 0:H2, :], line2[:, 0:LINE]).then_inc(s_line2, 16)
            stage_end(act, "norm_x")
            base = BASE["glu"]
            with act.Fori(0, 2) as i:
                for j in range(2):
                    act.wait_ge(unit_done, 4 * i + (U0["glu"] + 2 * j + 2))
                    act.wait_ge(s_ev, 4 * i + (base.ev + 2 * j))
                    nc.scalar.activation(SQ[:, 2 + j, :], psum[2 * j + 1][:, :], ACT.Sigmoid,
                                         bias=PRM[:, bass.ds(C0["b_in"] + 16 + j + 2 * i, 1)]).then_inc(s_glu, 1)
            stage_end(act, "glu")
            act_project(act, "qkv", BIG, 12, bias=("b_in", 0))
            stage_end(act, "qkv")
            act_turn(act, "turn_v", [VT1[:, t, :] for t in range(4)])
            stage_end(act, "turn_v")
            base = BASE["ln"]
            for k in range(4):
                act.wait_ge(s_dve, base.dve + 2 + k)
                nc.scalar.activation(SQ[:, k, :], CV[:, k, :], ACT.Square).then_inc(s_act, 1)
            act.wait_ge(s_dve, base.dve + 6)
            nc.scalar.activation(ST[:, 1, :], ST[:, 0, :], ACT.Sqrt).then_inc(s_act, 1)
            for k in range(4):
                act.wait_ge(s_dve, base.dve + 8 + k)
                nc.scalar.activation(CV[:, k, :], CV[:, k, :], ACT.Silu, bias=prm("b_conv_ln", k))
            stage_end(act, "ln")
            act_attend(act, "attend1", units1)
            stage_end(act, "attend1")
            act_turn(act, "turn_o", [OT1[:, j, :] for j in range(4)])
            stage_end(act, "turn_o")
            act_mix(act, "mix1", 3, 20, 28)
            stage_end(act, "mix1")
            act_project(act, "mixo1", Z1, DT)
            stage_end(act, "mixo1")
            act_norm(act, "post_mix", Z1, DT)
            stage_end(act, "post_mix")
            act_norm(act, "norm_ffn1", X, DT)
            stage_end(act, "norm_ffn1")
            act_up(act, "up1", True)
            stage_end(act, "up1")
            act_down(act, "down1", Z1)
            stage_end(act, "down1")
            act_norm(act, "post_ffn1", Z1, DT)
            stage_end(act, "post_ffn1")
            act_norm(act, "norm_r", X, DT)
            stage_end(act, "norm_r")
            base = BASE["rlora"]
            for j in range(3):
                act.wait_ge(unit_done, U0["rlora"] + j + 1)
                nc.scalar.activation(ZL[:, j, :], psum[j][:, :], ACT.Copy, scale=OMU[:, j:j + 1]).then_inc(s_act, 1)
            act.wait_ge(unit_done, U0["rlora"] + 4)
            for t in range(4):
                nc.scalar.activation(GT[:, t, :], psum[4 + t][:, 0:48], ACT.Sigmoid)
            for j in range(3):
                act.wait_ge(s_ev, base.ev + j + 1)
                part = ZL[0:64, 0, :] if j == 0 else ZL[:, j, :]
                nc.scalar.activation(part, part, ACT.Tanh if j == 0 else ACT.Sigmoid)
            stage_end(act, "rlora")
            act_rprep(act)
            stage_end(act, "rprep")
            act_rchunks(act)
            stage_end(act, "rchunks")
            act_rout(act)
            stage_end(act, "rout")
            act_norm(act, "norm_n", X, DT)
            stage_end(act, "norm_n")
            act_project(act, "nsa", NSA, 20)
            stage_end(act, "nsa")
            act_heads(act, "nheads", tiles(16, 8) + tiles(28, 2) + tiles(32, 2), 12, 1)
            stage_end(act, "nheads")
            for g in range(N_KV):
                lo = DH * (g % 2)
                nc.scalar.activation(SH[DH:P, g, 0:S - 1], KC[lo:lo + DH, g // 2, 1:S], ACT.Copy)
            stage_end(act, "cmp_k")
            base = BASE["cmp"]
            for kind, dst in enumerate((HC, HV)):
                act.wait_ge(unit_done, U0["cmp"] + 4 * (kind + 1))
                for c in range(2):
                    nc.scalar.activation(dst[:, c, :], psum[2 * kind + c][:, 0:4 * N_CMP], ACT.Gelu_apprx_tanh)\
                        .then_inc(s_act, 1)
            act.wait_ge(s_pe, base.pe + 1)
            nc.scalar.activation(SQ[:, 0, 0:4 * N_CMP], psum[4][:, 0:4 * N_CMP], ACT.Square).then_inc(s_act, 1)
            act.wait_ge(s_pe, base.pe + 2)
            nc.scalar.activation(VCT[0:N_CMP, :], psum[5][0:N_CMP, 0:4 * DH], ACT.Copy)
            act.wait_ge(e_done, DT + 1)
            nc.scalar.activation(ST[:, 1, 0:4 * N_CMP], ST[:, 0, 0:4 * N_CMP], ACT.Sqrt).then_inc(s_act, 1)
            stage_end(act, "cmp")
            act_turn(act, "nturn", [VT2[:, t, :] for t in range(4)])
            stage_end(act, "nturn")
            act_attend(act, "attend2", units2)
            stage_end(act, "attend2")
            act_turn(act, "turn_o2", [OT2[:, j, :] for j in range(8)])
            stage_end(act, "turn_o2")
            act_mix(act, "mix2", 4, None, None)
            stage_end(act, "mix2")
            stage_end(act, "mixo2")
            act_norm(act, "norm_c", X, DT)
            stage_end(act, "norm_c")
            act_project(act, "caq", Q3, 8)
            stage_end(act, "caq")
            act.wait_ge(s_mem, 16)
            act_norm(act, "norm_m", MEM, DT, N_MEM)
            stage_end(act, "norm_m")
            act_project(act, "cakv", BIG[:, 8:24, :], 16, width=N_MEM)
            stage_end(act, "cakv")
            act_heads(act, "qheads", tiles(0, 8), 8, 2)
            stage_end(act, "qheads")
            act_heads(act, "kheads", [K3[:, k, :] for k in range(8)], 8, 2, N_MEM)
            stage_end(act, "kheads")
            act_turn(act, "turn_v3", [VT3[:, b // 2, (b % 2) * S:(b % 2 + 1) * S] for b in range(4)])
            stage_end(act, "turn_v3")
            act_attend(act, "attend3", units3)
            stage_end(act, "attend3")
            act_turn(act, "turn_o3", [OT3[:, j, :] for j in range(8)])
            stage_end(act, "turn_o3")
            stage_end(act, "cao")
            act_norm(act, "norm_f", X, DT)
            stage_end(act, "norm_f")
            act_up(act, "up2", False)
            stage_end(act, "up2")
            stage_end(act, "down2")

        @block.vector
        def _(dve):
            V = nc.vector
            steps = Steps(s_chain)
            dve.wait_ge(s_prm, 32)
            V.tensor_scalar(OMU[:, :], prm("mu", 0, 28), -1.0, 1.0, ALU.mult, ALU.add)
            V.memset(GLU[:, :, 0:LEAD], 0.0)
            dve.wait_ge(unit_done, 48)
            V.tensor_tensor(MOD[:, :], psum[0][:, 0:48], prm("b_ada", 0, 48), ALU.add).then_inc(s_dve, 1)
            dve.wait_ge(s_dve, 1)
            V.scalar_tensor_tensor(GM[:, 8:16], MOD[:, 8:16], 1.0, prm("g_pre_mix", 0, 8), ALU.add, ALU.mult)
            V.tensor_tensor(GM[:, 16:24], MOD[:, 16:24], prm("g_post_mix", 0, 8), ALU.mult)
            V.scalar_tensor_tensor(GM[:, 24:32], MOD[:, 32:40], 1.0, prm("g_pre_ffn", 0, 8), ALU.add, ALU.mult)
            V.tensor_tensor(GM[:, 32:40], MOD[:, 40:48], prm("g_post_ffn", 0, 8), ALU.mult).then_inc(s_ev, 4)
            stage_end(dve, "ada")
            line2 = BIG[0:H2, 63:65, :].rearrange("p a b -> p (a b)")
            V.tensor_copy(line2[:, 0:S], psum[1][0:H2, :]).then_inc(s_tap0, 1)
            V.memset(line2[:, S:LINE], NEG).then_inc(s_tap0, 1)
            dve_norm(dve, "norm_x", X, H, GM[:, 8:16], DT, MOD[:, 0:8])
            stage_end(dve, "norm_x")
            base = BASE["glu"]
            with dve.Fori(0, 2) as i:
                for j in range(2):
                    dve.wait_ge(s_glu, 2 * i + (base.glu + j + 1))
                    V.scalar_tensor_tensor(GLU[:, 2 * i + j, LEAD:GPAD], psum[2 * j][:, :],
                                           PRM[:, bass.ds(C0["b_in"] + 12 + j + 2 * i, 1)], SQ[:, 2 + j, :],
                                           ALU.add, ALU.mult).then_inc(s_ev, 2)
            stage_end(dve, "glu")
            for j in range(4):
                V.tensor_scalar(CV[:, j, :], GLU[:, j, LEAD - CONV_K + 1:LEAD - CONV_K + 1 + S],
                                prm("w_dw_conv", j * CONV_K), prm("b_dw_conv", j), ALU.mult, ALU.add).then_inc(s_cv, 1)
            with dve.Fori(1, CONV_K) as t:
                for j in range(4):
                    dve.wait_ge(s_cv, 4 * t + (j - 3))
                    V.scalar_tensor_tensor(CV[:, j, :], GLU[:, j, bass.ds(LEAD - CONV_K + 1 + t, S)],
                                           PRM[:, bass.ds(C0["w_dw_conv"] + j * CONV_K + t, 1)], CV[:, j, :],
                                           ALU.mult, ALU.add).then_inc(s_cv, 1)
            stage_end(dve, "qkv")
            stage_end(dve, "turn_v")
            base = BASE["ln"]
            dve.wait_ge(s_pe, base.pe + 1)
            V.tensor_scalar(ST[:, 0, :], psum[6][:, :], 1.0 / 512, None, ALU.mult).then_inc(s_dve, 1)
            dve.wait_ge(s_dve, base.dve + 1)
            for k in range(4):
                V.tensor_tensor(CV[:, k, :], CV[:, k, :], ST[:, 0, :], ALU.subtract).then_inc(s_dve, 1)
            dve.wait_ge(s_pe, base.pe + 2)
            V.tensor_scalar(ST[:, 0, :], psum[7][:, :], 1.0 / 512, EPS, ALU.mult, ALU.add).then_inc(s_dve, 1)
            dve.wait_ge(s_act, base.act + 5)
            V.reciprocal(ST[:, 0, :], ST[:, 1, :]).then_inc(s_dve, 1)
            dve.wait_ge(s_dve, base.dve + 7)
            for k in range(4):
                V.scalar_tensor_tensor(CV[:, k, :], CV[:, k, :], prm("g_conv_ln", k), ST[:, 0, :], ALU.mult,
                                       ALU.mult).then_inc(s_dve, 1)
            stage_end(dve, "ln")
            dve_attend(dve, "attend1", units1, steps)
            stage_end(dve, "attend1")
            stage_end(dve, "turn_o")
            dve_mix(dve, "mix1", 3, Y1, "b_conv_o")
            stage_end(dve, "mix1")
            stage_end(dve, "mixo1")
            dve_residual(dve, "post_mix", Z1, GM[:, 16:24], DT)
            stage_end(dve, "post_mix")
            dve_norm(dve, "norm_ffn1", X, H, GM[:, 24:32], DT, MOD[:, 24:32])
            stage_end(dve, "norm_ffn1")
            dve_up(dve, "up1", True, HID)
            stage_end(dve, "up1")
            dve_down(dve, "down1", Z1)
            stage_end(dve, "down1")
            dve_residual(dve, "post_ffn1", Z1, GM[:, 32:40], DT)
            stage_end(dve, "post_ffn1")
            dve_norm(dve, "norm_r", X, H, prm("norm_mix", 0, 8), DT)
            stage_end(dve, "norm_r")
            base = BASE["rlora"]
            for j in range(3):
                dve.wait_ge(s_act, base.act + j + 1)
                V.scalar_tensor_tensor(ZL[:, j, 1:S], psum[j][:, 0:S - 1], prm("mu", j), ZL[:, j, 1:S], ALU.mult,
                                       ALU.add).then_inc(s_ev, 1)
            stage_end(dve, "rlora")
            dve_rprep(dve, steps)
            stage_end(dve, "rprep")
            dve_rchunks(dve)
            stage_end(dve, "rchunks")
            dve_rout(dve, steps)
            stage_end(dve, "rout")
            dve_norm(dve, "norm_n", X, H, prm("norm_mix", 0, 8), DT)
            stage_end(dve, "norm_n")
            stage_end(dve, "nsa")
            dve_heads(dve, "nheads", tiles(16, 8) + tiles(28, 2) + tiles(32, 2), 12, 1,
                      [prm("q_gain")] * 8 + [prm("k_gain", 1)] * 2 + [prm("k_gain", 2)] * 2, S, DH)
            stage_end(dve, "nheads")
            for g in range(N_KV):
                lo = DH * (g % 2)
                V.tensor_copy(SH[0:DH, g, :], KC[lo:lo + DH, g // 2, :])
            stage_end(dve, "cmp_k")
            base = BASE["cmp"]

            def blocks(dst, pe_name):
                for k in range(16):
                    last = V.tensor_scalar(dst[:, k, :].rearrange("p (g n) -> p g n", g=N_KV),
                                           SH[:, :, 2 * k:2 * k + CMP_STRIDE * (N_CMP - 1) + 1:CMP_STRIDE],
                                           prm(pe_name, k), None, ALU.add)
                return last

            blocks(BLK, "pe_k").then_inc(s_blk, 1)
            dve.wait_ge(s_blk, 1)
            for half in range(2):
                for g in range(N_KV):
                    lo = DH * (g % 2)
                    last = V.tensor_copy(SH[DH * half:DH * (half + 1), g, 0:S - half], VC[lo:lo + DH, g // 2, half:S])
            last.then_inc(s_blk, 1)
            dve.wait_ge(s_blk, 2)
            blocks(BLK_V, "pe_v").then_inc(s_blk, 1)
            dve.wait_ge(s_pe, base.pe + 6)
            V.tensor_scalar(ST[:, 0, 0:4 * N_CMP], psum[6][:, 0:4 * N_CMP], 1.0 / DH, EPS, ALU.mult, ALU.add)\
                .then_inc(e_done, 1)
            dve.wait_ge(s_act, base.act + 6)
            steps.link(dve, V.reciprocal(ST[:, 0, 0:4 * N_CMP], ST[:, 1, 0:4 * N_CMP]))
            V.scalar_tensor_tensor(KCN, psum[4][:, 0:4 * N_CMP], prm("k_gain", 0), ST[:, 0, 0:4 * N_CMP], ALU.mult,
                                   ALU.mult)
            stage_end(dve, "cmp")
            stage_end(dve, "nturn")
            dve_attend(dve, "attend2", units2, steps)
            stage_end(dve, "attend2")
            stage_end(dve, "turn_o2")
            dve_mix(dve, "mix2", 4, Y2, None)
            stage_end(dve, "mix2")
            dve_add_project(dve, "mixo2", 8)
            stage_end(dve, "mixo2")
            dve_norm(dve, "norm_c", X, H, prm("norm_cross", 0, 8), DT)
            stage_end(dve, "norm_c")
            stage_end(dve, "caq")
            dve_norm(dve, "norm_m", MEM, MN, prm("norm_mem", 0, 8), DT, width=N_MEM)
            stage_end(dve, "norm_m")
            stage_end(dve, "cakv")
            dve_heads(dve, "qheads", tiles(0, 8), 8, 2, [prm("ca_q_gain", k % 2) for k in range(8)], S, 256)
            stage_end(dve, "qheads")
            dve_heads(dve, "kheads", [K3[:, k, :] for k in range(8)], 8, 2, [prm("ca_k_gain", k % 2) for k in range(8)],
                      N_MEM, 256)
            stage_end(dve, "kheads")
            stage_end(dve, "turn_v3")
            dve_attend(dve, "attend3", units3, steps)
            stage_end(dve, "attend3")
            stage_end(dve, "turn_o3")
            dve_add_project(dve, "cao", 8)
            stage_end(dve, "cao")
            dve_norm(dve, "norm_f", X, H, prm("norm_ffn", 0, 8), DT)
            stage_end(dve, "norm_f")
            dve_up(dve, "up2", False, HID)
            stage_end(dve, "up2")
            dve.wait_ge(unit_done, N_UNITS)
            for n in range(DT):
                V.tensor_tensor(X[:, n, :], X[:, n, :], psum[n][:, :], ALU.add)
            stage_end(dve, "down2")



def t5_buckets():
    n = np.arange(S)
    exact = BUCKETS // 2
    nf = np.maximum(n, 1).astype(np.float32)
    large = exact + (np.log(nf / np.float32(exact)) / np.float32(np.log(128 / exact)) * np.float32(BUCKETS - exact)).astype(np.int32)
    return np.where(n < exact, n, np.minimum(large, BUCKETS - 1))


def constants():
    c = np.zeros((P, N_CONST), np.float32)

    def put(name, a):
        c[:a.shape[0], K0[name]:K0[name] + a.shape[1]] = a

    i, j = np.arange(CHUNK)[:, None], np.arange(CHUNK)[None, :]
    same = i // 16 == j // 16
    put("ident", np.eye(P))
    put("ones", np.ones((P, P)))
    put("blk", np.kron(np.eye(2), np.ones((64, 64))))
    for name, m in (("strict_up", i < j), ("incl_up", i <= j), ("up16", (i < j) & same), ("lo16", (i > j) & same),
                    ("lo_off", (i > j) & ~same), ("eye64", i == j)):
        put(name, np.tile(m, (2, 1)))
    put("scan", np.tile(np.arange(S) % CHUNK != 0, (P, 1)))
    onehot = np.zeros((BUCKETS, S))
    onehot[t5_buckets()[S - 1 - np.arange(S)], np.arange(S)] = 1
    return c, onehot.astype(np.float32)


def panels(w):
    k, n = w.shape
    return w.reshape(k // P, P, n // P, P).transpose(2, 1, 0, 3).reshape(n // P, P, k)


def pad_columns(w, n):
    return np.concatenate([w, np.zeros((w.shape[0], n - w.shape[1]), w.dtype)], 1)


def interleave(*units):
    return np.stack(units, 1).reshape(-1, P, D)


def kernel(**inputs):
    import concourse.bacc as bacc
    from concourse.bass_utils import run_bass_kernel_spmd

    a = {k: np.asarray(v) for k, v in inputs.items()}
    one = {k: (v[0] if k not in ("rel_bias_2",) else v) for k, v in a.items()}

    w_in = one["w_in"]
    up, up2 = panels(one["w_up"]), panels(one["ffn_up_2"])
    q, k, v, ga, gb = (w_in[:, 512 * n:512 * (n + 1)] for n in range(5))
    gate_a, gate_b = panels(w_in[:, 2560:3584]), panels(w_in[:, 3584:4608])
    both = np.concatenate([panels(one["w_attn_o"]), panels(one["w_conv_o"])], 2)
    z = one["w_in_2"]
    rk, kk_, rv = panels(z[:, 0:1024]), panels(z[:, 1024:2048]), panels(z[:, 2048:3072])
    zq = z[:, 3360:4384].reshape(D, 2, 2, HG, DH).transpose(0, 1, 3, 2, 4).reshape(D, D)
    z_gate = pad_columns(z[:, 5920:5968], P)
    zm = z[:, 5968:8016]
    down, down2 = (one[n].reshape(FT, P, D) for n in ("w_down", "ffn_down_2"))
    cmp_units = [one[n].reshape(4, 4, P, CMP_HIDDEN).transpose(0, 2, 1, 3).reshape(4, P, D)
                 for n in ("cmp_w1_k_2", "cmp_w1_v_2")]
    stream = np.concatenate([
        panels(one["w_ada"]), interleave(panels(ga), panels(gb)), panels(q), panels(k), panels(v),
        interleave(gate_a, both, gate_b), panels(one["w_mix_o"]), interleave(up[:FT], up[FT:]), down,
        panels(z[:, 3072:3328]), panels(pad_columns(z[:, 3328:3360], P)), panels(z_gate), interleave(kk_, rk, rv),
        panels(zq), panels(z[:, 4384:5920]), *cmp_units,
        interleave(panels(zm[:, :D]), panels(one["w_branch_rwkv_2"]), panels(zm[:, D:]), panels(one["w_branch_nsa_2"])),
        panels(one["w_mix_out_2"]), panels(one["ca_wq_2"]), panels(one["ca_wkv_2"]), panels(one["ca_wo_2"]),
        interleave(up2[:FT], up2[FT:]), down2], 0)
    assert stream.shape == (N_UNITS, P, D)

    def col(x):
        return x.reshape(-1, P).T

    def taps(x):
        return x.reshape(x.shape[0], -1, P).transpose(2, 1, 0).reshape(P, -1)

    mu = one["rwkv_mu_2"]
    mu_lora = np.concatenate([mu[3072:3328], np.pad(mu[3328:3360], (0, P - 32)), np.zeros(P, mu.dtype)])
    mu_rkv = np.stack([mu[1024:2048].reshape(8, P), mu[0:1024].reshape(8, P), mu[2048:3072].reshape(8, P)], 1)
    twice = lambda x: np.concatenate([x, x], -1)
    parts = {
        "c": col(one["c"]), "b_ada": col(one["b_ada"]), "b_in": col(one["b_in"]), "w_dw_conv": taps(one["w_dw_conv"]),
        "w_dw_ffn": taps(one["w_dw_ffn"]), "b_dw_ffn": col(one["b_dw_ffn"]), "mu": col(np.concatenate([mu_lora, mu_rkv.reshape(-1)])),
        "norm_mix": col(one["norm_mix_2"]), "w0": col(one["rwkv_w0_2"]), "a0": col(one["rwkv_a0_2"]),
        "kk": col(one["rwkv_kk_2"]), "ka": col(one["rwkv_ka_2"]), "rk": col(one["rwkv_rk_2"].reshape(-1)),
        "lnx_w": col(one["rwkv_lnx_w_2"]), "lnx_b": col(one["rwkv_lnx_b_2"]),
        "q_gain": twice(one["nsa_q_gain_2"])[:, None], "k_gain": twice(one["nsa_k_gain_2"]).T,
        "pe_k": col(one["cmp_pe_k_2"].reshape(-1)), "pe_v": col(one["cmp_pe_v_2"].reshape(-1)),
        "norm_cross": col(one["norm_cross_2"]), "norm_mem": col(one["norm_mem_2"]),
        "ca_q_gain": col(one["ca_q_gain_2"]), "ca_k_gain": col(one["ca_k_gain_2"]), "norm_ffn": col(one["norm_ffn_2"]),
        "ffn_conv": taps(one["ffn_conv_2"]), "ffn_conv_b": col(one["ffn_conv_b_2"]),
    }
    cols = np.concatenate([parts[n] if n in parts else col(one[n]) for n, _ in COLUMNS], 1)
    assert cols.shape == (P, N_COLS)

    const, onehot = constants()
    w2a2 = np.concatenate([one["rwkv_w2_2"], one["rwkv_a2_2"]], 0)
    g2 = np.pad(one["rwkv_g2_2"], ((0, 96), (0, 0))).reshape(2, P, D).transpose(1, 0, 2)
    w2k, w2v = (one[n].reshape(2, P, DH).transpose(1, 0, 2) for n in ("cmp_w2_k_2", "cmp_w2_v_2"))
    arrays = {
        "stream": stream, "cols": cols, "const": const, "onehot": onehot, "x_t": one["x"].T, "mem_t": one["mem_2"].T,
        "line1": one["rel_bias"][:, ::-1], "table2": one["rel_bias_2"], "w2a2": w2a2, "g2": g2,
        "cmp_w2": np.concatenate([w2k, w2k, w2v], 2),
    }
    arrays = {n: np.ascontiguousarray(x) for n, x in arrays.items()}
    nc = bacc.Bacc("TRN2", target_bir_lowering=False, num_devices=1)
    args = [nc.dram_tensor(n, x.shape, mybir.dt.from_np(x.dtype), kind="ExternalInput").ap() for n, x in arrays.items()]
    args.append(nc.dram_tensor("out_t", (D, S), F32, kind="ExternalOutput").ap())
    args.append(nc.dram_tensor("bias_lines", (2, H2, LINE), F32, kind="Internal").ap())
    args.append(nc.dram_tensor("bias_rows", (H1 + H2, P, S), F32, kind="Internal").ap())
    build_program(nc, *args)
    r = run_bass_kernel_spmd(nc, [arrays], core_ids=[0])
    return np.ascontiguousarray(r.results[0]["out_t"].T)[None]
```

```python
from collections import namedtuple
from contextlib import ExitStack

import numpy as np

import concourse.bass as bass
from concourse import mybir

ALU = mybir.AluOpType
ACT = mybir.ActivationFunctionType
F32 = mybir.dt.float32
F32R = mybir.dt.float32r
AX_X = mybir.AxisListType.X

P = 128
S = 512
D = 1024
DT = D // P
DH = 64
D_FF = 2816
FT = D_FF // P
NEG = -1e30
EPS = 1e-6

CHUNK = 64
H1 = 8
CONV_K = 31
MAX_REL = 128

R_HEADS = 16
LNX_EPS = 64e-5
H2, N_KV = 16, 4
HG = H2 // N_KV
BUCKETS = 32
CMP_BLOCK, CMP_STRIDE = 32, 16
N_CMP = (S - CMP_BLOCK) // CMP_STRIDE + 1
CMP_HIDDEN = 256
CA_HEADS = 4
N_MEM = 256
LINE = 640

W_SLOTS = 4
S_SLOTS = 2

STREAM = [
    ("ada", 48), ("glu", 8), ("qkv", 12), ("mix1", 24), ("mixo1", 8), ("up1", 44), ("down1", 22),
    ("rlora", 4), ("rkv", 24), ("nsa", 20), ("cmp", 8),
    ("mix2", 32), ("mixo2", 8), ("caq", 8), ("cakv", 16), ("cao", 8), ("up2", 44), ("down2", 22),
]
U0 = {}
N_UNITS = 0
for _name, _n in STREAM:
    U0[_name] = N_UNITS
    N_UNITS += _n
assert N_UNITS % W_SLOTS == 0

SPLIT = ("up1", "down1", "up2", "down2")
SPLIT0 = {}
N_SPLIT = 0
for _name, _n in STREAM:
    if _name in SPLIT:
        assert U0[_name] % S_SLOTS == 0
        SPLIT0[_name] = N_SPLIT
        N_SPLIT += _n

COLUMNS = [
    ("b_ada", 48), ("g_pre_mix", 8), ("g_post_mix", 8), ("b_in", 36), ("w_dw_conv", 4 * CONV_K),
    ("b_dw_conv", 4), ("g_conv_ln", 4), ("b_conv_ln", 4), ("b_conv_o", 8), ("g_pre_ffn", 8),
    ("g_post_ffn", 8), ("w_dw_ffn", 2 * FT * 3), ("b_dw_ffn", 2 * FT),
    ("norm_mix", 8), ("mu", 28), ("w0", 8), ("a0", 8), ("kk", 8), ("ka", 8), ("rk", 8),
    ("lnx_w", 8), ("lnx_b", 8), ("q_gain", 1), ("k_gain", 3), ("pe_k", 16), ("pe_v", 16),
    ("norm_cross", 8), ("norm_mem", 8), ("ca_q_gain", 2), ("ca_k_gain", 2), ("norm_ffn", 8),
    ("ffn_conv", FT * 3), ("ffn_conv_b", FT),
]
C0 = {}
N_COLS = 0
for _name, _n in COLUMNS:
    C0[_name] = N_COLS
    N_COLS += _n

CONSTS = [("ident", 128), ("ones", 128), ("blk", 128), ("strict_up", 64), ("incl_up", 64), ("up16", 64),
          ("lo16", 64), ("lo_off", 64), ("eye64", 64), ("scan", 512)]
K0 = {}
N_CONST = 0
for _name, _n in CONSTS:
    K0[_name] = N_CONST
    N_CONST += _n





def norm_steps(n):
    return dict(pe=n, act=n + 1, dve=n + 2)


def heads_steps(batches, n):
    return dict(pe=n, act=n + batches, dve=2 * n + batches)


def turn_steps(n):
    return dict(pe=n, act=n)


FFN1 = dict(ev=2 * FT, conv=FT, tap=2 * FT, gelu=FT, dve=2 * FT, prod=FT)
FFN2 = dict(ev=2 * FT, conv=FT, tap=FT, gelu=FT, dve=FT, prod=FT)
NORM_SPLIT = dict(pe=DT, act=2 * DT + 1, dve=2 * DT + 2)
MIX = dict(ev=DT, glu=2 * DT, dve=2 * DT)
STAGES = [
    ("ada", dict(act=1, dve=1, ev=4)), ("norm_x", norm_steps(DT)), ("glu", dict(ev=8, glu=4)),
    ("qkv", dict(ev=12)), ("turn_v", turn_steps(4)), ("ln", dict(pe=2, act=5, dve=11)),
    ("attend1", dict(att=H1 * 4)), ("turn_o", turn_steps(4)), ("mix1", MIX), ("mixo1", dict(ev=8)),
    ("post_mix", norm_steps(DT)), ("norm_ffn1", NORM_SPLIT), ("up1", FFN1), ("down1", dict()),
    ("post_ffn1", norm_steps(DT)),
    ("norm_r", norm_steps(DT)), ("rlora", dict(ev=3, act=3)), ("rprep", dict()), ("rchunks", dict()),
    ("rout", dict()), ("norm_n", norm_steps(DT)), ("nsa", dict(ev=20)), ("nheads", heads_steps(3, 12)),
    ("cmp_k", dict()), ("cmp", dict(pe=6, act=6)), ("nturn", turn_steps(4)), ("attend2", dict(att=H2 * 4 * 3)),
    ("turn_o2", turn_steps(8)), ("mix2", MIX), ("mixo2", dict(ev=8)), ("norm_c", norm_steps(DT)),
    ("caq", dict(ev=8)), ("norm_m", norm_steps(DT)), ("cakv", dict(ev=16)), ("qheads", heads_steps(2, 8)),
    ("kheads", heads_steps(2, 8)), ("turn_v3", turn_steps(4)), ("attend3", dict(att=CA_HEADS * 4)),
    ("turn_o3", turn_steps(8)), ("cao", dict(ev=8)), ("norm_f", NORM_SPLIT), ("up2", FFN2),
    ("down2", dict()),
]
RUN_ON = ("ada",)
COUNTERS = ("act", "dve", "pe", "ev", "att", "glu", "tap", "conv", "gelu", "prod")


Base = namedtuple("Base", ("index",) + COUNTERS)

BASE = {}
_values = {name: 0 for name in COUNTERS}
N_ENDS = 0
for _name, _steps in STAGES:
    BASE[_name] = Base(N_ENDS, **_values)
    N_ENDS += _name not in RUN_ON
    for _k, _v in _steps.items():
        _values[_k] += _v


def build_program(nc, stream, cols, const, onehot, c_rows, x_t, mem_t, line1, table2, w2a2, g2, cmp_w2, out, scratch, rows):
    with ExitStack() as ctx:
        def sb(name, shape):
            return ctx.enter_context(nc.sbuf_tensor(name, shape, F32))

        def sem(name):
            return ctx.enter_context(nc.semaphore(name))

        X = sb("X", [P, DT, S])
        H = sb("H", [P, DT, S])
        W = sb("W", [P, W_SLOTS, D])
        PRM = sb("PRM", [P, N_COLS])
        ZERO = sb("ZERO", [P, 8])
        CON = sb("CON", [P, N_CONST])
        SQ = sb("SQ", [P, 4, S])
        ST = sb("ST", [P, 2, S])
        MOD = sb("MOD", [P, 48])
        GM = sb("GM", [P, 5 * DT])
        OMU = sb("OMU", [P, 28])
        DEC = sb("DEC", [P, DT, S // CHUNK])
        GT = sb("GT", [P, S // P, 3 * H2])
        CW2 = sb("CW2", [P, 2, P + DH])
        TAB = sb("TAB", [BUCKETS, H2])
        SM = sb("SM", [P, 64])
        big_at = nc.sbuf_base
        BIG = sb("BIG", [P, 68, S])
        BIGR = nc.alloc_sbuf_tensor_at("BIGR", [P, 68, S], F32R, offset=big_at)
        psum = [ctx.enter_context(nc.psum_tensor(f"bank{b}", [P, S], F32)) for b in range(8)]

        def prm(name, j=0, n=1):
            return PRM[:, C0[name] + j:C0[name] + j + n]

        def con(name, n=None, lo=0, hi=P):
            width = dict(CONSTS)[name]
            return CON[lo:hi, K0[name]:K0[name] + (n or width)]

        s_prm = sem("params_loaded")
        s_x = sem("x_loaded")
        w_full = [sem(f"w_full{j}") for j in range(W_SLOTS)]
        unit_done = sem("unit_done")
        s_ev = sem("banks_read")
        s_act = sem("act_step")
        s_dve = sem("dve_step")
        s_pe = sem("pe_step")
        s_bar = sem("stage_end")
        s_sc = sem("scores_ready")
        s_sfree = sem("scores_read")
        s_mx = sem("max_ready")
        s_exp = sem("probs_ready")
        s_tr = sem("probs_turned")
        s_pt = sem("turned_copied")
        s_pv = sem("outputs_ready")
        s_of = sem("outputs_read")
        s_line = sem("bias_line")
        s_bias = sem("bias_loaded")
        s_out = sem("out_stored")
        s_glu = sem("gate_ready")
        s_tap = sem("first_tap_ready")
        s_conv = sem("conv_ready")
        s_gelu = sem("gelu_ready")
        s_prod = sem("hidden_product_ready")
        s_hi = sem("hidden_hi_ready")
        s_split = sem("weights_split")
        s_mem = sem("mem_loaded")
        s_c = sem("c_loaded")
        s_hot = sem("bias2_products")
        s_chain = sem("vector_chain")
        s_cv = sem("taps_done")
        s_blk = sem("blocks_ready")
        s_tap0 = sem("line_ready")
        s_pool = sem("pool_step")
        s_rows = sem("bias_rows_stored")
        s_small = sem("small_weights_loaded")
        s_lora = sem("lora_loaded")
        s_bias2 = sem("bias2_loaded")
        s_line2 = sem("bias2_line")
        e_keep = sem("unshifted_part_ready")
        e_shift = sem("shifted")
        e_log = sem("lora_products_ready")
        e_sig = sem("sigmoids_ready")
        e_scan = sem("log_decays_summed")
        e_dec = sem("decays_ready")
        e_kk = sem("kk_ready")
        e_sq = sem("kk_squared")
        e_ss = sem("kk_summed")
        e_root = sem("kk_norm_ready")
        e_rp = sem("bonus_terms_ready")
        e_bs = sem("bonus_summed")
        e_done = sem("tile_prepared")
        c_pe = sem("chunk_products")
        c_act = sem("chunk_copies")
        c_dve = sem("chunk_vector_steps")
        q_pe = sem("state_products")
        q_act = sem("state_copies")
        q_dve = sem("state_vector_steps")
        r_pe = sem("rout_products")
        r_act = sem("rout_scalar_steps")
        r_dve = sem("rout_vector_steps")

        class Steps:

            def __init__(self, s):
                self.s, self.n = s, 0

            def inc(self, ins):
                ins.then_inc(self.s, 1)
                self.n += 1

            def link(self, eng, ins):
                self.inc(ins)
                eng.wait_ge(self.s, self.n)

        def stage_end(eng, stage):
            eng.drain().then_inc(s_bar, 1)
            eng.wait_ge(s_bar, 3 * (BASE[stage].index + 1))


        def pe_unit(pe, stage, n, j, i, per, rhs, bank, ev_wait, lo=0):
            u = U0[stage] + j
            slot = u % W_SLOTS
            pe.wait_ge(w_full[slot], 16 * (u // W_SLOTS + 1) + (per // W_SLOTS) * 16 * i)
            if ev_wait is not None:
                pe.wait_ge(s_ev, ev_wait)
            for k, r in enumerate(rhs):
                last = nc.tensor.matmul(bank, W[:, slot, (lo + k) * P:(lo + k + 1) * P], r,
                                        start=(k == 0), stop=(k == len(rhs) - 1))
            return last

        def pe_project(pe, stage, rhs, n_units, width=S):
            base = BASE[stage]
            e0 = base.ev
            with pe.Fori(0, n_units // 4) as i:
                for j in range(4):
                    pe_unit(pe, stage, 0, j, i, 4, rhs, psum[j][:, 0:width], 4 * i + (e0 + j - 3))\
                        .then_inc(unit_done, 1)

        def act_project(act, stage, dst, n_units, bias=None, func=ACT.Identity, width=S):
            base = BASE[stage]
            u0 = U0[stage]
            with act.Fori(0, n_units // 4) as i:
                for j in range(4):
                    act.wait_ge(unit_done, 4 * i + (u0 + j + 1))
                    b = 0.0 if bias is None else PRM[:, bass.ds(C0[bias[0]] + bias[1] + j + 4 * i, 1)]
                    nc.scalar.activation(dst[:, 4 * i + j, 0:width], psum[j][:, 0:width], func, bias=b)\
                        .then_inc(s_ev, 1)

        def split_weights(pool, stage):
            n = dict(STREAM)[stage]
            u0, p0 = U0[stage], 2 * SPLIT0[stage]

            def one(j, i=None, per=1):
                u = u0 + j
                slot, half = u % W_SLOTS, u % S_SLOTS
                at = 0 if i is None else per * i
                pool.wait_ge(w_full[slot], 16 * (u // W_SLOTS + 1) + (0 if i is None else 16 * (per // W_SLOTS) * i))
                pool.wait_ge(unit_done, at + (u - S_SLOTS + 1))
                nc.gpsimd.tensor_tensor(WS[:, half, 0], W[:, slot, :], ZERO[:, 0:1].to_broadcast([P, D]), ALU.add)\
                    .then_inc(s_split, 1)
                pool.wait_ge(s_split, 2 * at + (p0 + 2 * j + 1))
                nc.gpsimd.tensor_tensor(WS[:, half, 1], W[:, slot, :], WS[:, half, 0], ALU.subtract)\
                    .then_inc(s_split, 1)

            with pool.Fori(0, n // W_SLOTS) as i:
                for j in range(W_SLOTS):
                    one(j, i, W_SLOTS)
            for j in range(n // W_SLOTS * W_SLOTS, n):
                one(j)

        def pe_split(out_ap, slot, w, hi, lo, start, stop):
            w = slice(w * P, (w + 1) * P)
            nc.tensor.matmul(out_ap, WS[:, slot, 0, w], hi, start=start, stop=False)
            nc.tensor.matmul(out_ap, WS[:, slot, 0, w], lo, start=False, stop=False)
            return nc.tensor.matmul(out_ap, WS[:, slot, 1, w], hi, start=False, stop=stop)

        def act_norm_hi(act, stage, n, shift):
            base = BASE[stage]
            for k in range(n):
                act.wait_ge(s_dve, base.dve + 2 + k + 1)
                b = 0.0 if shift is None else shift[:, k:k + 1]
                nc.scalar.activation(HH[0][:, k, :], H[:, k, :], ACT.Identity, bias=b).then_inc(s_act, 1)

        def dve_norm_lo(dve, stage, n, shift):
            base = BASE[stage]
            for k in range(n):
                dve.wait_ge(s_act, base.act + n + 1 + k + 1)
                if shift is None:
                    ins = nc.vector.tensor_tensor(HH[1][:, k, :], H[:, k, :], HH[0][:, k, :], ALU.subtract)
                else:
                    ins = nc.vector.scalar_tensor_tensor(HH[1][:, k, :], H[:, k, :], shift[:, k:k + 1],
                                                         HH[0][:, k, :], ALU.add, ALU.subtract)
                ins.then_inc(s_dve, 1)

        def pe_norm(pe, stage, n, width=S):
            base = BASE[stage]
            for k in range(n):
                pe.wait_ge(s_act, base.act + k + 1)
                nc.tensor.matmul(psum[7][:, 0:width], con("ones"), SQ[:, k % 4, 0:width],
                                 start=(k == 0), stop=(k == n - 1)).then_inc(s_pe, 1)

        def act_norm(act, stage, src, n, width=S):
            base = BASE[stage]
            for k in range(n):
                if k >= 4:
                    act.wait_ge(s_pe, base.pe + k - 3)
                nc.scalar.activation(SQ[:, k % 4, 0:width], src[:, k, 0:width], ACT.Square).then_inc(s_act, 1)
            act.wait_ge(s_dve, base.dve + 1)
            nc.scalar.activation(ST[:, 1, 0:width], ST[:, 0, 0:width], ACT.Sqrt).then_inc(s_act, 1)

        def dve_rstd(dve, stage, n, width=S):
            base = BASE[stage]
            dve.wait_ge(s_pe, base.pe + n)
            nc.vector.tensor_scalar(ST[:, 0, 0:width], psum[7][:, 0:width], 1.0 / (n * P), EPS, ALU.mult, ALU.add)\
                .then_inc(s_dve, 1)
            dve.wait_ge(s_act, base.act + n + 1)
            nc.vector.reciprocal(ST[:, 0, 0:width], ST[:, 1, 0:width]).then_inc(s_dve, 1)
            dve.wait_ge(s_dve, base.dve + 2)

        def dve_norm(dve, stage, src, dst, gain, n, shift=None, width=S):
            base = BASE[stage]
            dve_rstd(dve, stage, n, width)
            for k in range(n):
                nc.vector.scalar_tensor_tensor(dst[:, k, 0:width], src[:, k, 0:width], gain[:, k:k + 1],
                                               ST[:, 0, 0:width], ALU.mult, ALU.mult).then_inc(s_dve, 1)
            if shift is not None:
                for k in range(n):
                    dve.wait_ge(s_dve, base.dve + 2 + k + 1)
                    nc.vector.tensor_scalar_add(dst[:, k, 0:width], dst[:, k, 0:width], shift[:, k:k + 1])

        def dve_residual(dve, stage, src, gain, n):
            base = BASE[stage]
            dve_rstd(dve, stage, n)
            for k in range(n):
                nc.vector.scalar_tensor_tensor(src[:, k, :], src[:, k, :], gain[:, k:k + 1],
                                               ST[:, 0, :], ALU.mult, ALU.mult).then_inc(s_dve, 1)
            for k in range(n):
                dve.wait_ge(s_dve, base.dve + 2 + k + 1)
                nc.vector.tensor_tensor(X[:, k, :], X[:, k, :], src[:, k, :], ALU.add)

        def pe_turn(pe, stage, blocks):
            base = BASE[stage]
            for b, four in enumerate(blocks):
                if b >= 4:
                    pe.wait_ge(s_act, base.act + b - 3)
                for q, src in enumerate(four):
                    last = nc.tensor.transpose(psum[b % 4][:, q * P:(q + 1) * P], src, con("ident"))
                last.then_inc(s_pe, 1)

        def act_turn(act, stage, dsts):
            base = BASE[stage]
            for b, dst in enumerate(dsts):
                act.wait_ge(s_pe, base.pe + b + 1)
                n = dst.shape[-1] if len(dst.shape) == 2 else dst.shape[-1] * dst.shape[-2]
                src = psum[b % 4][:, 0:n]
                if len(dst.shape) == 3:
                    src = src.rearrange("p (a b) -> p a b", b=dst.shape[-1])
                nc.scalar.activation(dst, src, ACT.Copy).then_inc(s_act, 1)

        SCORE_BANK = (0, 1, 6)

        def pe_attend(pe, stage, units):
            a0 = BASE[stage].att
            n = len(units)
            for i in range(n + 3):
                if i < n:
                    u = units[i]
                    if a0 + i >= 3:
                        pe.wait_ge(s_sfree, a0 + i - 2)
                    for c, (q, k) in enumerate(zip(u["q"], u["k"])):
                        last = nc.tensor.matmul(psum[SCORE_BANK[i % 3]][:, 0:u["nk"]], q, k, start=(c == 0),
                                                stop=(c == len(u["q"]) - 1))
                    last.then_inc(s_sc, 1)
                if 2 <= i < n + 2:
                    j = i - 2
                    u = units[j]
                    pe.wait_ge(s_exp, a0 + j + 1)
                    if a0 + j >= 2:
                        pe.wait_ge(s_pt, a0 + j - 1)
                    for b in range((u["nk"] + P - 1) // P):
                        w = min(P, u["nk"] - b * P)
                        out_t, in_t = psum[2 + j % 2][0:w, b * P:(b + 1) * P], PB[:, j % 3, b * P:b * P + w]
                        if w == P:
                            last = nc.tensor.transpose(out_t, in_t, con("ident"))
                        else:
                            last = nc.tensor.matmul(out_t, in_t, con("ident"), start=True, stop=True)
                    last.then_inc(s_tr, 1)
                if i >= 3:
                    j = i - 3
                    u = units[j]
                    pe.wait_ge(s_pt, a0 + j + 1)
                    if a0 + j >= 2:
                        pe.wait_ge(s_of, a0 + j - 1)
                    for b, v in enumerate(u["v"]):
                        w = v.shape[0]
                        last = nc.tensor.matmul(psum[4 + j % 2][:, 0:v.shape[1]], PT[0:w, j % 2, b * P:(b + 1) * P],
                                                v, start=(b == 0), stop=(b == len(u["v"]) - 1))
                    last.then_inc(s_pv, 1)

        def dve_attend(dve, stage, units, steps):
            a0 = BASE[stage].att
            n = len(units)
            for i in range(n + 3):
                if i < n:
                    u = units[i]
                    nk = u["nk"]
                    buf, top = PB[:, i % 3, 0:nk], SM[:, i % 3:i % 3 + 1]
                    dve.wait_ge(s_sc, a0 + i + 1)
                    if a0 + i >= 3:
                        dve.wait_ge(s_tr, a0 + i - 2)
                    src = psum[SCORE_BANK[i % 3]][:, 0:nk]
                    if u["bias"] is None:
                        ins = nc.vector.tensor_scalar(buf, src, u["scale"], None, ALU.mult)
                    else:
                        ins = nc.vector.scalar_tensor_tensor(buf, src, u["scale"], u["bias"], ALU.mult, ALU.add)
                    ins.then_inc(s_sfree, 1)
                    dve.wait_ge(s_sfree, a0 + i + 1)
                    if u["guard"]:
                        steps.link(dve, nc.vector.tensor_reduce(top, buf, AX_X, ALU.max, negate=True))
                        nc.vector.tensor_scalar(top, top, -0.01 * NEG, None, ALU.min).then_inc(s_mx, 1)
                    else:
                        nc.vector.tensor_reduce(top, buf, AX_X, ALU.max, negate=True).then_inc(s_mx, 1)
                if i >= 3:
                    j = i - 3
                    u = units[j]
                    m = 4 + j % 8
                    dve.wait_ge(s_exp, a0 + j + 1)
                    if u["guard"]:
                        steps.link(dve, nc.vector.tensor_scalar(SM[:, 16 + j % 2:17 + j % 2], SM[:, m:m + 1], 0.5, None,
                                                                ALU.max))
                        steps.link(dve, nc.vector.reciprocal(SM[:, 18 + j % 2:19 + j % 2], SM[:, 16 + j % 2:17 + j % 2]))
                    else:
                        steps.link(dve, nc.vector.reciprocal(SM[:, 18 + j % 2:19 + j % 2], SM[:, m:m + 1]))
                    f = SM[:, 18 + j % 2:19 + j % 2]
                    if u["gate"] is not None:
                        steps.link(dve, nc.vector.tensor_tensor(SM[:, 20 + j % 2:21 + j % 2], f, u["gate"], ALU.mult))
                        f = SM[:, 20 + j % 2:21 + j % 2]
                    dve.wait_ge(s_pv, a0 + j + 1)
                    src = psum[4 + j % 2][:, 0:u["v"][0].shape[1]]
                    if u["add"]:
                        dve.wait_ge(s_of, a0 + j)
                        ins = nc.vector.scalar_tensor_tensor(u["out"], src, f, u["out"], ALU.mult, ALU.add)
                    else:
                        ins = nc.vector.tensor_scalar(u["out"], src, f, None, ALU.mult)
                    ins.then_inc(s_of, 1)

        def act_attend(act, stage, units):
            a0 = BASE[stage].att
            n = len(units)
            for i in range(n + 2):
                if i < n:
                    u = units[i]
                    nk = u["nk"]
                    m = 4 + i % 8
                    act.wait_ge(s_mx, a0 + i + 1)
                    if a0 + i >= 8:
                        act.wait_ge(s_of, a0 + i - 7)
                    nc.scalar.activation(PB[:, i % 3, 0:nk], PB[:, i % 3, 0:nk], ACT.Exp, bias=SM[:, i % 3:i % 3 + 1],
                                         accum_out=SM[:, m:m + 1]).then_inc(s_exp, 1)
                if i >= 2:
                    j = i - 2
                    u = units[j]
                    nb = (u["nk"] + P - 1) // P
                    w = min(P, u["nk"])
                    act.wait_ge(s_tr, a0 + j + 1)
                    if a0 + j >= 2:
                        act.wait_ge(s_pv, a0 + j - 1)
                    nc.scalar.activation(PT[0:w, j % 2, 0:nb * P], psum[2 + j % 2][0:w, 0:nb * P], ACT.Copy)\
                        .then_inc(s_pt, 1)

        def pe_mix(pe, stage, per, gate_rhs, rhs_a, rhs_b):
            base = BASE[stage]
            e0 = base.ev
            tiles = 4 if per == 3 else 2
            with pe.Fori(0, DT // tiles) as i:
                for j in range(tiles):
                    bk = [psum[4 * (j % 2) + q][:, :] for q in range(4)]
                    ev = tiles * i + (e0 + j - 1)
                    u = per * j
                    pe_unit(pe, stage, 0, u, i, per * tiles, gate_rhs, bk[0], ev).then_inc(unit_done, 1)
                    if per == 3:
                        pe_unit(pe, stage, 0, u + 1, i, per * tiles, rhs_a, bk[1], None)
                        pe_unit(pe, stage, 0, u + 1, i, per * tiles, rhs_b, bk[3], None, lo=4).then_inc(unit_done, 1)
                        pe_unit(pe, stage, 0, u + 2, i, per * tiles, gate_rhs, bk[2], None).then_inc(unit_done, 1)
                    else:
                        pe_unit(pe, stage, 0, u + 1, i, per * tiles, rhs_a, bk[1], None).then_inc(unit_done, 1)
                        pe_unit(pe, stage, 0, u + 2, i, per * tiles, gate_rhs, bk[2], None).then_inc(unit_done, 1)
                        pe_unit(pe, stage, 0, u + 3, i, per * tiles, rhs_b, bk[3], None).then_inc(unit_done, 1)

        def act_mix(act, stage, per, bias_a, bias_b):
            base = BASE[stage]
            tiles = 4 if per == 3 else 2
            e0, g0, u0 = base.ev, base.glu, U0[stage]
            with act.Fori(0, DT // tiles) as i:
                for j in range(tiles):
                    n = tiles * i + j
                    act.wait_ge(s_ev, tiles * i + (e0 + j - 1))
                    for h, bias in enumerate((bias_a, bias_b)):
                        act.wait_ge(unit_done, per * tiles * i + (u0 + per * j + 2 * h + 1))
                        b = 0.0 if bias is None else PRM[:, bass.ds(C0["b_in"] + bias + j + tiles * i, 1)]
                        nc.scalar.activation(SQ[:, 2 * (j % 2) + h, :], psum[4 * (j % 2) + 2 * h][:, :], ACT.Sigmoid,
                                             bias=b).then_inc(s_glu, 1)

        def dve_mix(dve, stage, per, dst, bias):
            base = BASE[stage]
            tiles = 4 if per == 3 else 2
            e0, g0, u0, d0 = base.ev, base.glu, U0[stage], base.dve
            with dve.Fori(0, DT // tiles) as i:
                for j in range(tiles):
                    last = per * tiles * i + (u0 + per * (j + 1))
                    dve.wait_ge(s_glu, 2 * tiles * i + (g0 + 2 * j + 2))
                    dve.wait_ge(unit_done, last)
                    t = SQ[:, 2 * (j % 2), :]
                    v = SQ[:, 2 * (j % 2) + 1, :]
                    nc.vector.tensor_tensor(t, psum[4 * (j % 2) + 1][:, :], t, ALU.mult).then_inc(s_dve, 1)
                    b = 0.0 if bias is None else PRM[:, bass.ds(C0[bias] + j + tiles * i, 1)]
                    nc.vector.scalar_tensor_tensor(v, psum[4 * (j % 2) + 3][:, :], b, v, ALU.add, ALU.mult)\
                        .then_inc(s_dve, 1)
                    dve.wait_ge(s_dve, 2 * tiles * i + (d0 + 2 * j + 2))
                    nc.vector.tensor_tensor(dst[:, tiles * i + j, :], t, v, ALU.add).then_inc(s_ev, 1)

        def pe_up(pe, stage):
            base = BASE[stage]
            e0 = base.ev
            with pe.Fori(0, FT // 2) as i:
                for j in range(4):
                    pe.wait_ge(s_split, 8 * i + (2 * SPLIT0[stage] + 2 * j + 2))
                    pe.wait_ge(s_ev, 4 * i + (e0 + j - 3))
                    for k in range(DT):
                        last = pe_split(psum[j][:, :], (U0[stage] + j) % S_SLOTS, k, HH[0][:, k, :], HH[1][:, k, :],
                                        start=(k == 0), stop=(k == DT - 1))
                    last.then_inc(unit_done, 1)

        def taps(name, j, i, t):
            return PRM[:, bass.ds(C0[name] + 3 * j + t + 6 * i, 1)]

        def act_up(act, stage, both):
            base = BASE[stage]
            e0, u0, c0, t0, g0 = base.ev, U0[stage], base.conv, base.tap, base.gelu
            w, b = ("w_dw_ffn", "b_dw_ffn") if both else ("ffn_conv", "ffn_conv_b")
            with act.Fori(0, FT // 2) as i:
                for j in range(2):
                    act.wait_ge(s_ev, 4 * i + (e0 + 2 * j - 2))
                    for h in range(2 if both else 1):
                        off = FT * h
                        act.wait_ge(unit_done, 4 * i + (u0 + 2 * j + h + 1))
                        nc.scalar.activation(SQ[:, 2 * j + h, :], psum[2 * j + h][:, :], ACT.Identity,
                                             scale=taps(w, off + j, i, 2),
                                             bias=PRM[:, bass.ds(C0[b] + off + j + 2 * i, 1)]).then_inc(s_tap, 1)
                    act.wait_ge(s_conv, 2 * i + (c0 + j + 1))
                    t = SQ[:, 2 * j + (1 if both else 0), :]
                    nc.scalar.activation(t, t, ACT.Gelu_apprx_tanh if both else ACT.Silu).then_inc(s_gelu, 1)
                    act.wait_ge(s_prod, 2 * i + (base.prod + j + 1))
                    nc.scalar.activation(HIDS[0][:, 2 * i + j, :], SQ[:, 2 * j, :], ACT.Copy).then_inc(s_hi, 1)

        def dve_up(dve, stage, both):
            base = BASE[stage]
            e0, u0, c0, t0, g0, d0 = base.ev, U0[stage], base.conv, base.tap, base.gelu, base.dve
            w = "w_dw_ffn" if both else "ffn_conv"
            nh = 2 if both else 1
            with dve.Fori(0, FT // 2) as i:
                for j in range(2):
                    for h in range(nh):
                        off = FT * h
                        t, bank = SQ[:, 2 * j + h, :], psum[2 * j + h]
                        dve.wait_ge(s_tap, 2 * nh * i + (t0 + nh * j + h + 1))
                        nc.vector.scalar_tensor_tensor(t[:, 1:S], bank[:, 0:S - 1], taps(w, off + j, i, 1),
                                                       t[:, 1:S], ALU.mult, ALU.add).then_inc(s_dve, 1)
                    for h in range(nh):
                        off = FT * h
                        t, bank = SQ[:, 2 * j + h, :], psum[2 * j + h]
                        dve.wait_ge(s_dve, 2 * nh * i + (d0 + nh * j + h + 1))
                        ins = nc.vector.scalar_tensor_tensor(t[:, 2:S], bank[:, 0:S - 2], taps(w, off + j, i, 0),
                                                             t[:, 2:S], ALU.mult, ALU.add)
                    ins.then_inc(s_conv, 1)
                    dve.wait_ge(s_gelu, 2 * i + (g0 + j + 1))
                    if both:
                        dve.wait_ge(s_conv, 2 * i + (c0 + j + 1))
                        val = SQ[:, 2 * j, :]
                        gt = SQ[:, 2 * j + 1, :]
                    else:
                        dve.wait_ge(unit_done, 4 * i + (u0 + 2 * j + 2))
                        val = psum[2 * j + 1][:, :]
                        gt = SQ[:, 2 * j, :]
                    nc.vector.tensor_tensor(SQ[:, 2 * j, :], val, gt, ALU.mult).then_inc(s_prod, 1)
                    dve.wait_ge(s_hi, 2 * i + (base.prod + j + 1))
                    nc.vector.tensor_tensor(HIDS[1][:, 2 * i + j, :], SQ[:, 2 * j, :], HIDS[0][:, 2 * i + j, :],
                                            ALU.subtract).then_inc(s_ev, 2)

        def pe_down(pe, stage):
            base = BASE[stage]
            u0 = U0[stage]

            def unit(j, i, k, start=False, stop=False):
                pe.wait_ge(s_split, 8 * i + (2 * SPLIT0[stage] + 2 * j + 2))
                for n in range(DT):
                    last = pe_split(psum[n][:, :], (u0 + j) % S_SLOTS, n, HIDS[0][:, k, :], HIDS[1][:, k, :],
                                    start=start, stop=stop)
                last.then_inc(unit_done, 1)

            unit(0, 0, 0, start=True)
            with pe.Fori(0, (FT - 2) // 4) as i:
                for j in range(4):
                    unit(1 + j, i, 4 * i + (1 + j))
            unit(FT - 1, 0, FT - 1, stop=True)

        def act_down(act, stage, dst):
            base = BASE[stage]
            act.wait_ge(unit_done, U0[stage] + FT)
            for n in range(0, DT, 2):
                nc.scalar.activation(dst[:, n, :], psum[n][:, :], ACT.Copy)

        def dve_down(dve, stage, dst):
            base = BASE[stage]
            dve.wait_ge(unit_done, U0[stage] + FT)
            for n in range(1, DT, 2):
                nc.vector.tensor_copy(dst[:, n, :], psum[n][:, :])


        def dve_add_project(dve, stage, n_units):
            base = BASE[stage]
            u0 = U0[stage]
            with dve.Fori(0, n_units // 4) as i:
                for j in range(4):
                    dve.wait_ge(unit_done, 4 * i + (u0 + j + 1))
                    nc.vector.tensor_tensor(X[:, 4 * i + j, :], X[:, 4 * i + j, :], psum[j][:, :], ALU.add)\
                        .then_inc(s_ev, 1)

        def pe_heads(pe, stage, n, ones, group, width=S):
            base = BASE[stage]
            for t in range(0, n, 4):
                for k in range(4):
                    b = 4 + k // group
                    pe.wait_ge(s_act, base.act + t + t // 4 + k + 1)
                    nc.tensor.matmul(psum[b][:, 0:width], ones, SQ[:, k, 0:width], start=(k % group == 0),
                                     stop=(k % group == group - 1)).then_inc(s_pe, 1)

        def act_heads(act, stage, src, n, group, width=S):
            base = BASE[stage]
            for t in range(0, n, 4):
                if t:
                    act.wait_ge(s_dve, base.dve + (2 * 4 + 1) * (t // 4))
                for k in range(4):
                    nc.scalar.activation(SQ[:, k, 0:width], src[t + k], ACT.Square).then_inc(s_act, 1)
                act.wait_ge(s_dve, base.dve + (2 * 4 + 1) * (t // 4) + 4 // group)
                nc.scalar.activation(SQ[:, 0:4 // group, 0:width], SQ[:, 0:4 // group, 0:width], ACT.Sqrt)\
                    .then_inc(s_act, 1)

        def dve_heads(dve, stage, src, n, group, gain, width, dim):
            base = BASE[stage]
            for t in range(0, n, 4):
                d0 = base.dve + (2 * 4 + 1) * (t // 4)
                for k in range(4 // group):
                    dve.wait_ge(s_pe, base.pe + t + 4)
                    nc.vector.tensor_scalar(SQ[:, k, 0:width], psum[4 + k][:, 0:width], 1.0 / dim, EPS, ALU.mult,
                                            ALU.add).then_inc(s_dve, 1)
                dve.wait_ge(s_act, base.act + t + t // 4 + 5)
                nc.vector.reciprocal(SQ[:, 0:4 // group, 0:width], SQ[:, 0:4 // group, 0:width]).then_inc(s_dve, 1)
                dve.wait_ge(s_dve, d0 + 4 // group + 1)
                for k in range(4):
                    ins = nc.vector.scalar_tensor_tensor(src[t + k], src[t + k], gain[t + k], SQ[:, k // group, 0:width],
                                                         ALU.mult, ALU.mult)
                    ins.then_inc(s_dve, 1 if k < 3 else 1 + 4 - 4 // group)

        h_tiles = [H[:, k, :] for k in range(DT)]

        def tiles(a, n):
            return [BIG[:, a + k, :] for k in range(n)]

        PB = BIG[:, 41:44, :]
        PT = BIG[:, 44:46, :]
        Q1, K1, V1 = BIG[:, 0:4, :], BIG[:, 4:8, :], BIG[:, 8:12, :]
        VT1 = BIG[:, 12:16, :]
        LEAD = 32
        GPAD = LEAD + S
        GLU = BIG[:, 16:21, :].rearrange("p a b -> p (a b)")[:, 0:4 * GPAD].rearrange("p (a b) -> p a b", b=GPAD)
        CV = BIG[:, 21:25, :]
        O1 = BIG[:, 25:29, :]
        OT1 = BIG[:, 29:33, :]
        BIAS1 = BIG[:, 33:41, :]
        Y1 = BIG[:, 46:54, :]
        Z1 = BIG[:, 54:62, :]
        HIDS = [BIGR[:, FT * h:FT * (h + 1), :] for h in range(2)]
        HH = [BIGR[:, 44 + DT * h:44 + DT * (h + 1), :] for h in range(2)]
        WS = BIGR[:, 60:68, :].rearrange("p a b -> p (a b)").rearrange("p (s h d) -> p s h d", s=S_SLOTS, h=2)
        RT, AT, BT, KT = BIG[:, 0:8, :], BIG[:, 8:16, :], BIG[:, 16:24, :], BIG[:, 24:32, :]
        RV, BON = BIG[:, 32:40, :], BIG[:, 40:48, :]
        ZL = BIG[:, 48:51, :]
        LR = BIG[:, 51:57, :].rearrange("p a b -> p (a b)").rearrange("p (a b) -> p a b", b=D)
        TMP = tiles(57, 11)
        YR = AT
        QN = BIG[:, 16:24, :]
        NSA = BIG[:, 16:36, :]
        KC, VC, KS, VS, KW, VW = (BIG[:, 24 + 2 * k:26 + 2 * k, :] for k in range(6))
        VT2 = BIG[:, 36:40, :]
        SH = BIG[:, 0:4, :]
        BLK = BIG[:, 4:8, :].rearrange("p a b -> p (a b)")[:, 0:16 * 4 * N_CMP].rearrange("p (k n) -> p k n", k=16)
        BLK_V = BIG[:, 48:52, :].rearrange("p a b -> p (a b)")[:, 0:16 * 4 * N_CMP].rearrange("p (k n) -> p k n", k=16)
        HC = BIG[:, 40, 0:2 * 4 * N_CMP].rearrange("p (c n) -> p c n", c=2)
        HV = BIG[:, 46, 0:2 * 4 * N_CMP].rearrange("p (c n) -> p c n", c=2)
        KCN = BIG[:, 47, 0:4 * N_CMP]
        VCT = BIG[:, 47, 128:128 + 4 * DH]
        BIAS2 = BIG[:, 52:68, :]
        O2 = BIG[:, 0:8, :].rearrange("p a b -> p (a b)").rearrange("p (a b) -> p a b", b=D)
        OT2 = BIG[:, 16:24, :]
        Y2 = BIG[:, 24:32, :]
        Q3, K3, V3 = BIG[:, 0:8, :], BIG[:, 8:16, 0:N_MEM], BIG[:, 16:24, 0:N_MEM]
        VT3 = BIG[:, 24:28, :].rearrange("p a b -> p (a b)").rearrange("p (a b) -> p a b", b=D)
        MEM, MN = BIG[:, 48:56, :], BIG[:, 56:64, :]
        O3 = BIG[:, 28:36, :].rearrange("p a b -> p (a b)").rearrange("p (a b) -> p a b", b=D)
        OT3 = BIG[:, 8:16, :]

        CB = BIG[:, 0:2, :].rearrange("p a b -> p (a b)")
        MP = [BIG[:, 2 + 2 * k:4 + 2 * k, :].rearrange("p a b -> p (a b)") for k in range(2)]

        units1 = []
        for h in range(H1):
            lo = DH * (h % 2)
            for qi in range(S // P):
                nk = P * (qi + 1)
                units1.append(dict(
                    q=[Q1[lo:lo + DH, h // 2, qi * P:(qi + 1) * P]], k=[K1[lo:lo + DH, h // 2, 0:nk]], nk=nk,
                    bias=BIAS1[:, h, S - nk:S], scale=DH ** -0.5,
                    v=[VT1[:, b, h * DH:(h + 1) * DH] for b in range(qi + 1)],
                    out=O1[:, qi, h * DH:(h + 1) * DH], gate=None, add=False, guard=False))

        units2 = []
        for h in range(H2):
            g, hg = h // HG, h % HG
            lo = DH * (g % 2)
            for qi in range(S // P):
                nk = P * (qi + 1)
                q = QN[lo:lo + DH, (g // 2) * HG + hg, qi * P:(qi + 1) * P]
                out_ap = O2[:, qi, h * DH:(h + 1) * DH]
                for br, (keys, vcol) in enumerate(((KS, 0), (KW, N_KV * DH))):
                    units2.append(dict(
                        q=[q], k=[keys[lo:lo + DH, g // 2, 0:nk]], nk=nk, bias=BIAS2[:, h, S - nk:S],
                        scale=DH ** -0.5, v=[VT2[:, b, vcol + g * DH:vcol + (g + 1) * DH] for b in range(qi + 1)],
                        out=out_ap, gate=GT[:, qi, 3 * h + 1 + br:3 * h + 2 + br], add=(br == 1), guard=False))
                nc_keys = min(N_CMP, (P * (qi + 1) - CMP_BLOCK) // CMP_STRIDE + 1)
                first = S - P * (qi + 1) + CMP_BLOCK - 1
                units2.append(dict(
                    q=[q], k=[KCN[lo:lo + DH, g * N_CMP:g * N_CMP + nc_keys]], nk=nc_keys,
                    bias=BIAS2[:, h, first:first + CMP_STRIDE * (nc_keys - 1) + 1:CMP_STRIDE], scale=DH ** -0.5,
                    v=[VCT[0:nc_keys, g * DH:(g + 1) * DH]], out=out_ap, gate=GT[:, qi, 3 * h:3 * h + 1],
                    add=True, guard=True))

        units3 = []
        for h in range(CA_HEADS):
            for qi in range(S // P):
                units3.append(dict(
                    q=[Q3[:, 2 * h + c, qi * P:(qi + 1) * P] for c in range(2)],
                    k=[K3[:, 2 * h + c, :] for c in range(2)], nk=N_MEM, bias=None, scale=(D // CA_HEADS) ** -0.5,
                    v=[VT3[:, b, h * 256:(h + 1) * 256] for b in range(2)],
                    out=O3[:, qi, h * 256:(h + 1) * 256], gate=None, add=False, guard=False))

        free = TMP + tiles(51, 2) + h_tiles + [SQ[:, k, :] for k in range(4)] + [ST[:, k, :] for k in range(2)]
        HANDED = [free[9 * p:9 * p + 9] for p in range(2)]
        ND, MD, MO, N2, M2, Rs, U0s, Us, TS = free[18:27]
        N4, M4, M8, F2, U1s, TN = ND, MD, N2, M2, Rs, U0s
        N_CH = S // CHUNK

        def pair3(ap):
            return ap.rearrange("p (j c) -> p j c", c=CHUNK)

        def mask3(name):
            return con(name).rearrange("p (j c) -> p j c", j=1).to_broadcast([P, DT, CHUNK])

        def pe_rchunks(pe):
            def full(tile, c):
                return lambda lo, j: tile[lo:lo + DH, j, c * CHUNK:(c + 1) * CHUNK]

            def loc(tile):
                return lambda lo, j: tile[lo:lo + CHUNK, j * CHUNK:(j + 1) * CHUNK]

            def eye():
                return lambda lo, j: CON[lo:lo + DH, K0["ident"] + lo:K0["ident"] + lo + DH]

            def products(done, bank, *pairs):
                for j in range(DT):
                    for lo in (0, CHUNK):
                        for q, (lhs, rhs) in enumerate(pairs):
                            last = nc.tensor.matmul(psum[bank][lo:lo + CHUNK, j * CHUNK:(j + 1) * CHUNK],
                                                    lhs(lo, j), rhs(lo, j), start=(q == 0), stop=(q == len(pairs) - 1))
                last.then_inc(done, 1)

            def apart(c, n):
                r, a, b, k, v = (full(t, c) for t in (RT, AT, BT, KT, RV))
                XI, FT2 = HANDED[c % 2][6:8]
                if n == 1 and c:
                    pe.wait_ge(c_act, 11 * c)
                    pe.wait_ge(c_dve, 10 * c)
                vec = {7: 1, 8: 3, 9: 5, 10: 6, 11: 7, 14: 8, 16: 9, 17: 10}
                cop = {11: 5, 12: 5, 13: 5, 14: 7, 15: 7, 16: 8, 19: 10}
                if n in vec:
                    pe.wait_ge(c_dve, 10 * c + vec[n])
                if n in cop:
                    pe.wait_ge(c_act, 11 * c + cop[n])
                operands = {
                    1: (b, a), 2: (a, b), 3: (k, a), 4: (b, r), 5: (k, r), 6: (b, eye()), 7: (k, eye()), 8: (v, eye()),
                    9: (loc(MD), loc(ND)),
                    10: (loc(ND), loc(MD)),
                    11: (loc(M2), loc(XI)),
                    12: (loc(M2), loc(N2)),
                    13: (loc(N2), loc(M2)),
                    14: (loc(M4), loc(XI)),
                    15: (loc(N4), loc(M4)),
                    16: (loc(M8), loc(XI)),
                    17: (loc(MO), loc(XI)),
                    18: (loc(XI), loc(MO)),
                    19: (loc(F2), loc(FT2)),
                }
                products(c_pe, (n - 1) % 6, operands[n])

            def along(c, n):
                AKT, RBT, RKT, Bt, Kt, Vt, XI, FT2, FT4 = HANDED[c % 2]
                if n == 1:
                    pe.wait_ge(q_dve, 4 * c + 1)
                    if c:
                        pe.wait_ge(q_act, 3 * c)
                    products(q_pe, 6, (full(AT, c), loc(TS)), (loc(AKT), loc(Vt)))
                elif n == 2:
                    pe.wait_ge(q_act, 3 * c + 1)
                    products(q_pe, 7, (loc(XI), loc(Rs)))
                elif n == 3:
                    pe.wait_ge(q_act, 3 * c + 2)
                    pe.wait_ge(c_act, 11 * (c + 1))
                    products(q_pe, 6, (loc(FT4), loc(U0s)))
                elif n == 4:
                    pe.wait_ge(q_dve, 4 * c + 2)
                    products(q_pe, 7, (loc(FT2), loc(U1s)))
                elif n == 5:
                    pe.wait_ge(q_dve, 4 * c + 3)
                    products(q_pe, 6, (loc(TS), full(RT, c)), (loc(Us), loc(RBT)), (loc(Vt), loc(RKT)))
                else:
                    products(q_pe, 7, (loc(Bt), loc(Us)), (loc(Kt), loc(Vt)))

            for c in range(N_CH + 1):
                for kind, n in ORDER:
                    if kind == "apart" and c < N_CH:
                        apart(c, n)
                    if kind == "along" and c >= 1:
                        along(c - 1, n)

        ORDER = [("apart", n) for n in range(1, 11)] + [
            ("along", 1), ("apart", 11), ("apart", 12), ("apart", 13), ("along", 2), ("apart", 14), ("apart", 15),
            ("along", 3), ("apart", 16), ("along", 4), ("apart", 17), ("apart", 18), ("along", 5), ("apart", 19),
            ("along", 6)]

        def act_rchunks(act):
            for c in range(N_CH + 1):
                Bt, Kt, Vt, XI, FT2, FT4 = HANDED[c % 2][3:]
                copies = {6: (Bt, 5), 7: (Kt, 0), 8: (Vt, 1), 9: (N2, 2), 10: (M2, 3), 12: (N4, 5), 13: (M4, 0),
                          15: (M8, 2), 17: (FT2, 4), 18: (F2, 5), 19: (FT4, 0)}
                for kind, n in ORDER:
                    if kind == "apart" and c < N_CH and n in copies:
                        dst, bank = copies[n]
                        act.wait_ge(c_pe, 19 * c + n)
                        nc.scalar.activation(dst, psum[bank][:, :], ACT.Copy).then_inc(c_act, 1)
                    if kind == "along" and c >= 1 and n in (1, 2):
                        act.wait_ge(q_pe, 6 * (c - 1) + n)
                        nc.scalar.activation((Rs, U0s)[n - 1], psum[5 + n][:, :], ACT.Copy).then_inc(q_act, 1)
                    if kind == "along" and c >= 1 and n == 5:
                        act.wait_ge(q_pe, 6 * (c - 1) + 5)
                        nc.scalar.activation(RT[:, :, (c - 1) * CHUNK:c * CHUNK], pair3(psum[6][:, :]), ACT.Copy)\
                            .then_inc(q_act, 1)

        def dve_rchunks(dve):
            nc.vector.memset(TS, 0.0).then_inc(q_dve, 1)
            for c in range(N_CH + 1):
                AKT, RBT, RKT, Bt, Kt, Vt, XI, FT2, FT4 = HANDED[c % 2]

                def masked(dst, bank, mask):
                    nc.vector.tensor_tensor(pair3(dst), pair3(psum[bank][:, :]), mask3(mask), ALU.mult).then_inc(c_dve, 1)

                for kind, n in ORDER:
                    if kind == "apart" and c < N_CH:
                        if n in (1, 2, 3, 4, 5, 11, 14, 16):
                            dve.wait_ge(c_pe, 19 * c + n)
                        if n == 1:
                            masked(ND, 0, "up16")
                        if n == 2:
                            masked(MD, 1, "lo16")
                            masked(MO, 1, "lo_off")
                            dve.wait_ge(c_dve, 10 * c + 1)
                            nc.vector.tensor_tensor(pair3(XI), pair3(ND), mask3("eye64"), ALU.add).then_inc(c_dve, 1)
                        if n == 3:
                            masked(AKT, 2, "strict_up")
                        if n == 4:
                            masked(RBT, 3, "incl_up")
                        if n == 5:
                            masked(RKT, 4, "incl_up")
                        if n in (11, 14, 16):
                            dve.wait_ge(c_dve, 10 * c + {11: 4, 14: 8, 16: 9}[n])
                            nc.vector.tensor_tensor(XI, psum[(n - 1) % 6][:, :], XI, ALU.add).then_inc(c_dve, 1)
                    if kind == "along" and c >= 1:
                        if n in (3, 4, 6):
                            dve.wait_ge(q_pe, 6 * (c - 1) + n)
                        if n == 3:
                            dve.wait_ge(q_act, 3 * (c - 1) + 2)
                            nc.vector.tensor_tensor(U1s, psum[6][:, :], U0s, ALU.add).then_inc(q_dve, 1)
                        if n == 4:
                            dve.wait_ge(q_dve, 4 * (c - 1) + 2)
                            nc.vector.tensor_tensor(Us, psum[7][:, :], U1s, ALU.add).then_inc(q_dve, 1)
                        if n == 6:
                            nc.vector.tensor_tensor(TN, psum[7][:, :], TS, ALU.add).then_inc(q_dve, 1)
                            dve.wait_ge(q_dve, 4 * (c - 1) + 4)
                            nc.vector.tensor_tensor(pair3(TS), pair3(TN),
                                                    DEC[:, :, c - 1:c].to_broadcast([P, DT, CHUNK]), ALU.mult)\
                                .then_inc(q_dve, 1)

        UK = U0["rkv"]
        EH = float(np.exp(-0.5))

        def pe_rprep(pe):
            pe.wait_ge(s_lora, 32)

            def sums(j):
                pe.wait_ge(e_sq, j + 1)
                nc.tensor.matmul(psum[5][:, :], con("blk"), SQ[:, 0, :], start=True, stop=True).then_inc(e_ss, 1)
                pe.wait_ge(e_rp, j + 1)
                nc.tensor.matmul(psum[6][:, :], con("blk"), SQ[:, 1, :], start=True, stop=True).then_inc(e_bs, 1)

            for j in range(DT):
                if j:
                    pe.wait_ge(e_sig, 2 * j)
                nc.tensor.matmul(psum[3][:, :], LR[0:64, 0, j * P:(j + 1) * P], ZL[0:64, 0, :], start=True, stop=True)
                nc.tensor.matmul(psum[4][:, :], LR[64:128, 0, j * P:(j + 1) * P], ZL[64:128, 0, :], start=True,
                                 stop=True).then_inc(e_log, 1)
                for q in range(3):
                    if j:
                        pe.wait_ge(e_shift, 3 * j - 2 + q)
                    pe_unit(pe, "rkv", 0, 3 * j + q, 0, 0, h_tiles, psum[q][:, :], None).then_inc(unit_done, 1)
                    if q == 0 and j:
                        sums(j - 1)
            sums(DT - 1)

        def act_rprep(act):
            sw, a, cs, ex, rt = TMP[0], TMP[1], TMP[2], TMP[3], TMP[4]
            for j in range(DT):
                act.wait_ge(e_log, j + 1)
                if j:
                    act.wait_ge(e_done, j)
                nc.scalar.activation(sw, psum[3][:, :], ACT.Sigmoid, bias=prm("w0", j)).then_inc(e_sig, 1)
                nc.scalar.activation(a, psum[4][:, :], ACT.Sigmoid, bias=prm("a0", j)).then_inc(e_sig, 1)
                for q, dst in enumerate((KT, RT, RV)):
                    act.wait_ge(unit_done, UK + 3 * j + q + 1)
                    nc.scalar.activation(dst[:, j, :], psum[q][:, :], ACT.Copy, scale=OMU[:, 4 + 3 * j + q:5 + 3 * j + q])\
                        .then_inc(e_keep, 1)
                act.wait_ge(e_kk, j + 1)
                nc.scalar.activation(SQ[:, 0, :], TMP[5], ACT.Square).then_inc(e_sq, 1)
                act.wait_ge(e_scan, j + 1)
                nc.scalar.activation(rt, cs, ACT.Exp, scale=-EH).then_inc(e_dec, 1)
                nc.scalar.activation(ex, ex, ACT.Exp, scale=-EH).then_inc(e_dec, 1)
                nc.scalar.activation(TMP[8], cs, ACT.Exp, scale=EH).then_inc(e_dec, 1)
                act.wait_ge(e_ss, j + 1)
                nc.scalar.activation(TMP[6], psum[5][:, :], ACT.Sqrt).then_inc(e_root, 1)

        def dve_rprep(dve, steps):
            V = nc.vector
            sw, a, cs, ex, inc, kk, nrm, k2, inv = TMP[0], TMP[1], TMP[2], TMP[3], TMP[4], TMP[5], TMP[6], TMP[7], TMP[8]
            for j in range(DT):
                k, r, v = KT[:, j, :], RT[:, j, :], RV[:, j, :]
                for q, dst in enumerate((k, r, v)):
                    dve.wait_ge(e_keep, 3 * j + q + 1)
                    V.scalar_tensor_tensor(dst[:, 1:S], psum[q][:, 0:S - 1], prm("mu", 4 + 3 * j + q), dst[:, 1:S],
                                           ALU.mult, ALU.add).then_inc(e_shift, 1)
                dve.wait_ge(e_shift, 3 * j + 3)
                V.tensor_scalar(kk, k, prm("kk", j), None, ALU.mult).then_inc(e_kk, 1)
                dve.wait_ge(e_sig, 2 * j + 2)
                steps.link(dve, V.tensor_tensor_scan(cs, con("scan"), sw, 0.0, ALU.mult, ALU.add))
                V.tensor_tensor(ex, cs, sw, ALU.subtract).then_inc(e_scan, 1)
                steps.link(dve, V.tensor_scalar(k2, a, 1.0, prm("ka", j), ALU.subtract, ALU.mult))
                steps.link(dve, V.scalar_tensor_tensor(k2, k2, 1.0, k, ALU.add, ALU.mult))
                if j:
                    dve.wait_ge(e_bs, j)
                V.scalar_tensor_tensor(SQ[:, 1, :], r, prm("rk", j), k2, ALU.mult, ALU.mult).then_inc(e_rp, 1)
                dve.wait_ge(e_dec, 3 * j + 3)
                V.tensor_copy(DEC[:, j, :], inc[:, CHUNK - 1:S:CHUNK])
                dve.wait_ge(e_rp, j + 1)
                V.tensor_tensor(r, r, inc, ALU.mult)
                V.tensor_tensor(k, k2, inv, ALU.mult)
                dve.wait_ge(e_root, j + 1)
                steps.link(dve, V.tensor_scalar(nrm, nrm, 1e-12, None, ALU.max))
                steps.link(dve, V.reciprocal(nrm, nrm))
                dve.wait_ge(e_kk, j + 1)
                steps.link(dve, V.tensor_tensor(kk, kk, nrm, ALU.mult))
                V.scalar_tensor_tensor(AT[:, j, :], kk, -1.0, ex, ALU.mult, ALU.mult)
                steps.link(dve, V.tensor_tensor(a, a, inv, ALU.mult))
                V.tensor_tensor(BT[:, j, :], kk, a, ALU.mult)
                dve.wait_ge(e_bs, j + 1)
                V.tensor_tensor(BON[:, j, :], psum[6][:, :], v, ALU.mult).then_inc(e_done, 1)

        def pe_rout(pe):
            for j in range(DT):
                if j:
                    pe.wait_ge(r_dve, 6 * j)
                nc.tensor.matmul(psum[0][:, :], con("blk"), RT[:, j, :], start=True, stop=True).then_inc(r_pe, 1)
                nc.tensor.matmul(psum[2][:, :], LR[:, 1, j * P:(j + 1) * P], ZL[:, 1, :], start=True, stop=False)
                nc.tensor.matmul(psum[2][:, :], LR[0:32, 2, j * P:(j + 1) * P], ZL[0:32, 2, :], start=False, stop=True)\
                    .then_inc(r_pe, 1)
                pe.wait_ge(r_act, 3 * j + 1)
                nc.tensor.matmul(psum[1][:, :], con("blk"), TMP[0], start=True, stop=True).then_inc(r_pe, 1)

        def act_rout(act):
            for j in range(DT):
                act.wait_ge(r_dve, 6 * j + 1)
                nc.scalar.activation(TMP[0], RT[:, j, :], ACT.Square).then_inc(r_act, 1)
                act.wait_ge(r_dve, 6 * j + 2)
                nc.scalar.activation(TMP[1], TMP[1], ACT.Sqrt).then_inc(r_act, 1)
                act.wait_ge(r_dve, 6 * j + 4)
                nc.scalar.activation(YR[:, j, :], RT[:, j, :], ACT.Identity, bias=prm("lnx_b", j)).then_inc(r_act, 1)

        def dve_rout(dve, steps):
            V = nc.vector
            for j in range(DT):
                y = RT[:, j, :]
                dve.wait_ge(r_pe, 3 * j + 1)
                V.scalar_tensor_tensor(y, psum[0][:, :], -1.0 / DH, y, ALU.mult, ALU.add).then_inc(r_dve, 1)
                dve.wait_ge(r_pe, 3 * j + 3)
                V.tensor_scalar(TMP[1], psum[1][:, :], 1.0 / DH, LNX_EPS, ALU.mult, ALU.add).then_inc(r_dve, 1)
                dve.wait_ge(r_act, 3 * j + 2)
                V.reciprocal(TMP[2], TMP[1]).then_inc(r_dve, 1)
                dve.wait_ge(r_dve, 6 * j + 3)
                V.scalar_tensor_tensor(y, y, prm("lnx_w", j), TMP[2], ALU.mult, ALU.mult).then_inc(r_dve, 1)
                dve.wait_ge(r_act, 3 * j + 3)
                V.tensor_tensor(YR[:, j, :], YR[:, j, :], BON[:, j, :], ALU.add).then_inc(r_dve, 1)
                dve.wait_ge(r_dve, 6 * j + 5)
                V.tensor_tensor(YR[:, j, :], psum[2][:, :], YR[:, j, :], ALU.mult).then_inc(r_dve, 1)

        block = ctx.enter_context(nc.Block())

        @block.sync
        def _(sp):
            sp.dma_start(PRM[:], cols[:, :]).then_inc(s_prm, 16)
            sp.dma_start(CON[:], const[:, :]).then_inc(s_prm, 16)
            for j in range(W_SLOTS):
                sp.dma_start(W[:, j, :], stream[j]).then_inc(w_full[j], 16)
            with sp.Fori(1, N_UNITS // W_SLOTS) as i:
                for j in range(W_SLOTS):
                    sp.wait_ge(unit_done, W_SLOTS * i + (j - W_SLOTS + 1))
                    sp.dma_start(W[:, j, :], stream[W_SLOTS * i + j]).then_inc(w_full[j], 16)
            sp.wait_ge(s_bar, 3 * N_ENDS)
            sp.dma_start(out.rearrange("(k p) t -> p k t", p=P), X[:]).then_inc(s_out, 16)
            sp.wait_ge(s_out, 16)

        @block.gpsimd
        def _(pool):
            pool.memset(ZERO[:, :], 0.0).then_inc(s_pool, 1)
            pool.dma_start(CB, c_rows[:, :]).then_inc(s_c, 16)
            pool.dma_start(X[:], x_t.rearrange("(k p) t -> p k t", p=P)).then_inc(s_x, 16)
            pool.dma_start(TAB[:], table2[:, :]).then_inc(s_small, 16)
            pool.dma_start(CW2[:], cmp_w2[:, :, :]).then_inc(s_small, 16)
            pool.dma_start(BIG[0:BUCKETS, 60, :], onehot[:, :]).then_inc(s_small, 16)
            line = BIG[0:H1, 61:63, :].rearrange("p a b -> p (a b)")
            pool.dma_start(line[:, 383:383 + 257], line1[:, :]).then_inc(s_line, 16)
            pool.wait_ge(s_line, 16)
            pool.tensor_copy(line[:, 0:383], line[:, 383:384].to_broadcast([H1, 383])).then_inc(s_pool, 1)
            pool.wait_ge(s_pool, 2)
            pool.dma_start(scratch[0, 0:H1, :], line[:, 0:LINE]).then_inc(s_line, 16)
            pool.wait_ge(s_line, 32)
            toeplitz = bass.AP(tensor=scratch.tensor, offset=P - 1, ap=[[LINE, H1], [-1, P], [1, S]])
            pool.dma_start(rows[0:H1], toeplitz).then_inc(s_rows, 16)
            pool.wait_ge(s_rows, 16)
            pool.dma_start(BIAS1[:, :, :], rows[0:H1].rearrange("h p m -> p h m")).then_inc(s_bias, 16)
            pool.wait_ge(s_bias, 16)
            pool.memset(BIAS1[0:CHUNK, :, S - CHUNK:S], NEG).then_inc(s_pool, 1)
            pool.wait_ge(s_line2, 16)
            toeplitz2 = bass.AP(tensor=scratch.tensor, offset=H2 * LINE + P - 1, ap=[[LINE, H2], [-1, P], [1, S]])
            pool.dma_start(rows[H1:H1 + H2], toeplitz2).then_inc(s_rows, 16)
            pool.wait_ge(s_rows, 32)
            pool.wait_ge(s_bar, 3 * BASE["norm_ffn1"].index)
            split_weights(pool, "up1")
            split_weights(pool, "down1")
            pool.wait_ge(s_bar, 3 * (BASE["norm_r"].index))
            pool.dma_start(LR[:, 0, :], w2a2[:, :]).then_inc(s_lora, 16)
            pool.dma_start(LR[:, 1:3, :], g2[:, :, :]).then_inc(s_lora, 16)
            pool.wait_ge(s_bar, 3 * (BASE["norm_n"].index))
            pool.dma_start(BIAS2[:, :, :], rows[H1:H1 + H2].rearrange("h p m -> p h m")).then_inc(s_bias2, 16)
            pool.wait_ge(s_bar, 3 * (BASE["norm_c"].index))
            pool.dma_start(MEM[:, :, 0:N_MEM], mem_t.rearrange("(k p) t -> p k t", p=P)).then_inc(s_mem, 16)
            pool.wait_ge(s_bar, 3 * BASE["norm_f"].index)
            split_weights(pool, "up2")
            split_weights(pool, "down2")

        @block.tensor
        def _(pe):
            pe.wait_ge(s_small, 48)
            nc.tensor.matmul(psum[1][0:H2, :], TAB[:, :], BIG[0:BUCKETS, 60, :], start=True, stop=True)\
                .then_inc(s_hot, 1)
            pe_norm(pe, "norm_x", DT)
            stage_end(pe, "norm_x")
            pe_project(pe, "glu", h_tiles, 8)
            stage_end(pe, "glu")
            pe_project(pe, "qkv", h_tiles, 12)
            stage_end(pe, "qkv")
            pe_turn(pe, "turn_v", [[V1[:, j, t * P:(t + 1) * P] for j in range(4)] for t in range(4)])
            stage_end(pe, "turn_v")
            base = BASE["ln"]
            for k in range(4):
                last = nc.tensor.matmul(psum[6][:, :], con("ones"), CV[:, k, :], start=(k == 0), stop=(k == 3))
            last.then_inc(s_pe, 1)
            for k in range(4):
                pe.wait_ge(s_act, base.act + k + 1)
                last = nc.tensor.matmul(psum[7][:, :], con("ones"), SQ[:, k, :], start=(k == 0), stop=(k == 3))
            last.then_inc(s_pe, 1)
            stage_end(pe, "ln")
            pe.wait_ge(s_pool, 3)
            pe_attend(pe, "attend1", units1)
            stage_end(pe, "attend1")
            pe_turn(pe, "turn_o", [[O1[:, t, j * P:(j + 1) * P] for t in range(4)] for j in range(4)])
            stage_end(pe, "turn_o")
            pe_mix(pe, "mix1", 3, h_tiles, [OT1[:, k, :] for k in range(4)], [CV[:, k, :] for k in range(4)])
            stage_end(pe, "mix1")
            pe_project(pe, "mixo1", [Y1[:, k, :] for k in range(DT)], DT)
            stage_end(pe, "mixo1")
            pe_norm(pe, "post_mix", DT)
            stage_end(pe, "post_mix")
            pe_norm(pe, "norm_ffn1", DT)
            stage_end(pe, "norm_ffn1")
            pe_up(pe, "up1")
            stage_end(pe, "up1")
            pe_down(pe, "down1")
            stage_end(pe, "down1")
            pe_norm(pe, "post_ffn1", DT)
            stage_end(pe, "post_ffn1")
            pe_norm(pe, "norm_r", DT)
            stage_end(pe, "norm_r")
            base = BASE["rlora"]
            for j in range(3):
                pe_unit(pe, "rlora", 0, j, 0, 0, h_tiles, psum[j][:, :], None).then_inc(unit_done, 1)
            slot = (U0["rlora"] + 3) % W_SLOTS
            pe.wait_ge(w_full[slot], 16 * ((U0["rlora"] + 3) // W_SLOTS + 1))
            for t in range(4):
                for k in range(DT):
                    last = nc.tensor.matmul(psum[4 + t][:, 0:48], H[:, k, t * P:(t + 1) * P],
                                            W[:, slot, k * P:k * P + 48], start=(k == 0), stop=(k == DT - 1))
            last.then_inc(unit_done, 1)
            stage_end(pe, "rlora")
            pe_rprep(pe)
            stage_end(pe, "rprep")
            pe_rchunks(pe)
            stage_end(pe, "rchunks")
            pe_rout(pe)
            stage_end(pe, "rout")
            pe_norm(pe, "norm_n", DT)
            stage_end(pe, "norm_n")
            pe_project(pe, "nsa", h_tiles, 20)
            stage_end(pe, "nsa")
            pe_heads(pe, "nheads", 12, con("blk"), 1)
            stage_end(pe, "nheads")
            stage_end(pe, "cmp_k")
            base = BASE["cmp"]
            for kind in range(2):
                blk = (BLK, BLK_V)[kind]
                pe.wait_ge(s_blk, 1 + 2 * kind)
                for q in range(4):
                    slot = (U0["cmp"] + 4 * kind + q) % W_SLOTS
                    pe.wait_ge(w_full[slot], 16 * ((U0["cmp"] + 4 * kind + q) // W_SLOTS + 1))
                    for kk in range(4):
                        for c in range(2):
                            last = nc.tensor.matmul(psum[2 * kind + c][:, 0:4 * N_CMP],
                                                    W[:, slot, kk * 256 + c * P:kk * 256 + (c + 1) * P],
                                                    blk[:, 4 * q + kk, :], start=(q == 0 and kk == 0),
                                                    stop=(q == 3 and kk == 3))
                    last.then_inc(unit_done, 1)
            pe.wait_ge(s_act, base.act + 2)
            for c in range(2):
                last = nc.tensor.matmul(psum[4][:, 0:4 * N_CMP], CW2[:, c, 0:P], HC[:, c, :], start=(c == 0), stop=(c == 1))
            last.then_inc(s_pe, 1)
            pe.wait_ge(s_act, base.act + 4)
            for g in range(N_KV):
                for c in range(2):
                    last = nc.tensor.matmul(psum[5][0:N_CMP, g * DH:(g + 1) * DH], HV[:, c, g * N_CMP:(g + 1) * N_CMP],
                                            CW2[:, c, P:P + DH], start=(c == 0), stop=(c == 1))
            last.then_inc(s_pe, 1)
            pe.wait_ge(s_act, base.act + 5)
            nc.tensor.matmul(psum[6][:, 0:4 * N_CMP], con("blk"), SQ[:, 0, 0:4 * N_CMP], start=True, stop=True)\
                .then_inc(s_pe, 4)
            stage_end(pe, "cmp")
            pe_turn(pe, "nturn", [[(VS, VS, VW, VW)[j][:, j % 2, t * P:(t + 1) * P] for j in range(4)] for t in range(4)])
            stage_end(pe, "nturn")
            pe.wait_ge(s_bias2, 16)
            pe_attend(pe, "attend2", units2)
            stage_end(pe, "attend2")
            pe_turn(pe, "turn_o2", [[O2[:, t, j * P:(j + 1) * P] for t in range(4)] for j in range(8)])
            stage_end(pe, "turn_o2")
            pe_mix(pe, "mix2", 4, h_tiles, [YR[:, k, :] for k in range(DT)], [OT2[:, k, :] for k in range(DT)])
            stage_end(pe, "mix2")
            pe_project(pe, "mixo2", [Y2[:, k, :] for k in range(DT)], DT)
            stage_end(pe, "mixo2")
            pe_norm(pe, "norm_c", DT)
            stage_end(pe, "norm_c")
            pe_project(pe, "caq", h_tiles, 8)
            stage_end(pe, "caq")
            pe_norm(pe, "norm_m", DT, N_MEM)
            stage_end(pe, "norm_m")
            pe_project(pe, "cakv", [MN[:, k, 0:N_MEM] for k in range(DT)], 16, N_MEM)
            stage_end(pe, "cakv")
            pe_heads(pe, "qheads", 8, con("ones"), 2)
            stage_end(pe, "qheads")
            pe_heads(pe, "kheads", 8, con("ones"), 2, N_MEM)
            stage_end(pe, "kheads")
            pe_turn(pe, "turn_v3", [[V3[:, 4 * (b % 2) + q, (b // 2) * P:(b // 2 + 1) * P] for q in range(4)] for b in range(4)])
            stage_end(pe, "turn_v3")
            pe_attend(pe, "attend3", units3)
            stage_end(pe, "attend3")
            pe_turn(pe, "turn_o3", [[O3[:, t, j * P:(j + 1) * P] for t in range(4)] for j in range(8)])
            stage_end(pe, "turn_o3")
            pe_project(pe, "cao", [OT3[:, k, :] for k in range(DT)], 8)
            stage_end(pe, "cao")
            pe_norm(pe, "norm_f", DT)
            stage_end(pe, "norm_f")
            pe_up(pe, "up2")
            stage_end(pe, "up2")
            pe_down(pe, "down2")
            stage_end(pe, "down2")

        @block.scalar
        def _(act):
            act.wait_ge(s_prm, 32)
            act.wait_ge(s_c, 16)
            nc.scalar.activation(CB, CB, ACT.Silu).then_inc(s_act, 1)
            act.wait_ge(s_x, 16)
            act_norm(act, "norm_x", X, DT)
            line2 = BIG[0:H2, 63:65, :].rearrange("p a b -> p (a b)")
            act.wait_ge(s_tap0, 2)
            act.dma_start(scratch[1, 0:H2, :], line2[:, 0:LINE]).then_inc(s_line2, 16)
            stage_end(act, "norm_x")
            base = BASE["glu"]
            with act.Fori(0, 2) as i:
                for j in range(2):
                    act.wait_ge(unit_done, 4 * i + (U0["glu"] + 2 * j + 2))
                    act.wait_ge(s_ev, 4 * i + (base.ev + 2 * j))
                    nc.scalar.activation(SQ[:, 2 + j, :], psum[2 * j + 1][:, :], ACT.Sigmoid,
                                         bias=PRM[:, bass.ds(C0["b_in"] + 16 + j + 2 * i, 1)]).then_inc(s_glu, 1)
            stage_end(act, "glu")
            act_project(act, "qkv", BIG, 12, bias=("b_in", 0))
            stage_end(act, "qkv")
            act_turn(act, "turn_v", [VT1[:, t, :] for t in range(4)])
            stage_end(act, "turn_v")
            base = BASE["ln"]
            for k in range(4):
                act.wait_ge(s_dve, base.dve + 2 + k)
                nc.scalar.activation(SQ[:, k, :], CV[:, k, :], ACT.Square).then_inc(s_act, 1)
            act.wait_ge(s_dve, base.dve + 6)
            nc.scalar.activation(ST[:, 1, :], ST[:, 0, :], ACT.Sqrt).then_inc(s_act, 1)
            for k in range(4):
                act.wait_ge(s_dve, base.dve + 8 + k)
                nc.scalar.activation(CV[:, k, :], CV[:, k, :], ACT.Silu, bias=prm("b_conv_ln", k))
            stage_end(act, "ln")
            act_attend(act, "attend1", units1)
            stage_end(act, "attend1")
            act_turn(act, "turn_o", [OT1[:, j, :] for j in range(4)])
            stage_end(act, "turn_o")
            act_mix(act, "mix1", 3, 20, 28)
            stage_end(act, "mix1")
            act_project(act, "mixo1", Z1, DT)
            stage_end(act, "mixo1")
            act_norm(act, "post_mix", Z1, DT)
            stage_end(act, "post_mix")
            act_norm(act, "norm_ffn1", X, DT)
            act_norm_hi(act, "norm_ffn1", DT, MOD[:, 24:32])
            stage_end(act, "norm_ffn1")
            act_up(act, "up1", True)
            stage_end(act, "up1")
            act_down(act, "down1", Z1)
            stage_end(act, "down1")
            act_norm(act, "post_ffn1", Z1, DT)
            stage_end(act, "post_ffn1")
            act_norm(act, "norm_r", X, DT)
            stage_end(act, "norm_r")
            base = BASE["rlora"]
            for j in range(3):
                act.wait_ge(unit_done, U0["rlora"] + j + 1)
                nc.scalar.activation(ZL[:, j, :], psum[j][:, :], ACT.Copy, scale=OMU[:, j:j + 1]).then_inc(s_act, 1)
            act.wait_ge(unit_done, U0["rlora"] + 4)
            for t in range(4):
                nc.scalar.activation(GT[:, t, :], psum[4 + t][:, 0:48], ACT.Sigmoid)
            for j in range(3):
                act.wait_ge(s_ev, base.ev + j + 1)
                part = ZL[0:64, 0, :] if j == 0 else ZL[:, j, :]
                nc.scalar.activation(part, part, ACT.Tanh if j == 0 else ACT.Sigmoid)
            stage_end(act, "rlora")
            act_rprep(act)
            stage_end(act, "rprep")
            act_rchunks(act)
            stage_end(act, "rchunks")
            act_rout(act)
            stage_end(act, "rout")
            act_norm(act, "norm_n", X, DT)
            stage_end(act, "norm_n")
            act_project(act, "nsa", NSA, 20)
            stage_end(act, "nsa")
            act_heads(act, "nheads", tiles(16, 8) + tiles(28, 2) + tiles(32, 2), 12, 1)
            stage_end(act, "nheads")
            for g in range(N_KV):
                lo = DH * (g % 2)
                nc.scalar.activation(SH[DH:P, g, 0:S - 1], KC[lo:lo + DH, g // 2, 1:S], ACT.Copy)
            stage_end(act, "cmp_k")
            base = BASE["cmp"]
            for kind, dst in enumerate((HC, HV)):
                act.wait_ge(unit_done, U0["cmp"] + 4 * (kind + 1))
                for c in range(2):
                    nc.scalar.activation(dst[:, c, :], psum[2 * kind + c][:, 0:4 * N_CMP], ACT.Gelu_apprx_tanh)\
                        .then_inc(s_act, 1)
            act.wait_ge(s_pe, base.pe + 1)
            nc.scalar.activation(SQ[:, 0, 0:4 * N_CMP], psum[4][:, 0:4 * N_CMP], ACT.Square).then_inc(s_act, 1)
            act.wait_ge(s_pe, base.pe + 2)
            nc.scalar.activation(VCT[0:N_CMP, :], psum[5][0:N_CMP, 0:4 * DH], ACT.Copy)
            act.wait_ge(e_done, DT + 1)
            nc.scalar.activation(ST[:, 1, 0:4 * N_CMP], ST[:, 0, 0:4 * N_CMP], ACT.Sqrt).then_inc(s_act, 1)
            stage_end(act, "cmp")
            act_turn(act, "nturn", [VT2[:, t, :] for t in range(4)])
            stage_end(act, "nturn")
            act_attend(act, "attend2", units2)
            stage_end(act, "attend2")
            act_turn(act, "turn_o2", [OT2[:, j, :] for j in range(8)])
            stage_end(act, "turn_o2")
            act_mix(act, "mix2", 4, None, None)
            stage_end(act, "mix2")
            stage_end(act, "mixo2")
            act_norm(act, "norm_c", X, DT)
            stage_end(act, "norm_c")
            act_project(act, "caq", Q3, 8)
            stage_end(act, "caq")
            act.wait_ge(s_mem, 16)
            act_norm(act, "norm_m", MEM, DT, N_MEM)
            stage_end(act, "norm_m")
            act_project(act, "cakv", BIG[:, 8:24, :], 16, width=N_MEM)
            stage_end(act, "cakv")
            act_heads(act, "qheads", tiles(0, 8), 8, 2)
            stage_end(act, "qheads")
            act_heads(act, "kheads", [K3[:, k, :] for k in range(8)], 8, 2, N_MEM)
            stage_end(act, "kheads")
            act_turn(act, "turn_v3", [VT3[:, b // 2, (b % 2) * S:(b % 2 + 1) * S] for b in range(4)])
            stage_end(act, "turn_v3")
            act_attend(act, "attend3", units3)
            stage_end(act, "attend3")
            act_turn(act, "turn_o3", [OT3[:, j, :] for j in range(8)])
            stage_end(act, "turn_o3")
            stage_end(act, "cao")
            act_norm(act, "norm_f", X, DT)
            act_norm_hi(act, "norm_f", DT, None)
            stage_end(act, "norm_f")
            act_up(act, "up2", False)
            stage_end(act, "up2")
            stage_end(act, "down2")

        @block.vector
        def _(dve):
            V = nc.vector
            steps = Steps(s_chain)
            dve.wait_ge(s_prm, 32)
            V.tensor_scalar(OMU[:, :], prm("mu", 0, 28), -1.0, 1.0, ALU.mult, ALU.add)
            V.memset(GLU[:, :, 0:LEAD], 0.0)
            dve.wait_ge(s_act, 1)

            def modulate(j, i=None):
                dve.wait_ge(w_full[j], 16 if i is None else 16 * i + 16)
                if i is not None:
                    dve.wait_ge(unit_done, W_SLOTS * i + (j - 1))
                elif j >= 2:
                    dve.wait_ge(unit_done, j - 1)
                at = MOD[:, j:j + 1] if i is None else MOD[:, bass.ds(W_SLOTS * i + j, 1)]
                V.scalar_tensor_tensor(MP[j % 2], W[:, j, :], 1.0, CB, ALU.mult, ALU.mult, accum_out=at)\
                    .then_inc(unit_done, 1)

            for j in range(W_SLOTS):
                modulate(j)
            with dve.Fori(1, 48 // W_SLOTS) as i:
                for j in range(W_SLOTS):
                    modulate(j, i)
            dve.wait_ge(unit_done, 48)
            V.tensor_tensor(MOD[:, :], MOD[:, :], prm("b_ada", 0, 48), ALU.add).then_inc(s_dve, 1)
            dve.wait_ge(s_dve, 1)
            V.scalar_tensor_tensor(GM[:, 8:16], MOD[:, 8:16], 1.0, prm("g_pre_mix", 0, 8), ALU.add, ALU.mult)
            V.tensor_tensor(GM[:, 16:24], MOD[:, 16:24], prm("g_post_mix", 0, 8), ALU.mult)
            V.scalar_tensor_tensor(GM[:, 24:32], MOD[:, 32:40], 1.0, prm("g_pre_ffn", 0, 8), ALU.add, ALU.mult)
            V.tensor_tensor(GM[:, 32:40], MOD[:, 40:48], prm("g_post_ffn", 0, 8), ALU.mult).then_inc(s_ev, 4)
            dve.wait_ge(s_ev, 4)
            line2 = BIG[0:H2, 63:65, :].rearrange("p a b -> p (a b)")
            dve.wait_ge(s_hot, 1)
            V.tensor_copy(line2[:, 0:S], psum[1][0:H2, :]).then_inc(s_tap0, 1)
            V.memset(line2[:, S:LINE], NEG).then_inc(s_tap0, 1)
            dve_norm(dve, "norm_x", X, H, GM[:, 8:16], DT, MOD[:, 0:8])
            stage_end(dve, "norm_x")
            base = BASE["glu"]
            with dve.Fori(0, 2) as i:
                for j in range(2):
                    dve.wait_ge(s_glu, 2 * i + (base.glu + j + 1))
                    V.scalar_tensor_tensor(GLU[:, 2 * i + j, LEAD:GPAD], psum[2 * j][:, :],
                                           PRM[:, bass.ds(C0["b_in"] + 12 + j + 2 * i, 1)], SQ[:, 2 + j, :],
                                           ALU.add, ALU.mult).then_inc(s_ev, 2)
            stage_end(dve, "glu")
            for j in range(4):
                V.tensor_scalar(CV[:, j, :], GLU[:, j, LEAD - CONV_K + 1:LEAD - CONV_K + 1 + S],
                                prm("w_dw_conv", j * CONV_K), prm("b_dw_conv", j), ALU.mult, ALU.add).then_inc(s_cv, 1)
            with dve.Fori(1, CONV_K) as t:
                for j in range(4):
                    dve.wait_ge(s_cv, 4 * t + (j - 3))
                    V.scalar_tensor_tensor(CV[:, j, :], GLU[:, j, bass.ds(LEAD - CONV_K + 1 + t, S)],
                                           PRM[:, bass.ds(C0["w_dw_conv"] + j * CONV_K + t, 1)], CV[:, j, :],
                                           ALU.mult, ALU.add).then_inc(s_cv, 1)
            stage_end(dve, "qkv")
            stage_end(dve, "turn_v")
            base = BASE["ln"]
            dve.wait_ge(s_pe, base.pe + 1)
            V.tensor_scalar(ST[:, 0, :], psum[6][:, :], 1.0 / 512, None, ALU.mult).then_inc(s_dve, 1)
            dve.wait_ge(s_dve, base.dve + 1)
            for k in range(4):
                V.tensor_tensor(CV[:, k, :], CV[:, k, :], ST[:, 0, :], ALU.subtract).then_inc(s_dve, 1)
            dve.wait_ge(s_pe, base.pe + 2)
            V.tensor_scalar(ST[:, 0, :], psum[7][:, :], 1.0 / 512, EPS, ALU.mult, ALU.add).then_inc(s_dve, 1)
            dve.wait_ge(s_act, base.act + 5)
            V.reciprocal(ST[:, 0, :], ST[:, 1, :]).then_inc(s_dve, 1)
            dve.wait_ge(s_dve, base.dve + 7)
            for k in range(4):
                V.scalar_tensor_tensor(CV[:, k, :], CV[:, k, :], prm("g_conv_ln", k), ST[:, 0, :], ALU.mult,
                                       ALU.mult).then_inc(s_dve, 1)
            stage_end(dve, "ln")
            dve_attend(dve, "attend1", units1, steps)
            stage_end(dve, "attend1")
            stage_end(dve, "turn_o")
            dve_mix(dve, "mix1", 3, Y1, "b_conv_o")
            stage_end(dve, "mix1")
            stage_end(dve, "mixo1")
            dve_residual(dve, "post_mix", Z1, GM[:, 16:24], DT)
            stage_end(dve, "post_mix")
            dve_norm(dve, "norm_ffn1", X, H, GM[:, 24:32], DT)
            dve_norm_lo(dve, "norm_ffn1", DT, MOD[:, 24:32])
            stage_end(dve, "norm_ffn1")
            dve_up(dve, "up1", True)
            stage_end(dve, "up1")
            dve_down(dve, "down1", Z1)
            stage_end(dve, "down1")
            dve_residual(dve, "post_ffn1", Z1, GM[:, 32:40], DT)
            stage_end(dve, "post_ffn1")
            dve_norm(dve, "norm_r", X, H, prm("norm_mix", 0, 8), DT)
            stage_end(dve, "norm_r")
            base = BASE["rlora"]
            for j in range(3):
                dve.wait_ge(s_act, base.act + j + 1)
                V.scalar_tensor_tensor(ZL[:, j, 1:S], psum[j][:, 0:S - 1], prm("mu", j), ZL[:, j, 1:S], ALU.mult,
                                       ALU.add).then_inc(s_ev, 1)
            stage_end(dve, "rlora")
            dve_rprep(dve, steps)
            stage_end(dve, "rprep")
            dve_rchunks(dve)
            stage_end(dve, "rchunks")
            dve_rout(dve, steps)
            stage_end(dve, "rout")
            dve_norm(dve, "norm_n", X, H, prm("norm_mix", 0, 8), DT)
            stage_end(dve, "norm_n")
            stage_end(dve, "nsa")
            dve_heads(dve, "nheads", tiles(16, 8) + tiles(28, 2) + tiles(32, 2), 12, 1,
                      [prm("q_gain")] * 8 + [prm("k_gain", 1)] * 2 + [prm("k_gain", 2)] * 2, S, DH)
            stage_end(dve, "nheads")
            for g in range(N_KV):
                lo = DH * (g % 2)
                V.tensor_copy(SH[0:DH, g, :], KC[lo:lo + DH, g // 2, :])
            stage_end(dve, "cmp_k")
            base = BASE["cmp"]

            def blocks(dst, pe_name):
                for k in range(16):
                    last = V.tensor_scalar(dst[:, k, :].rearrange("p (g n) -> p g n", g=N_KV),
                                           SH[:, :, 2 * k:2 * k + CMP_STRIDE * (N_CMP - 1) + 1:CMP_STRIDE],
                                           prm(pe_name, k), None, ALU.add)
                return last

            blocks(BLK, "pe_k").then_inc(s_blk, 1)
            dve.wait_ge(s_blk, 1)
            for half in range(2):
                for g in range(N_KV):
                    lo = DH * (g % 2)
                    last = V.tensor_copy(SH[DH * half:DH * (half + 1), g, 0:S - half], VC[lo:lo + DH, g // 2, half:S])
            last.then_inc(s_blk, 1)
            dve.wait_ge(s_blk, 2)
            blocks(BLK_V, "pe_v").then_inc(s_blk, 1)
            dve.wait_ge(s_pe, base.pe + 6)
            V.tensor_scalar(ST[:, 0, 0:4 * N_CMP], psum[6][:, 0:4 * N_CMP], 1.0 / DH, EPS, ALU.mult, ALU.add)\
                .then_inc(e_done, 1)
            dve.wait_ge(s_act, base.act + 6)
            steps.link(dve, V.reciprocal(ST[:, 0, 0:4 * N_CMP], ST[:, 1, 0:4 * N_CMP]))
            V.scalar_tensor_tensor(KCN, psum[4][:, 0:4 * N_CMP], prm("k_gain", 0), ST[:, 0, 0:4 * N_CMP], ALU.mult,
                                   ALU.mult)
            stage_end(dve, "cmp")
            stage_end(dve, "nturn")
            dve_attend(dve, "attend2", units2, steps)
            stage_end(dve, "attend2")
            stage_end(dve, "turn_o2")
            dve_mix(dve, "mix2", 4, Y2, None)
            stage_end(dve, "mix2")
            dve_add_project(dve, "mixo2", 8)
            stage_end(dve, "mixo2")
            dve_norm(dve, "norm_c", X, H, prm("norm_cross", 0, 8), DT)
            stage_end(dve, "norm_c")
            stage_end(dve, "caq")
            dve_norm(dve, "norm_m", MEM, MN, prm("norm_mem", 0, 8), DT, width=N_MEM)
            stage_end(dve, "norm_m")
            stage_end(dve, "cakv")
            dve_heads(dve, "qheads", tiles(0, 8), 8, 2, [prm("ca_q_gain", k % 2) for k in range(8)], S, 256)
            stage_end(dve, "qheads")
            dve_heads(dve, "kheads", [K3[:, k, :] for k in range(8)], 8, 2, [prm("ca_k_gain", k % 2) for k in range(8)],
                      N_MEM, 256)
            stage_end(dve, "kheads")
            stage_end(dve, "turn_v3")
            dve_attend(dve, "attend3", units3, steps)
            stage_end(dve, "attend3")
            stage_end(dve, "turn_o3")
            dve_add_project(dve, "cao", 8)
            stage_end(dve, "cao")
            dve_norm(dve, "norm_f", X, H, prm("norm_ffn", 0, 8), DT)
            dve_norm_lo(dve, "norm_f", DT, None)
            stage_end(dve, "norm_f")
            dve_up(dve, "up2", False)
            stage_end(dve, "up2")
            dve.wait_ge(unit_done, N_UNITS)
            for n in range(DT):
                V.tensor_tensor(X[:, n, :], X[:, n, :], psum[n][:, :], ALU.add)
            stage_end(dve, "down2")



def t5_buckets():
    n = np.arange(S)
    exact = BUCKETS // 2
    nf = np.maximum(n, 1).astype(np.float32)
    large = exact + (np.log(nf / np.float32(exact)) / np.float32(np.log(128 / exact)) * np.float32(BUCKETS - exact)).astype(np.int32)
    return np.where(n < exact, n, np.minimum(large, BUCKETS - 1))


def constants():
    c = np.zeros((P, N_CONST), np.float32)

    def put(name, a):
        c[:a.shape[0], K0[name]:K0[name] + a.shape[1]] = a

    i, j = np.arange(CHUNK)[:, None], np.arange(CHUNK)[None, :]
    same = i // 16 == j // 16
    put("ident", np.eye(P))
    put("ones", np.ones((P, P)))
    put("blk", np.kron(np.eye(2), np.ones((64, 64))))
    for name, m in (("strict_up", i < j), ("incl_up", i <= j), ("up16", (i < j) & same), ("lo16", (i > j) & same),
                    ("lo_off", (i > j) & ~same), ("eye64", i == j)):
        put(name, np.tile(m, (2, 1)))
    put("scan", np.tile(np.arange(S) % CHUNK != 0, (P, 1)))
    onehot = np.zeros((BUCKETS, S))
    onehot[t5_buckets()[S - 1 - np.arange(S)], np.arange(S)] = 1
    return c, onehot.astype(np.float32)


def panels(w):
    k, n = w.shape
    return w.reshape(k // P, P, n // P, P).transpose(2, 1, 0, 3).reshape(n // P, P, k)


def pad_columns(w, n):
    return np.concatenate([w, np.zeros((w.shape[0], n - w.shape[1]), w.dtype)], 1)


def interleave(*units):
    return np.stack(units, 1).reshape(-1, P, D)


def kernel(**inputs):
    import concourse.bacc as bacc
    from concourse.bass_utils import run_bass_kernel_spmd

    a = {k: np.asarray(v) for k, v in inputs.items()}
    one = {k: (v[0] if k not in ("rel_bias_2",) else v) for k, v in a.items()}

    w_in = one["w_in"]
    up, up2 = panels(one["w_up"]), panels(one["ffn_up_2"])
    q, k, v, ga, gb = (w_in[:, 512 * n:512 * (n + 1)] for n in range(5))
    gate_a, gate_b = panels(w_in[:, 2560:3584]), panels(w_in[:, 3584:4608])
    both = np.concatenate([panels(one["w_attn_o"]), panels(one["w_conv_o"])], 2)
    z = one["w_in_2"]
    rk, kk_, rv = panels(z[:, 0:1024]), panels(z[:, 1024:2048]), panels(z[:, 2048:3072])
    zq = z[:, 3360:4384].reshape(D, 2, 2, HG, DH).transpose(0, 1, 3, 2, 4).reshape(D, D)
    z_gate = pad_columns(z[:, 5920:5968], P)
    zm = z[:, 5968:8016]
    down, down2 = (one[n].reshape(FT, P, D) for n in ("w_down", "ffn_down_2"))
    cmp_units = [one[n].reshape(4, 4, P, CMP_HIDDEN).transpose(0, 2, 1, 3).reshape(4, P, D)
                 for n in ("cmp_w1_k_2", "cmp_w1_v_2")]
    stream = np.concatenate([
        one["w_ada"].T.reshape(48, P, D), interleave(panels(ga), panels(gb)), panels(q), panels(k), panels(v),
        interleave(gate_a, both, gate_b), panels(one["w_mix_o"]), interleave(up[:FT], up[FT:]), down,
        panels(z[:, 3072:3328]), panels(pad_columns(z[:, 3328:3360], P)), panels(z_gate), interleave(kk_, rk, rv),
        panels(zq), panels(z[:, 4384:5920]), *cmp_units,
        interleave(panels(zm[:, :D]), panels(one["w_branch_rwkv_2"]), panels(zm[:, D:]), panels(one["w_branch_nsa_2"])),
        panels(one["w_mix_out_2"]), panels(one["ca_wq_2"]), panels(one["ca_wkv_2"]), panels(one["ca_wo_2"]),
        interleave(up2[:FT], up2[FT:]), down2], 0)
    assert stream.shape == (N_UNITS, P, D)

    def col(x):
        return x.reshape(-1, P).T

    def taps(x):
        return x.reshape(x.shape[0], -1, P).transpose(2, 1, 0).reshape(P, -1)

    mu = one["rwkv_mu_2"]
    mu_lora = np.concatenate([mu[3072:3328], np.pad(mu[3328:3360], (0, P - 32)), np.zeros(P, mu.dtype)])
    mu_rkv = np.stack([mu[1024:2048].reshape(8, P), mu[0:1024].reshape(8, P), mu[2048:3072].reshape(8, P)], 1)
    twice = lambda x: np.concatenate([x, x], -1)
    parts = {
        "b_ada": col(one["b_ada"]), "b_in": col(one["b_in"]), "w_dw_conv": taps(one["w_dw_conv"]),
        "w_dw_ffn": taps(one["w_dw_ffn"]), "b_dw_ffn": col(one["b_dw_ffn"]), "mu": col(np.concatenate([mu_lora, mu_rkv.reshape(-1)])),
        "norm_mix": col(one["norm_mix_2"]), "w0": col(one["rwkv_w0_2"]), "a0": col(one["rwkv_a0_2"]),
        "kk": col(one["rwkv_kk_2"]), "ka": col(one["rwkv_ka_2"]), "rk": col(one["rwkv_rk_2"].reshape(-1)),
        "lnx_w": col(one["rwkv_lnx_w_2"]), "lnx_b": col(one["rwkv_lnx_b_2"]),
        "q_gain": twice(one["nsa_q_gain_2"])[:, None], "k_gain": twice(one["nsa_k_gain_2"]).T,
        "pe_k": col(one["cmp_pe_k_2"].reshape(-1)), "pe_v": col(one["cmp_pe_v_2"].reshape(-1)),
        "norm_cross": col(one["norm_cross_2"]), "norm_mem": col(one["norm_mem_2"]),
        "ca_q_gain": col(one["ca_q_gain_2"]), "ca_k_gain": col(one["ca_k_gain_2"]), "norm_ffn": col(one["norm_ffn_2"]),
        "ffn_conv": taps(one["ffn_conv_2"]), "ffn_conv_b": col(one["ffn_conv_b_2"]),
    }
    cols = np.concatenate([parts[n] if n in parts else col(one[n]) for n, _ in COLUMNS], 1)
    assert cols.shape == (P, N_COLS)

    const, onehot = constants()
    w2a2 = np.concatenate([one["rwkv_w2_2"], one["rwkv_a2_2"]], 0)
    g2 = np.pad(one["rwkv_g2_2"], ((0, 96), (0, 0))).reshape(2, P, D).transpose(1, 0, 2)
    w2k, w2v = (one[n].reshape(2, P, DH).transpose(1, 0, 2) for n in ("cmp_w2_k_2", "cmp_w2_v_2"))
    arrays = {
        "stream": stream, "cols": cols, "const": const, "onehot": onehot, "c_rows": np.tile(a["c"], (P, 1)), "x_t": one["x"].T, "mem_t": one["mem_2"].T,
        "line1": one["rel_bias"][:, ::-1], "table2": one["rel_bias_2"], "w2a2": w2a2, "g2": g2,
        "cmp_w2": np.concatenate([w2k, w2k, w2v], 2),
    }
    arrays = {n: np.ascontiguousarray(x) for n, x in arrays.items()}
    nc = bacc.Bacc("TRN2", target_bir_lowering=False, num_devices=1)
    args = [nc.dram_tensor(n, x.shape, mybir.dt.from_np(x.dtype), kind="ExternalInput").ap() for n, x in arrays.items()]
    args.append(nc.dram_tensor("out_t", (D, S), F32, kind="ExternalOutput").ap())
    args.append(nc.dram_tensor("bias_lines", (2, H2, LINE), F32, kind="Internal").ap())
    args.append(nc.dram_tensor("bias_rows", (H1 + H2, P, S), F32, kind="Internal").ap())
    build_program(nc, *args)
    r = run_bass_kernel_spmd(nc, [arrays], core_ids=[0])
    return np.ascontiguousarray(r.results[0]["out_t"].T)[None]
```
